# Optimizing a Trainium2 kernel written in Bass

```python
import math
import jax
import jax.numpy as jnp
from jax import lax
import numpy as np
import jax, jax.numpy as jnp

D_MODEL = 1024
BATCH = 1
SEQ = 256
DEPTH = 2

MEM_LEN = 256
N_BRANCHES = 4
MIX_WIDTH = D_MODEL // N_BRANCHES
HEAD_DIM = 64
MIX_HEADS = MIX_WIDTH // HEAD_DIM

NSA_CMP_LEN = 32
NSA_CMP_STRIDE = 16
NSA_SLC_LEN = 64
NSA_TOP_N = 8
NSA_WINDOW = 512
Q_BLOCK = 128
FORCE_BONUS = 1e4
N_BUCKETS = 32
MAX_DISTANCE = 128

RET_CHUNK = 128
ROPE_BASE = 10000.0
RET_NORM_EPS = 1e-5

RWKV_DECAY_LORA = 32
RWKV_AAA_LORA = 32
RWKV_GATE_LORA = 64
RWKV_GN_EPS = 64e-5
RWKV_SIZES = (MIX_WIDTH, MIX_WIDTH, MIX_WIDTH, RWKV_DECAY_LORA, RWKV_AAA_LORA, RWKV_GATE_LORA)
RWKV_COLS = sum(RWKV_SIZES)

CONV_WIDTH = 3

XA_HEADS = 4
XA_HEAD_DIM = D_MODEL // XA_HEADS
D_FF = 4 * D_MODEL

IN_SIZES = (MIX_WIDTH, 6 * HEAD_DIM, 3 * MIX_HEADS, 4 * MIX_WIDTH, RWKV_COLS, 3 * MIX_WIDTH, N_BRANCHES * D_MODEL)
IN_COLS = sum(IN_SIZES)

RMS_EPS = 1e-6
NEG_INF = -1e30


def split_cols(z, sizes):
    return jnp.split(z, np.cumsum(sizes)[:-1].tolist(), axis=-1)

def rms_norm(x, g):
    xf = x.astype(jnp.float32)
    y = xf * lax.rsqrt(jnp.mean(xf * xf, axis=-1, keepdims=True) + RMS_EPS)
    return (y * g.astype(jnp.float32)).astype(x.dtype)

def head_norm(u, eps):
    mu = jnp.mean(u, axis=-1, keepdims=True)
    var = jnp.mean(jnp.square(u - mu), axis=-1, keepdims=True)
    return (u - mu) * lax.rsqrt(var + eps)

def t5_bucket(dist):
    n = jnp.maximum(dist, 0)
    max_exact = N_BUCKETS // 2
    nf = jnp.maximum(n, 1).astype(jnp.float32)
    large = max_exact + (jnp.log(nf / max_exact) / math.log(MAX_DISTANCE / max_exact)
                         * (N_BUCKETS - max_exact)).astype(jnp.int32)
    large = jnp.minimum(large, N_BUCKETS - 1)
    return jnp.where(n < max_exact, n, large)

def masked_softmax(s, valid):
    return jax.nn.softmax(jnp.where(valid, s, NEG_INF), axis=-1)

def nsa_mixer(q, kv, gate_logits, cmp_w, cmp_pe, rel_bias):
    B, S, H, Dh = q.shape
    dt = q.dtype
    f32 = jnp.float32
    scale = Dh ** -0.5
    k_c, v_c, k_s, v_s, k_w, v_w = jnp.split(kv, 6, axis=-1)

    n_cmp = (S - NSA_CMP_LEN) // NSA_CMP_STRIDE + 1
    cmp_start = jnp.arange(n_cmp) * NSA_CMP_STRIDE
    cmp_idx = cmp_start[:, None] + jnp.arange(NSA_CMP_LEN)[None, :]
    k_cmp = jnp.einsum('bnld,lde->bne', k_c[:, cmp_idx] + cmp_pe, cmp_w[0])
    v_cmp = jnp.einsum('bnld,lde->bne', v_c[:, cmp_idx] + cmp_pe, cmp_w[1])
    cmp_end = cmp_start + NSA_CMP_LEN - 1

    n_slc = S // NSA_SLC_LEN
    top_n = min(NSA_TOP_N, n_slc)
    slc_start = jnp.arange(n_slc) * NSA_SLC_LEN
    overlap = jnp.clip(jnp.minimum(cmp_start[:, None] + NSA_CMP_LEN, slc_start[None, :] + NSA_SLC_LEN)
                       - jnp.maximum(cmp_start[:, None], slc_start[None, :]), 0).astype(f32) / NSA_CMP_LEN
    k_blk = k_s.reshape(B, n_slc, NSA_SLC_LEN, Dh)
    v_blk = v_s.reshape(B, n_slc, NSA_SLC_LEN, Dh)
    b_idx = jnp.arange(B)[:, None, None]

    k_wp = jnp.pad(k_w, ((0, 0), (NSA_WINDOW, 0), (0, 0)))
    v_wp = jnp.pad(v_w, ((0, 0), (NSA_WINDOW, 0), (0, 0)))

    gates = jax.nn.sigmoid(gate_logits.astype(f32)).reshape(B, S, H, 3)
    n_qb = S // Q_BLOCK
    q_b = q.reshape(B, n_qb, Q_BLOCK, H, Dh).swapaxes(0, 1)
    g_b = gates.reshape(B, n_qb, Q_BLOCK, H, 3).swapaxes(0, 1)
    bias_f = rel_bias.astype(f32)

    def block_fn(args):
        qb, gb, bi = args
        t = bi * Q_BLOCK + jnp.arange(Q_BLOCK)

        d_c = t[:, None] - cmp_end[None, :]
        s_c = (jnp.einsum('bqhd,bnd->bhqn', qb, k_cmp).astype(f32) * scale
               + bias_f[t5_bucket(d_c)].transpose(2, 0, 1))
        p_c = masked_softmax(s_c, d_c >= 0) * (t >= NSA_CMP_LEN - 1)[:, None].astype(f32)
        o_c = jnp.einsum('bhqn,bnd->bqhd', p_c.astype(dt), v_cmp)

        imp = jnp.einsum('bhqn,nm->bqm', p_c, overlap)
        blk = jnp.arange(n_slc)
        cur = t // NSA_SLC_LEN
        forced = (blk[None, :] == 0) | (blk[None, :] == cur[:, None]) | (blk[None, :] == cur[:, None] - 1)
        imp = jnp.where(forced, imp + FORCE_BONUS, imp)
        imp = jnp.where(blk[None, :] <= cur[:, None], imp, NEG_INF)
        _, sel = lax.top_k(imp, top_n)

        k_g = k_blk[b_idx, sel].reshape(B, Q_BLOCK, top_n * NSA_SLC_LEN, Dh)
        v_g = v_blk[b_idx, sel].reshape(B, Q_BLOCK, top_n * NSA_SLC_LEN, Dh)
        pos_s = (sel[..., None] * NSA_SLC_LEN + jnp.arange(NSA_SLC_LEN)).reshape(B, Q_BLOCK, -1)
        d_s = t[None, :, None] - pos_s
        s_s = (jnp.einsum('bqhd,bqkd->bhqk', qb, k_g).astype(f32) * scale
               + bias_f[t5_bucket(d_s)].transpose(0, 3, 1, 2))
        p_s = masked_softmax(s_s, (d_s >= 0)[:, None])
        o_s = jnp.einsum('bhqk,bqkd->bqhd', p_s.astype(dt), v_g)

        k_wb = lax.dynamic_slice_in_dim(k_wp, bi * Q_BLOCK, NSA_WINDOW + Q_BLOCK, axis=1)
        v_wb = lax.dynamic_slice_in_dim(v_wp, bi * Q_BLOCK, NSA_WINDOW + Q_BLOCK, axis=1)
        pos_w = bi * Q_BLOCK - NSA_WINDOW + jnp.arange(NSA_WINDOW + Q_BLOCK)
        d_w = t[:, None] - pos_w[None, :]
        valid_w = (d_w >= 0) & (d_w < NSA_WINDOW) & (pos_w[None, :] >= 0)
        s_w = (jnp.einsum('bqhd,bkd->bhqk', qb, k_wb).astype(f32) * scale
               + bias_f[t5_bucket(d_w)].transpose(2, 0, 1))
        p_w = masked_softmax(s_w, valid_w)
        o_w = jnp.einsum('bhqk,bkd->bqhd', p_w.astype(dt), v_wb)

        out = gb[..., 0:1] * o_c + gb[..., 1:2] * o_s + gb[..., 2:3] * o_w
        return out.astype(dt)

    out = lax.map(block_fn, (q_b, g_b, jnp.arange(n_qb)))
    return out.swapaxes(0, 1).reshape(B, S, H * Dh)

def rotary(u, pos):
    half = u.shape[-1] // 2
    inv_freq = ROPE_BASE ** (-jnp.arange(half, dtype=jnp.float32) / half)
    ang = pos.astype(jnp.float32)[:, None] * inv_freq[None, :]
    cos = jnp.cos(ang)[None, :, None, :]
    sin = jnp.sin(ang)[None, :, None, :]
    u1, u2 = u[..., :half], u[..., half:]
    return jnp.concatenate([u1 * cos - u2 * sin, u2 * cos + u1 * sin], axis=-1)

def retention_mixer(q, k, v, g, norm_g):
    B, S, C = q.shape
    H = C // HEAD_DIM
    f32 = jnp.float32
    pos = jnp.arange(S)
    qh = rotary(q.reshape(B, S, H, HEAD_DIM).astype(f32), pos) * HEAD_DIM ** -0.5
    kh = rotary(k.reshape(B, S, H, HEAD_DIM).astype(f32), pos)
    vh = v.reshape(B, S, H, HEAD_DIM).astype(f32)
    L = min(RET_CHUNK, S)
    nc = S // L
    lg = jnp.log(1.0 - 2.0 ** (-5.0 - jnp.arange(H, dtype=f32)))
    n = jnp.arange(L, dtype=f32)
    diff = n[:, None] - n[None, :]
    inner_decay = jnp.where(diff >= 0, jnp.exp(jnp.maximum(diff, 0.0)[None] * lg[:, None, None]), 0.0)
    q_decay = jnp.exp((n + 1.0)[None, :] * lg[:, None])
    k_decay = jnp.exp((L - 1.0 - n)[None, :] * lg[:, None])
    chunk_decay = jnp.exp(L * lg)

    def to_chunks(u):
        return u.reshape(B, nc, L, H, HEAD_DIM).transpose(1, 0, 3, 2, 4)

    def step(state, inp):
        qc, kc, vc = inp
        att = jnp.einsum('bhld,bhmd->bhlm', qc, kc) * inner_decay
        o = (jnp.einsum('bhlm,bhmd->bhld', att, vc)
             + jnp.einsum('bhld,bhde->bhle', qc, state) * q_decay[None, :, :, None])
        state = (state * chunk_decay[None, :, None, None]
                 + jnp.einsum('bhmd,bhme->bhde', kc * k_decay[None, :, :, None], vc))
        return state, o

    state0 = jnp.zeros((B, H, HEAD_DIM, HEAD_DIM), f32)
    _, o = lax.scan(step, state0, (to_chunks(qh), to_chunks(kh), to_chunks(vh)))
    o = o.transpose(1, 0, 3, 2, 4).reshape(B, S, H, HEAD_DIM)
    o = head_norm(o, RET_NORM_EPS) * norm_g.astype(f32).reshape(H, HEAD_DIM)
    return (jax.nn.silu(g.astype(f32)) * o.reshape(B, S, C)).astype(q.dtype)

def rwkv7_mixer(z, mu, w0, w2, a0, a2, g2, k_k, k_a, r_k, ln_g, ln_b):
    B, S, _ = z.shape
    C = MIX_WIDTH
    H = C // HEAD_DIM
    N = HEAD_DIM
    dt = z.dtype
    f32 = jnp.float32
    zf = z.astype(f32)
    zf = zf + (jnp.pad(zf, ((0, 0), (1, 0), (0, 0)))[:, :-1] - zf) * mu
    r, k, v, wl, al, gl = split_cols(zf, RWKV_SIZES)
    w_log = -jax.nn.softplus(-(w0 + jnp.tanh(wl) @ w2)) - 0.5
    decay = jnp.exp(-jnp.exp(w_log))
    a = jax.nn.sigmoid(a0 + al @ a2)
    g = jax.nn.sigmoid(gl) @ g2
    kk = (k * k_k).reshape(B, S, H, N)
    kk = kk / jnp.maximum(jnp.sqrt(jnp.sum(kk * kk, axis=-1, keepdims=True)), 1e-12)
    k = k * (1.0 + (a - 1.0) * k_a)

    def heads(u):
        return u.reshape(B, S, H, N)

    rh, wh, kh, vh, ah = heads(r), heads(decay), heads(k), heads(v), heads(a)

    def seq_first(u):
        return u.transpose(1, 0, 2, 3)

    def step(state, inp):
        r_t, w_t, k_t, v_t, kk_t, a_t = inp
        sa = jnp.einsum('bhvk,bhk->bhv', state, -kk_t)
        state = (state * w_t[:, :, None, :]
                 + sa[..., None] * (kk_t * a_t)[:, :, None, :]
                 + v_t[..., None] * k_t[:, :, None, :])
        return state, jnp.einsum('bhvk,bhk->bhv', state, r_t)

    state0 = jnp.zeros((B, H, N, N), f32)
    xs = (seq_first(rh), seq_first(wh), seq_first(kh), seq_first(vh), seq_first(kk), seq_first(ah))
    _, y = lax.scan(step, state0, xs)
    y = y.transpose(1, 0, 2, 3)
    y = head_norm(y, RWKV_GN_EPS) * ln_g.astype(f32).reshape(H, N) + ln_b.astype(f32).reshape(H, N)
    y = y + jnp.sum(rh * kh * r_k.astype(f32).reshape(H, N), axis=-1, keepdims=True) * vh
    return (y.reshape(B, S, C) * g).astype(dt)

def short_conv_mixer(z, conv_w):
    b_g, c_g, xt = jnp.split(z, 3, axis=-1)
    u = c_g * xt
    C = u.shape[-1]
    y = lax.conv_general_dilated(u, conv_w[:, None, :].astype(u.dtype), window_strides=(1,),
                                 padding=[(CONV_WIDTH - 1, 0)],
                                 dimension_numbers=('NWC', 'WIO', 'NWC'),
                                 feature_group_count=C)
    return b_g * y

def cross_attention(h, m, wq, wkv, wo):
    B, S, D = h.shape
    M = m.shape[1]
    q = (h @ wq).reshape(B, S, XA_HEADS, XA_HEAD_DIM)
    k, v = jnp.split(m @ wkv, 2, axis=-1)
    k = k.reshape(B, M, XA_HEADS, XA_HEAD_DIM)
    v = v.reshape(B, M, XA_HEADS, XA_HEAD_DIM)
    s = jnp.einsum('bshd,bmhd->bhsm', q, k).astype(jnp.float32) * XA_HEAD_DIM ** -0.5
    p = jax.nn.softmax(s, axis=-1).astype(h.dtype)
    o = jnp.einsum('bhsm,bmhd->bshd', p, v).reshape(B, S, D)
    return o @ wo

def first_inputs(seed: int = 0) -> dict:
    key = jax.random.key(seed)
    ks = iter(jax.random.split(key, 48))
    f32 = jnp.float32

    def nrm(shape, scale):
        return scale * jax.random.normal(next(ks), shape, f32)

    def gain(shape):
        return 1.0 + 0.02 * jax.random.normal(next(ks), shape, f32)

    def unif(shape, lo, hi):
        return jax.random.uniform(next(ks), shape, f32, lo, hi)

    return {
        'x': nrm((BATCH, SEQ, D_MODEL), 1.0),
        'mem': nrm((BATCH, MEM_LEN, D_MODEL), 1.0),
        'ln_mix_pre': gain((DEPTH, D_MODEL)),
        'w_in': nrm((DEPTH, D_MODEL, IN_COLS), D_MODEL ** -0.5),
        'nsa_cmp_w': nrm((DEPTH, 2, NSA_CMP_LEN, HEAD_DIM, HEAD_DIM), (NSA_CMP_LEN * HEAD_DIM) ** -0.5),
        'nsa_cmp_pe': nrm((DEPTH, NSA_CMP_LEN, HEAD_DIM), 0.02),
        'rel_bias': nrm((N_BUCKETS, MIX_HEADS), 0.5),
        'ret_norm_g': gain((DEPTH, MIX_WIDTH)),
        'rwkv_mu': unif((DEPTH, RWKV_COLS), 0.0, 1.0),
        'rwkv_w0': unif((DEPTH, MIX_WIDTH), -6.0, 1.0),
        'rwkv_w2': nrm((DEPTH, RWKV_DECAY_LORA, MIX_WIDTH), 0.1),
        'rwkv_a0': nrm((DEPTH, MIX_WIDTH), 0.1),
        'rwkv_a2': nrm((DEPTH, RWKV_AAA_LORA, MIX_WIDTH), 0.1),
        'rwkv_g2': nrm((DEPTH, RWKV_GATE_LORA, MIX_WIDTH), RWKV_GATE_LORA ** -0.5),
        'rwkv_k_k': 0.85 + 0.02 * jax.random.normal(next(ks), (DEPTH, MIX_WIDTH), f32),
        'rwkv_k_a': gain((DEPTH, MIX_WIDTH)),
        'rwkv_r_k': nrm((DEPTH, MIX_WIDTH), 0.1),
        'rwkv_ln_g': gain((DEPTH, MIX_WIDTH)),
        'rwkv_ln_b': nrm((DEPTH, MIX_WIDTH), 0.02),
        'conv_w': nrm((DEPTH, CONV_WIDTH, MIX_WIDTH), CONV_WIDTH ** -0.5),
        'w_branch': nrm((DEPTH, N_BRANCHES, MIX_WIDTH, D_MODEL), MIX_WIDTH ** -0.5),
        'w_mix_out': nrm((DEPTH, D_MODEL, D_MODEL), D_MODEL ** -0.5),
        'ln_mix_post': gain((DEPTH, D_MODEL)),
        'ln_xa_pre': gain((DEPTH, D_MODEL)),
        'ln_mem': gain((DEPTH, D_MODEL)),
        'xa_wq': nrm((DEPTH, D_MODEL, D_MODEL), D_MODEL ** -0.5),
        'xa_wkv': nrm((DEPTH, D_MODEL, 2 * D_MODEL), D_MODEL ** -0.5),
        'xa_wo': nrm((DEPTH, D_MODEL, D_MODEL), D_MODEL ** -0.5),
        'ln_xa_post': gain((DEPTH, D_MODEL)),
        'ln_mlp_pre': gain((DEPTH, D_MODEL)),
        'mlp_w1': nrm((DEPTH, D_MODEL, D_FF), D_MODEL ** -0.5),
        'mlp_w2': nrm((DEPTH, D_FF, D_MODEL), D_FF ** -0.5),
        'ln_mlp_post': gain((DEPTH, D_MODEL)),
    }

def first_block(x, mem, ln_mix_pre, w_in, nsa_cmp_w, nsa_cmp_pe, rel_bias, ret_norm_g,
              rwkv_mu, rwkv_w0, rwkv_w2, rwkv_a0, rwkv_a2, rwkv_g2, rwkv_k_k, rwkv_k_a, rwkv_r_k,
              rwkv_ln_g, rwkv_ln_b, conv_w, w_branch, w_mix_out, ln_mix_post,
              ln_xa_pre, ln_mem, xa_wq, xa_wkv, xa_wo, ln_xa_post,
              ln_mlp_pre, mlp_w1, mlp_w2, ln_mlp_post):
    B, S, _ = x.shape
    for l in range(DEPTH):
        h = rms_norm(x, ln_mix_pre[l])
        z = h @ w_in[l]
        z_q, z_kv, z_g, z_ret, z_rwkv, z_conv, z_gate = split_cols(z, IN_SIZES)
        o_nsa = nsa_mixer(z_q.reshape(B, S, MIX_HEADS, HEAD_DIM), z_kv, z_g,
                          nsa_cmp_w[l], nsa_cmp_pe[l], rel_bias)
        r_q, r_k, r_v, r_g = jnp.split(z_ret, 4, axis=-1)
        o_ret = retention_mixer(r_q, r_k, r_v, r_g, ret_norm_g[l])
        o_rwkv = rwkv7_mixer(z_rwkv, rwkv_mu[l], rwkv_w0[l], rwkv_w2[l], rwkv_a0[l], rwkv_a2[l],
                             rwkv_g2[l], rwkv_k_k[l], rwkv_k_a[l], rwkv_r_k[l],
                             rwkv_ln_g[l], rwkv_ln_b[l])
        o_conv = short_conv_mixer(z_conv, conv_w[l])
        gates = jax.nn.sigmoid(z_gate).reshape(B, S, N_BRANCHES, D_MODEL)
        branches = (o_nsa, o_ret, o_rwkv, o_conv)
        merged = gates[:, :, 0] * (branches[0] @ w_branch[l, 0])
        for m in range(1, N_BRANCHES):
            merged = merged + gates[:, :, m] * (branches[m] @ w_branch[l, m])
        x = x + rms_norm(merged @ w_mix_out[l], ln_mix_post[l])

        h = rms_norm(x, ln_xa_pre[l])
        mn = rms_norm(mem, ln_mem[l])
        x = x + rms_norm(cross_attention(h, mn, xa_wq[l], xa_wkv[l], xa_wo[l]), ln_xa_post[l])

        h = rms_norm(x, ln_mlp_pre[l])
        x = x + rms_norm(jnp.square(jax.nn.relu(h @ mlp_w1[l])) @ mlp_w2[l], ln_mlp_post[l])
    return x


N_EVEN = (DEPTH + 1) // 2
N_ODD = DEPTH // 2
EPS = 1e-6
LRU_WIDTH = D_MODEL // 2
LRU_BLOCKS = 8
LRU_BLOCK = LRU_WIDTH // LRU_BLOCKS
CONV_W = 4
LRU_C = 8.0
FOX_HEADS = 8
FOX_HEAD_DIM = (D_MODEL // 2) // FOX_HEADS
FOX_WIDTH = FOX_HEADS * FOX_HEAD_DIM
EVEN_SPLITS = [LRU_WIDTH, 2 * LRU_WIDTH, 2 * LRU_WIDTH + FOX_WIDTH, 2 * LRU_WIDTH + 2 * FOX_WIDTH, 2 * LRU_WIDTH + 3 * FOX_WIDTH]
EVEN_IN = 2 * LRU_WIDTH + 3 * FOX_WIDTH + FOX_HEADS
GLA_HEADS = 4
GLA_DK = (D_MODEL // 2) // GLA_HEADS
GLA_DV = D_MODEL // GLA_HEADS
GLA_RANK = 16
GLA_TAU = 16.0
GLA_CHUNK = 64
GLA_KW = GLA_HEADS * GLA_DK
GLA_VW = GLA_HEADS * GLA_DV
ODD_SPLITS = [GLA_KW, 2 * GLA_KW, 2 * GLA_KW + GLA_VW, 2 * GLA_KW + 2 * GLA_VW]
ODD_IN = 2 * GLA_KW + 2 * GLA_VW + GLA_RANK
D_FF_2 = 2816
N_EXPERTS = 8
TOP_K = 2
D_FF_EXPERT = 3584


def rms_norm_2(x, g):
    xf = x.astype(jnp.float32)
    y = xf * lax.rsqrt(jnp.mean(xf * xf, axis=-1, keepdims=True) + EPS)
    return (y * g.astype(jnp.float32)).astype(x.dtype)

def causal_depthwise_conv(x, w, b):
    s = x.shape[1]
    xp = jnp.pad(x, ((0, 0), (CONV_W - 1, 0), (0, 0)))
    out = b
    for j in range(CONV_W):
        out = out + xp[:, j:j + s] * w[j]
    return out

def block_diag_linear(x, w, b):
    xb = x.reshape(x.shape[0], x.shape[1], LRU_BLOCKS, LRU_BLOCK)
    return jnp.einsum('bsni,nij->bsnj', xb, w).reshape(x.shape) + b

def rglru(x, ga_w, ga_b, gx_w, gx_b, lam):
    xf = x.astype(jnp.float32)
    r = jax.nn.sigmoid(block_diag_linear(xf, ga_w.astype(jnp.float32), ga_b.astype(jnp.float32)))
    i = jax.nn.sigmoid(block_diag_linear(xf, gx_w.astype(jnp.float32), gx_b.astype(jnp.float32)))
    log_a = -LRU_C * r * jax.nn.softplus(-lam.astype(jnp.float32))
    a = jnp.exp(log_a)
    u = jnp.sqrt(-jnp.expm1(2.0 * log_a)) * (i * xf)

    def combine(c1, c2):
        a1, b1 = c1
        a2, b2 = c2
        return a1 * a2, a2 * b1 + b2

    _, h = lax.associative_scan(combine, (a, u), axis=1)
    return h

def fox_attention(q, k, v, log_f):
    bsz, s, h, dh = q.shape
    nb = s // Q_BLOCK
    c = jnp.cumsum(log_f, axis=1).transpose(0, 2, 1)
    qh = q.transpose(0, 2, 1, 3) * (dh ** -0.5)
    kh = k.transpose(0, 2, 1, 3)
    vh = v.transpose(0, 2, 1, 3)
    qb = qh.reshape(bsz, h, nb, Q_BLOCK, dh).transpose(2, 0, 1, 3, 4)
    cb = c.reshape(bsz, h, nb, Q_BLOCK).transpose(2, 0, 1, 3)
    pos_b = jnp.arange(s).reshape(nb, Q_BLOCK)
    k_pos = jnp.arange(s)

    def one_block(args):
        q_blk, c_blk, p_blk = args
        logits = jnp.einsum('bhqd,bhkd->bhqk', q_blk, kh).astype(jnp.float32)
        logits = logits + c_blk[..., None] - c[:, :, None, :]
        mask = p_blk[:, None] >= k_pos[None, :]
        logits = jnp.where(mask, logits, -jnp.inf)
        p = jax.nn.softmax(logits, axis=-1)
        return jnp.einsum('bhqk,bhkd->bhqd', p.astype(vh.dtype), vh)

    ob = lax.map(one_block, (qb, cb, pos_b))
    return ob.transpose(1, 0, 3, 2, 4).reshape(bsz, s, h * dh)

def gla_chunked(q, k, v, log_a):
    bsz, s, h, dk = q.shape
    dv = v.shape[-1]
    n = s // GLA_CHUNK

    def chunks(t):
        return t.reshape(bsz, n, GLA_CHUNK, h, t.shape[-1]).transpose(1, 0, 3, 2, 4)

    qc, kc, vc, gc = chunks(q), chunks(k), chunks(v), chunks(log_a)
    b = jnp.cumsum(gc, axis=3)
    b_last = b[:, :, :, -1:, :]
    q_dec = qc * jnp.exp(b)
    k_intra = kc * jnp.exp(-b)
    k_state = kc * jnp.exp(b_last - b)
    chunk_decay = jnp.exp(b_last[:, :, :, 0, :])
    causal = jnp.tril(jnp.ones((GLA_CHUNK, GLA_CHUNK), dtype=bool))
    scores = jnp.where(causal, jnp.einsum('nbhid,nbhjd->nbhij', q_dec, k_intra), 0.0)
    o_intra = jnp.einsum('nbhij,nbhje->nbhie', scores, vc)

    def step(state, xs):
        q_n, k_n, v_n, d_n = xs
        o_n = jnp.einsum('bhid,bhde->bhie', q_n, state)
        state = d_n[..., None] * state + jnp.einsum('bhjd,bhje->bhde', k_n, v_n)
        return state, o_n

    state0 = jnp.zeros((bsz, h, dk, dv), jnp.float32)
    _, o_inter = lax.scan(step, state0, (q_dec, k_state, vc, chunk_decay))
    o = o_intra + o_inter
    return o.transpose(1, 0, 3, 2, 4).reshape(bsz, s, h, dv)

def even_mixer(hn, w_in, conv_w, conv_b, ga_w, ga_b, gx_w, gx_b, lam, f_b, w_out):
    bsz, s, _ = hn.shape
    proj = hn @ w_in
    xr, yr, q, k, v, f_logit = jnp.split(proj, EVEN_SPLITS, axis=-1)
    xc = causal_depthwise_conv(xr, conv_w, conv_b)
    h_lru = rglru(xc, ga_w, ga_b, gx_w, gx_b, lam)
    y_a = (h_lru * jax.nn.gelu(yr.astype(jnp.float32))).astype(hn.dtype)
    log_f = jax.nn.log_sigmoid((f_logit + f_b).astype(jnp.float32))
    shp = (bsz, s, FOX_HEADS, FOX_HEAD_DIM)
    y_b = fox_attention(q.reshape(shp), k.reshape(shp), v.reshape(shp), log_f).astype(hn.dtype)
    return jnp.concatenate([y_a, y_b], axis=-1) @ w_out

def odd_mixer(hn, w_in, gate_w2, gate_b, head_norm, w_out):
    bsz, s, _ = hn.shape
    proj = hn @ w_in
    q, k, v, g, lr = jnp.split(proj, ODD_SPLITS, axis=-1)
    log_a = jax.nn.log_sigmoid((lr @ gate_w2 + gate_b).astype(jnp.float32)) / GLA_TAU
    kshp = (bsz, s, GLA_HEADS, GLA_DK)
    o = gla_chunked((q.astype(jnp.float32) * (GLA_DK ** -0.5)).reshape(kshp),
                    k.astype(jnp.float32).reshape(kshp),
                    v.astype(jnp.float32).reshape(bsz, s, GLA_HEADS, GLA_DV),
                    log_a.reshape(kshp))
    o = o * lax.rsqrt(jnp.mean(o * o, axis=-1, keepdims=True) + EPS)
    o = o * head_norm.astype(jnp.float32).reshape(GLA_HEADS, GLA_DV)
    o = o.reshape(bsz, s, GLA_VW) * jax.nn.silu(g.astype(jnp.float32))
    return o.astype(hn.dtype) @ w_out

def swiglu(hn, w1, w3, w2):
    return (jax.nn.silu(hn @ w1) * (hn @ w3)) @ w2

def moe_swiglu(hn, router, w1, w3, w2):
    bsz, s, d = hn.shape
    t = hn.reshape(-1, d)
    logits = (t @ router).astype(jnp.float32)
    top_vals, top_idx = lax.top_k(logits, TOP_K)
    top_w = jax.nn.softmax(top_vals, axis=-1)
    gates = jnp.sum(top_w[..., None] * jax.nn.one_hot(top_idx, N_EXPERTS, dtype=jnp.float32), axis=1)
    out = jnp.zeros_like(t)
    for e in range(N_EXPERTS):
        h_e = jax.nn.silu(t @ w1[e]) * (t @ w3[e])
        out = out + gates[:, e:e + 1].astype(t.dtype) * (h_e @ w2[e])
    return out.reshape(bsz, s, d)

def second_inputs(seed: int = 0) -> dict:
    key = jax.random.key(seed)
    ks = iter(jax.random.split(key, 32))
    f32 = jnp.float32
    out_scale = (2.0 * DEPTH) ** -0.5

    def dense(shape, fan_in, scale=1.0):
        return jax.random.normal(next(ks), shape, f32) * (scale * fan_in ** -0.5)

    def gain(shape):
        return 1.0 + 0.02 * jax.random.normal(next(ks), shape, f32)

    def small(shape):
        return 0.02 * jax.random.normal(next(ks), shape, f32)

    x = jax.random.normal(next(ks), (BATCH, SEQ, D_MODEL), f32)
    norm_mix = gain((DEPTH, D_MODEL))
    norm_ffn = gain((DEPTH, D_MODEL))
    norm_final = gain((D_MODEL,))
    ev_w_in = dense((N_EVEN, D_MODEL, EVEN_IN), D_MODEL)
    ev_conv_w = dense((N_EVEN, CONV_W, LRU_WIDTH), CONV_W)
    ev_conv_b = small((N_EVEN, LRU_WIDTH))
    ev_ga_w = dense((N_EVEN, LRU_BLOCKS, LRU_BLOCK, LRU_BLOCK), LRU_BLOCK)
    ev_ga_b = small((N_EVEN, LRU_WIDTH))
    ev_gx_w = dense((N_EVEN, LRU_BLOCKS, LRU_BLOCK, LRU_BLOCK), LRU_BLOCK)
    ev_gx_b = small((N_EVEN, LRU_WIDTH))
    u = jax.random.uniform(next(ks), (N_EVEN, LRU_WIDTH), f32, minval=0.9, maxval=0.999)
    p = u ** (1.0 / LRU_C)
    ev_lambda = jnp.log(p) - jnp.log1p(-p)
    ev_f_b = 2.0 + 0.1 * jax.random.normal(next(ks), (N_EVEN, FOX_HEADS), f32)
    ev_w_out = dense((N_EVEN, D_MODEL, D_MODEL), D_MODEL, out_scale)
    ev_ffn_w1 = dense((N_EVEN, D_MODEL, D_FF_2), D_MODEL)
    ev_ffn_w3 = dense((N_EVEN, D_MODEL, D_FF_2), D_MODEL)
    ev_ffn_w2 = dense((N_EVEN, D_FF_2, D_MODEL), D_FF_2, out_scale)
    od_w_in = dense((N_ODD, D_MODEL, ODD_IN), D_MODEL)
    od_gate_w2 = dense((N_ODD, GLA_RANK, GLA_KW), GLA_RANK)
    od_gate_b = small((N_ODD, GLA_KW))
    od_head_norm = gain((N_ODD, GLA_VW))
    od_w_out = dense((N_ODD, GLA_VW, D_MODEL), GLA_VW, out_scale)
    od_router = dense((N_ODD, D_MODEL, N_EXPERTS), D_MODEL)
    od_exp_w1 = dense((N_ODD, N_EXPERTS, D_MODEL, D_FF_EXPERT), D_MODEL)
    od_exp_w3 = dense((N_ODD, N_EXPERTS, D_MODEL, D_FF_EXPERT), D_MODEL)
    od_exp_w2 = dense((N_ODD, N_EXPERTS, D_FF_EXPERT, D_MODEL), D_FF_EXPERT, out_scale)
    return {"x": x, "norm_mix": norm_mix, "norm_ffn": norm_ffn, "norm_final": norm_final,
            "ev_w_in": ev_w_in, "ev_conv_w": ev_conv_w, "ev_conv_b": ev_conv_b,
            "ev_ga_w": ev_ga_w, "ev_ga_b": ev_ga_b, "ev_gx_w": ev_gx_w, "ev_gx_b": ev_gx_b,
            "ev_lambda": ev_lambda, "ev_f_b": ev_f_b, "ev_w_out": ev_w_out,
            "ev_ffn_w1": ev_ffn_w1, "ev_ffn_w3": ev_ffn_w3, "ev_ffn_w2": ev_ffn_w2,
            "od_w_in": od_w_in, "od_gate_w2": od_gate_w2, "od_gate_b": od_gate_b,
            "od_head_norm": od_head_norm, "od_w_out": od_w_out, "od_router": od_router,
            "od_exp_w1": od_exp_w1, "od_exp_w3": od_exp_w3, "od_exp_w2": od_exp_w2}

def second_block(x, norm_mix, norm_ffn, norm_final,
              ev_w_in, ev_conv_w, ev_conv_b, ev_ga_w, ev_ga_b, ev_gx_w, ev_gx_b,
              ev_lambda, ev_f_b, ev_w_out, ev_ffn_w1, ev_ffn_w3, ev_ffn_w2,
              od_w_in, od_gate_w2, od_gate_b, od_head_norm, od_w_out, od_router,
              od_exp_w1, od_exp_w3, od_exp_w2):
    h = x
    for layer in range(DEPTH):
        j = layer // 2
        hn = rms_norm_2(h, norm_mix[layer])
        if layer % 2 == 0:
            h = h + even_mixer(hn, ev_w_in[j], ev_conv_w[j], ev_conv_b[j], ev_ga_w[j], ev_ga_b[j],
                               ev_gx_w[j], ev_gx_b[j], ev_lambda[j], ev_f_b[j], ev_w_out[j])
            h = h + swiglu(rms_norm_2(h, norm_ffn[layer]), ev_ffn_w1[j], ev_ffn_w3[j], ev_ffn_w2[j])
        else:
            h = h + odd_mixer(hn, od_w_in[j], od_gate_w2[j], od_gate_b[j], od_head_norm[j], od_w_out[j])
            h = h + moe_swiglu(rms_norm_2(h, norm_ffn[layer]), od_router[j], od_exp_w1[j],
                               od_exp_w3[j], od_exp_w2[j])
    return rms_norm_2(h, norm_final)


def setup_inputs(seed=0):
    out = dict(first_inputs(seed))
    for name, value in second_inputs(seed + 1).items():
        if name != "x":
            out[name + "_2"] = value
    return out


def reference(
    x, mem, ln_mix_pre, w_in, nsa_cmp_w, nsa_cmp_pe, rel_bias, ret_norm_g, rwkv_mu, rwkv_w0,
    rwkv_w2, rwkv_a0, rwkv_a2, rwkv_g2, rwkv_k_k, rwkv_k_a, rwkv_r_k, rwkv_ln_g, rwkv_ln_b,
    conv_w, w_branch, w_mix_out, ln_mix_post, ln_xa_pre, ln_mem, xa_wq, xa_wkv, xa_wo,
    ln_xa_post, ln_mlp_pre, mlp_w1, mlp_w2, ln_mlp_post, norm_mix_2, norm_ffn_2, norm_final_2,
    ev_w_in_2, ev_conv_w_2, ev_conv_b_2, ev_ga_w_2, ev_ga_b_2, ev_gx_w_2, ev_gx_b_2,
    ev_lambda_2, ev_f_b_2, ev_w_out_2, ev_ffn_w1_2, ev_ffn_w3_2, ev_ffn_w2_2, od_w_in_2,
    od_gate_w2_2, od_gate_b_2, od_head_norm_2, od_w_out_2, od_router_2, od_exp_w1_2,
    od_exp_w3_2, od_exp_w2_2,
):
    x = first_block(
        x, mem, ln_mix_pre, w_in, nsa_cmp_w, nsa_cmp_pe, rel_bias, ret_norm_g, rwkv_mu, rwkv_w0,
        rwkv_w2, rwkv_a0, rwkv_a2, rwkv_g2, rwkv_k_k, rwkv_k_a, rwkv_r_k, rwkv_ln_g, rwkv_ln_b,
        conv_w, w_branch, w_mix_out, ln_mix_post, ln_xa_pre, ln_mem, xa_wq, xa_wkv, xa_wo,
        ln_xa_post, ln_mlp_pre, mlp_w1, mlp_w2, ln_mlp_post,
    )
    return second_block(
        x, norm_mix_2, norm_ffn_2, norm_final_2, ev_w_in_2, ev_conv_w_2, ev_conv_b_2, ev_ga_w_2,
        ev_ga_b_2, ev_gx_w_2, ev_gx_b_2, ev_lambda_2, ev_f_b_2, ev_w_out_2, ev_ffn_w1_2,
        ev_ffn_w3_2, ev_ffn_w2_2, od_w_in_2, od_gate_w2_2, od_gate_b_2, od_head_norm_2,
        od_w_out_2, od_router_2, od_exp_w1_2, od_exp_w3_2, od_exp_w2_2,
    )


_drawn_inputs = setup_inputs


def setup_inputs(seed=0):
    import zlib

    import numpy as np

    out = dict(_drawn_inputs(seed))
    spreads = {}
    factors = {'nsa_cmp_pe': 5.785,
     'ret_norm_g': 5.321,
     'rwkv_w2': 3.366,
     'rwkv_a0': 2.883,
     'rwkv_k_k': 5.744,
     'rwkv_k_a': 4.569,
     'rwkv_ln_g': 5.78,
     'rwkv_ln_b': 6.197,
     'ln_xa_pre': 2.961,
     'ln_xa_post': 2.781,
     'ln_mlp_pre': 3.108,
     'ln_mlp_post': 3.304,
     'norm_mix_2': 6.098,
     'norm_ffn_2': 5.494,
     'norm_final_2': 8.184,
     'ev_conv_b_2': 6.596,
     'ev_ga_w_2': 3.684,
     'ev_ga_b_2': 27.174,
     'ev_gx_b_2': 8.0,
     'ev_f_b_2': 62.812,
     'od_gate_b_2': 8.0,
     'od_head_norm_2': 25.347}
    for name, (base, spread) in spreads.items():
        noise = np.random.default_rng([zlib.crc32(name.encode()), seed]).standard_normal(out[name].shape)
        drawn = base * np.exp(spread * noise) if base else spread * noise
        out[name] = jnp.asarray(drawn.astype(out[name].dtype))
    for name, factor in factors.items():
        out[name] = (out[name] * factor).astype(out[name].dtype)
    return out
```

```python
import math
from contextlib import ExitStack

import numpy as np

import concourse.bass as bass
from concourse import mybir

F32 = mybir.dt.float32
U32 = mybir.dt.uint32
I32 = mybir.dt.int32
ALU = mybir.AluOpType
ACT = mybir.ActivationFunctionType
AX = mybir.AxisListType.X

P = 128
D = 1024
T = 256
NT = T // P
KD = D // P
DEPTH = 2
HD = 64
H = 4
MW = H * HD
CH = 64
NC = T // CH
HC = H * NC
UNIT = 1024

Q0, KV0, G0, RET0, RWKV0, CONV0, GATE0 = np.cumsum([0, MW, 6 * HD, 3 * H, 4 * MW, 3 * MW + 128, 3 * MW]).tolist()
CMP_LEN, CMP_STRIDE = 32, 16
NCMP = (T - CMP_LEN) // CMP_STRIDE + 1
NBUCKET = 32
NEG = -1e30
SPAN = 2 * T
FF1, FF2, FFE = 4096, 2816, 3584
NEXP = 8
SLOTS = 128
STEP = 256
LEVELS = [2, 4, 8, 16, 32]
SIDE = (0, 1, 3, 2)

C_IDENT, C_RMASK, C_LEVEL, C_M1T, C_M1, C_SEL, C_IOTA, C_TMASK, C_CAUSAL, C_COS, C_SIN, C_ONES, C_ZEROS, C_EPS, C_BEFORE, C_W = np.cumsum(
    [0, 128, 128, 64 * len(LEVELS), 64, 64, NEXP * 128, SLOTS, 1, NT * T, NT * 32, NT * 32, 128, 128, 1, 128]).tolist()


def constants():
    c = np.zeros((P, C_W), np.float32)
    c[:, C_IDENT:C_IDENT + 128] = np.eye(128)
    i = np.arange(CH)
    c[:CH, C_RMASK:C_RMASK + 64] = i[:, None] < i[None, :]
    c[:CH, C_RMASK + 64:C_RMASK + 128] = i[:, None] <= i[None, :]
    for n, b in enumerate([1] + LEVELS):
        low = ((i[:, None] // (2 * b) == i[None, :] // (2 * b)) & (i[:, None] // b % 2 == 1) & (i[None, :] // b % 2 == 0))
        if b == 1:
            c[:CH, C_M1:C_M1 + 64] = -1.0 * low
            c[:CH, C_M1T:C_M1T + 64] = -1.0 * low.T
        else:
            c[:CH, C_LEVEL + 64 * (n - 1):C_LEVEL + 64 * n] = low.T
    for e in range(NEXP):
        c[e, C_SEL + 128 * e:C_SEL + 128 * (e + 1)] = 1.0
    c[:, C_IOTA:C_IOTA + SLOTS] = np.arange(SLOTS)
    c[:, C_TMASK] = np.arange(P) >= CMP_LEN - 1
    t = np.arange(T)
    for n in range(NT):
        tt = t[n * P:(n + 1) * P]
        c[:, C_CAUSAL + n * T:C_CAUSAL + (n + 1) * T] = np.where(tt[:, None] >= t[None, :], 0.0, NEG)
        freq = np.float32(10000.0) ** (-np.arange(32, dtype=np.float32) / np.float32(32))
        ang = tt.astype(np.float32)[:, None] * freq[None, :]
        c[:, C_COS + n * 32:C_COS + (n + 1) * 32] = np.cos(ang)
        c[:, C_SIN + n * 32:C_SIN + (n + 1) * 32] = np.sin(ang)
    c[:, C_ONES:C_ONES + 128] = 1.0
    c[:, C_BEFORE:C_BEFORE + P] = np.arange(P)[:, None] < np.arange(P)[None, :]
    c[:, C_EPS] = 1e-6
    decay = np.zeros((P, H, NT, T), np.float64)
    for h in range(H):
        lg = math.log(1.0 - 2.0 ** (-5.0 - h))
        for n in range(NT):
            diff = t[None, :] - t[n * P:(n + 1) * P, None]
            decay[:, h, n, :] = np.where(diff >= 0, np.exp(np.maximum(diff, 0) * lg), 0.0) * HD ** -0.5
    hot = np.zeros((NBUCKET + 1, SPAN), np.float32)
    for j in range(SPAN):
        d = T - 1 - j
        if d < 0:
            hot[NBUCKET, j] = 1.0
        elif d < NBUCKET // 2:
            hot[d, j] = 1.0
        else:
            half = NBUCKET // 2
            b = half + int(np.float32(np.log(np.float32(d) / np.float32(half))) / np.float32(math.log(128 / half)) * np.float32(half))
            hot[min(b, NBUCKET - 1), j] = 1.0
    return {"consts": c, "decay": decay.astype(np.float32).reshape(P, -1), "hot": hot}


class Signal:

    def __init__(self, nc, ctx, name):
        self.sem = ctx.enter_context(nc.semaphore(name))
        self.posted = 0
        self.taken = {}
        self.per_round = 0


class Loop:

    def __init__(self):
        self.reg = None
        self.touched = {}


def build(nc, a, out):
    ctx = ExitStack()
    signals = {}
    loop = Loop()

    def count_of(name):
        if name not in signals:
            signals[name] = Signal(nc, ctx, name)
        return signals[name]

    def sem(name):
        return count_of(name).sem

    def value(s, count):
        return count if loop.reg is None else loop.reg * s.per_round + count

    def up(name, by=1):
        s = count_of(name)
        s.posted += by
        if loop.reg is not None:
            loop.touched[(s, "")] = s.per_round
        return by

    def at(name):
        return value(count_of(name), count_of(name).posted)

    def due(who, name, by=1):
        s = count_of(name)
        s.taken[who] = s.taken.get(who, 0) + by
        if loop.reg is not None:
            loop.touched[(s, who)] = s.per_round
        return value(s, s.taken[who])

    def enter(reg):
        loop.reg = reg
        loop.touched = {}

    def leave(rounds):
        for (s, who), per in loop.touched.items():
            if who:
                s.taken[who] += per * (rounds - 1)
            else:
                s.posted += per * (rounds - 1)
        loop.reg = None

    def counts_now():
        return {n: (s.posted, dict(s.taken)) for n, s in signals.items()}

    def go_back(before):
        for n, s in signals.items():
            posted, taken = before.get(n, (0, {}))
            s.posted, s.taken = posted, dict(taken)

    def sb(name, shape, dt=F32):
        return ctx.enter_context(nc.sbuf_tensor(name, shape, dt))

    with ctx:
        x = sb("x", [P, NT, D])
        hT = sb("hT", [P, KD, T])
        fbT = sb("fbT", [P, 8 * UNIT])
        bias = fbT[:, 0:2048].rearrange("p (t h s) -> p t h s", t=NT, h=H)
        decay = fbT[:, 2048:4096].rearrange("p (h n t) -> p h n t", h=H, n=NT)
        oT = fbT[:, 4096:6144].rearrange("p (m k t) -> p m k t", m=4, k=2)
        memT = fbT[:, 6144:8192].rearrange("p (k t) -> p k t", k=KD)
        merged = sb("merged", [P, KD, T])
        gainrow = sb("gainrow", [P, D])
        slabA = sb("slabA", [P, 2, 4096])
        slabB = sb("slabB", [P, 2, 2048])
        work = sb("work", [P, 16 * UNIT])
        cst = sb("cst", [P, C_W])
        resets = sb("resets", [P, HC, CH])
        ps = ctx.enter_context(nc.psum_tensor("ps", [P, 8, 512], F32))
        stat = sb("stat", [P, 64])
        st2 = sb("st2", [P, 64])

        def U(n, units=1, off=0, size=None, parts=P):
            size = units * UNIT if size is None else size
            return work[0:parts, n * UNIT + off:n * UNIT + off + size]

        def banks(b, n=1, parts=P):
            return ps[0:parts, b:b + n, :].rearrange("p b c -> p (b c)")

        ident = cst[:, C_IDENT:C_IDENT + 128]
        ones = cst[:, C_ONES:C_ONES + 64]
        zeros = cst[:, C_ZEROS:C_ZEROS + 128]
        sel = cst[0:NEXP, C_SEL:C_SEL + NEXP * 128].rearrange("p (e m) -> p e m", e=NEXP)
        causal = cst[:, C_CAUSAL:C_CAUSAL + NT * T].rearrange("p (n t) -> p n t", n=NT)

        gT = {n: sb(n, [P, DEPTH, KD]) for n in ("ln_mix_pre", "ln_xa_pre", "ln_mem", "ln_mlp_pre", "norm_mix_2", "norm_ffn_2")}
        peT = sb("peT", [HD, DEPTH, CMP_LEN])
        relb = sb("relb", [NBUCKET + 1, H])
        retg = sb("retg", [P, DEPTH, MW])
        muT = sb("muT", [HD, DEPTH, 15])
        vecs = {n: sb(n, [HD, DEPTH, H]) for n in ("rwkv_w0", "rwkv_a0", "rwkv_k_k", "rwkv_k_a", "rwkv_r_k")}
        lng = sb("lng", [HD, DEPTH, MW])
        lnb = sb("lnb", [HD, DEPTH, MW])
        w2s = sb("w2s", [32, DEPTH, MW])
        a2s = sb("a2s", [32, DEPTH, MW])
        g2s = sb("g2s", [HD, DEPTH, MW])
        convw = sb("convw", [P, DEPTH, 3, 2])
        convw2 = sb("convw2", [P, 4, 4])
        vec2 = {n: sb(n, [P, 4]) for n in ("ev_conv_b_2", "ev_ga_b_2", "ev_gx_b_2", "ev_lambda_2", "od_gate_b_2")}
        fb = sb("fb", [8, 1])
        gw2 = sb("gw2", [16, 512])
        routw = sb("routw", [P, KD, NEXP])

        pick = fbT[:, 0:2048].rearrange("p (e t c) -> p e t c", e=NEXP, t=NT)
        pick_gate = fbT[:, 2048:4096].rearrange("p (e t c) -> p e t c", e=NEXP, t=NT)
        spread = fbT[:, 4096:6144]
        chosen = fbT[:, 6144:6160].rearrange("p (t e) -> p t e", t=NT)
        slot = fbT[:, 6160:6176].rearrange("p (t e) -> p t e", t=NT)
        load = fbT[:, 6176:6184]
        most = fbT[0:1, 6184:6185]
        most_int = fbT[0:1, 6185:6186].bitcast(I32)
        slot_x = U(8).rearrange("p (k c) -> p k c", k=KD)
        spread_e = U(9, size=T)
        slot_y = U(10)

        toep = nc.dram_tensor("toep", (H, P, SPAN), F32, kind="Internal").ap()

        class Ring:

            def __init__(self, name, buf):
                self.name, self.buf, self.used = name, buf, f"{name}_used"
                self.loaded = self.taken = 0

            def load(self, sp, parts):
                n = self.loaded
                self.loaded += 1
                if n >= 2:
                    sp.wait_ge(sem(self.used), due("sp", self.used))
                full = f"{self.name}_full{n % 2}"
                for dst, src in parts:
                    sp.dma_start(dst(self.buf[:, n % 2, :]), src).then_inc(sem(full), up(full, 16))

            def take(self, pe, parts=1):
                n = self.taken
                self.taken += 1
                full = f"{self.name}_full{n % 2}"
                pe.wait_ge(sem(full), due("pe", full, 16 * parts))
                return self.buf[:, n % 2, :]

        ringA, ringB = Ring("slabA", slabA), Ring("slabB", slabB)

        def cols(w, c0, n, pk=True):
            src = w.rearrange("(p k) n -> p k n" if pk else "(k p) n -> p k n", p=P)[:, :, c0:c0 + n]
            return (lambda s: s[:, 0:KD * n].rearrange("p (k n) -> p k n", k=KD)), src

        def kview(slab, n):
            return slab[:, 0:KD * n].rearrange("p (k n) -> p k n", k=KD)

        for name, by in (("slabA_full0", 16 * 2 * 7), ("slabA_full1", 16 * 2 * 7), ("slabB_full0", 16 * 7), ("slabB_full1", 16 * 7),
                         ("slabA_used", 14), ("slabB_used", 14), ("hidden_psum", 28), ("hidden_act", 28),
                         ("hidden_ready", 28), ("gate_order", 28),
                         ("slot_hidden_psum", 14), ("slot_hidden_act", 14), ("slot_hidden_ready", 14), ("slot_x_psum", 1),
                         ("slot_spread", 1), ("slot_x", 1), ("slot_y_psum", 1), ("slot_y", 1)):
            count_of(name).per_round = by

        block = ctx.enter_context(nc.Block())

        @block.sync
        def _(sp):
            def linear(w, n, pk=True):
                for c0 in range(0, n, 512):
                    ringA.load(sp, [cols(w, c0, min(512, n - c0), pk)])

            def ffn_step(w1, w3, w2, c0):
                def half(i):
                    return lambda s: s[:, 2048 * i:2048 * (i + 1)].rearrange("p (k n) -> p k n", k=KD)
                srcs = [w.rearrange("(p k) n -> p k n", p=P)[:, :, c0:c0 + STEP] for w in ([w1, w3] if w3 is not None else [w1])]
                ringA.load(sp, [(half(i), s) for i, s in enumerate(srcs)])
                ringB.load(sp, [(lambda s: s.rearrange("p (j n) -> p j n", j=2),
                                 w2[c0:c0 + STEP, :].rearrange("(j p) n -> p j n", p=P))])

            for l in range(DEPTH):
                w = a["w_in"][l]
                ringA.load(sp, [cols(w, 0, 512)])
                ringA.load(sp, [cols(w, 512, RET0 - 512)])
                ringA.load(sp, [(lambda s: s[0:HD, :].rearrange("d (c e) -> d c e", e=HD),
                                 a["nsa_cmp_w"][l].rearrange("c l d e -> d (c l) e"))])
                for c0, c1 in ((RET0, RET0 + 512), (RET0 + 512, RWKV0), (CONV0, CONV0 + 512), (CONV0 + 512, GATE0),
                               (RWKV0, RWKV0 + 512), (RWKV0 + 512, CONV0)):
                    ringA.load(sp, [cols(w, c0, c1 - c0)])
                for m in SIDE:
                    for half in range(2):
                        ringA.load(sp, [cols(w, GATE0 + m * D + half * 512, 512)])
                        if half == 0:
                            ringB.load(sp, [(lambda s: s.rearrange("p (k n) -> p k n", k=2),
                                             a["w_branch"][l][m].rearrange("(k p) n -> p k n", p=P))])
                linear(a["w_mix_out"][l], D, False)
                linear(a["xa_wq"][l], D)
                linear(a["xa_wkv"][l], 2 * D)
                linear(a["xa_wo"][l], D, False)
                for i in range(FF1 // STEP):
                    ffn_step(a["mlp_w1"][l], None, a["mlp_w2"][l], i * STEP)
            linear(a["ev_w_in_2"][0], 2568)
            linear(a["ev_w_out_2"][0], D, False)
            for i in range(FF2 // STEP):
                ffn_step(a["ev_ffn_w1_2"][0], a["ev_ffn_w3_2"][0], a["ev_ffn_w2_2"][0], i * STEP)
            linear(a["od_w_in_2"][0], 3088)
            linear(a["od_w_out_2"][0], D, False)
            with sp.Fori(0, NEXP) as e:
                enter(e)
                for i in range(FFE // STEP):
                    c = slice(i * STEP, (i + 1) * STEP)
                    ringA.load(sp, [((lambda s, w=w: s[:, 2048 * w:2048 * (w + 1)].rearrange("p (k n) -> p k n", k=KD)),
                                     a[n][0].rearrange("e (p k) n -> p e k n", p=P)[:, bass.ds(e, 1), :, c].rearrange("p e k n -> p (e k) n"))
                                    for w, n in enumerate(("od_exp_w1_2", "od_exp_w3_2"))])
                    ringB.load(sp, [(lambda s: s.rearrange("p (j n) -> p j n", j=2),
                                     a["od_exp_w2_2"][0][:, c, :].rearrange("e (j p) n -> p e j n", p=P)[:, bass.ds(e, 1), :, :].rearrange("p e j n -> p (e j) n"))])
                leave(NEXP)
            sp.wait_ge(sem("result_rows"), due("sp", "result_rows", NT))
            sp.dma_start(out.rearrange("b (n p) d -> p (b n) d", p=P), x[:, :, :]).then_inc(sem("result_out"), up("result_out", 16))
            sp.wait_ge(sem("result_out"), due("sp", "result_out", 16))

        posts = ("ln_mix_post", "ln_xa_post", "ln_mlp_post")

        PROJ = 3
        proj = {"pe": 0, "act": 0, "held": 0}

        @block.gpsimd
        def _(pool):
            def small(dst, src):
                pool.dma_start(dst, src).then_inc(sem("params_loaded"), up("params_loaded", 16))

            def row(ap1, parts):
                return bass.AP(tensor=ap1.tensor, offset=ap1.offset, ap=[[0, parts], [1, ap1.shape[0]]])

            def sum_branches():
                for u in range(4 * KD):
                    m, c = u // KD, u % KD
                    gate, branch = (gainrow[:, (u % 2 * 2 + i) * T:(u % 2 * 2 + i + 1) * T] for i in range(2))
                    pool.wait_ge(sem("side_gate"), due("pool", "side_gate"))
                    if m == 0:
                        nc.gpsimd.tensor_tensor(merged[:, c, :], gate, branch, ALU.mult).then_inc(sem("side_summed"), up("side_summed"))
                        pool.wait_ge(sem("side_summed"), at("side_summed"))
                    else:
                        nc.gpsimd.tensor_tensor(gate, gate, branch, ALU.mult).then_inc(sem("side_product"), up("side_product"))
                        pool.wait_ge(sem("side_product"), at("side_product"))
                        nc.gpsimd.tensor_tensor(merged[:, c, :], merged[:, c, :], gate, ALU.add).then_inc(sem("side_summed"), up("side_summed"))
                        pool.wait_ge(sem("side_summed"), at("side_summed"))

            pool.dma_start(x[:, :, :], a["x"].rearrange("b (n p) d -> p (b n) d", p=P)).then_inc(sem("x_loaded"), up("x_loaded", 16))
            pool.dma_start(cst[:, :], a["consts"]).then_inc(sem("consts_loaded"), up("consts_loaded", 16))
            pool.dma_start(merged[:, :, :].rearrange("p k t -> p (k t)").rearrange("p (n d) -> p n d", n=NT),
                                a["mem"].rearrange("b (n p) d -> p (b n) d", p=P)).then_inc(sem("consts_loaded"), up("consts_loaded", 16))
            pool.wait_ge(sem("cleared"), due("pool", "cleared", 1))
            with nc.allow_non_contiguous_dma(reason="small parameters, once"):
                small(relb[0:NBUCKET, :], a["rel_bias"])
                small(U(0, size=SPAN, parts=NBUCKET + 1), a["hot"])
                small(fbT[:, 2048:4096], a["decay"])
                for n, t in gT.items():
                    small(t[:, :, :], a[n].rearrange("l (p k) -> p l k", p=P))
                small(peT[:, :, :], a["nsa_cmp_pe"].rearrange("l n d -> d l n"))
                for l in range(DEPTH):
                    small(muT[:, l, 0:12], a["rwkv_mu"][l, 0:768].rearrange("(g p) -> p g", p=HD))
                    small(muT[0:32, l, 12:14], a["rwkv_mu"][l, 768:832].rearrange("(g p) -> p g", p=32))
                    small(muT[:, l, 14:15], a["rwkv_mu"][l, 832:896].rearrange("(g p) -> p g", p=HD))
                    small(retg[:, l, :], row(a["ret_norm_g"][l], P))
                    small(lng[:, l, :], row(a["rwkv_ln_g"][l], HD))
                    small(lnb[:, l, :], row(a["rwkv_ln_b"][l], HD))
                    small(convw[:, l, :, :], a["conv_w"][l].rearrange("j (k p) -> p j k", p=P))
                for n, t in vecs.items():
                    small(t[:, :, :], a[n].rearrange("l (h p) -> p l h", p=HD))
                small(w2s[:, :, :], a["rwkv_w2"].rearrange("l r c -> r l c"))
                small(a2s[:, :, :], a["rwkv_a2"].rearrange("l r c -> r l c"))
                small(g2s[:, :, :], a["rwkv_g2"].rearrange("l r c -> r l c"))
                small(convw2[:, :, :], a["ev_conv_w_2"][0].rearrange("j (k p) -> p j k", p=P))
                for n, t in vec2.items():
                    small(t[:, :], a[n][0].rearrange("(k p) -> p k", p=P))
                small(fb[:, :], a["ev_f_b_2"].rearrange("a h -> h a"))
                small(gw2[:, :], a["od_gate_w2_2"][0])
                small(routw[:, :, :], a["od_router_2"][0].rearrange("(p k) e -> p k e", p=P))
                pool.wait_ge(sem("bias_rows"), due("pool", "bias_rows"))
                pool.dma_start(toep.rearrange("h p j -> p h j"), U(2, 2).rearrange("p (h j) -> p h j", h=H)).then_inc(sem("bias_out"), up("bias_out", 16))
                pool.wait_ge(sem("bias_out"), due("pool", "bias_out", 16))
                for n in range(NT):
                    src = bass.AP(tensor=toep.tensor, offset=toep.offset + T - 1 - P * n,
                                  ap=[[SPAN - 1, P], [P * SPAN, H], [1, T]])
                    pool.dma_start(bias[:, n, :, :], src).then_inc(sem("bias_table"), up("bias_table", 16))
                first = True
                for l in range(DEPTH):
                    for n in posts:
                        if n == "ln_mix_post":
                            sum_branches()
                        if not first:
                            pool.wait_ge(sem("gainrow_used"), due("pool", "gainrow_used"))
                        first = False
                        pool.dma_start(gainrow[:, :], row(a[n][l], P)).then_inc(sem("gainrow_loaded"), up("gainrow_loaded", 16))
                pool.wait_ge(sem("lru_gate_cleared"), due("pool", "lru_gate_cleared"))
                gd = fbT[:, 0:1024].rearrange("p (w c n) -> p w c n", w=2, c=4)
                for w, n in enumerate(("ev_ga_w_2", "ev_gx_w_2")):
                    for half in range(2):
                        r = slice(HD * half, HD * (half + 1))
                        pool.dma_start(gd[r, w, :, r], a[n][0].rearrange("(c f) i j -> f i c j", f=2)[half]).then_inc(sem("lru_gate_loaded"), up("lru_gate_loaded", 16))
                for src in (a["od_head_norm_2"][0], a["norm_final_2"]):
                    pool.wait_ge(sem("gainrow_used"), due("pool", "gainrow_used"))
                    pool.dma_start(gainrow[:, :], row(src, P)).then_inc(sem("gainrow_loaded"), up("gainrow_loaded", 16))


        @block.tensor
        def _(pe):
            mm = nc.tensor.matmul

            def tr(o, i, n):
                return nc.tensor.transpose(o, i, ident[0:n, 0:n])

            def add_zero(o):
                return mm(o, zeros[0:1, 0:o.shape[0]], zeros[0:1, 0:1], start=False, stop=True, skip_group_check=True)

            side = {}

            def group(pieces, done=None):
                g = proj["pe"]
                proj["pe"] += 1
                if proj["held"] == PROJ:
                    pe.wait_ge(sem("proj_free"), due("pe", "proj_free"))
                else:
                    proj["held"] += 1
                for lhs, rhs, rows, c0, n in pieces:
                    for k in range(KD):
                        last = mm(ps[0:rows, g % PROJ, c0:c0 + n], lhs(k), rhs(k), start=(k == 0), stop=(k == KD - 1))
                if done is None:
                    last.then_inc(sem("proj_ready"), up("proj_ready"))
                else:
                    last.then_inc(sem(done.used), up(done.used))
                    lhs, rhs, rows, c0, n = pieces[-1]
                    add_zero(ps[0:min(rows, 32), g % PROJ, c0:c0 + 1]).then_inc(sem("proj_ready"), up("proj_ready"))

            def chT(slab, n, c0, width, dst=0):
                v = kview(slab, n)
                return (lambda k: v[:, k, c0:c0 + width]), (lambda k: hT[:, k, :]), width, dst, T

            def rowsof(slab, n, c0, width, t, dst=0, src=None):
                v, s = kview(slab, n), (hT if src is None else src)
                return (lambda k: s[:, k, t * P:(t + 1) * P]), (lambda k: v[:, k, c0:c0 + width]), P, dst, width

            def norm_T(src):
                for t in range(NT):
                    pe.wait_ge(sem("norm_rows"), due("pe", "norm_rows"))
                    for half in range(2):
                        b = 4 + 2 * t + half
                        for j in range(4):
                            k = 4 * half + j
                            last = tr(ps[:, b, j * P:(j + 1) * P], src[:, t, k::KD], P)
                        last.then_inc(sem("norm_T"), up("norm_T"))

            def take_hT():
                pe.wait_ge(sem("hT_ready"), due("pe", "hT_ready"))

            def softmax_T(n_keys):
                pe.wait_ge(sem("weights_ready"), due("pe", "weights_ready"))
                S = U(0)
                n_st = max(1, n_keys // P)
                w = min(n_keys, P)
                for h in range(4):
                    for s in range(n_st):
                        last = tr(banks(6, 2, w)[:, (h * n_st + s) * P:(h * n_st + s + 1) * P],
                                  S[:, h * n_keys + s * P:h * n_keys + s * P + w], P)
                last.then_inc(sem("weightsT_psum"), up("weightsT_psum"))
                pe.wait_ge(sem("weightsT_ready"), due("pe", "weightsT_ready"))

            def nsa():
                qT = U(2, parts=HD).rearrange("p (h t) -> p h t", h=H)
                kT = U(3, parts=HD).rearrange("p (h t) -> p h t", h=H)
                vr = U(4, size=256).rearrange("p (t c) -> p t c", t=NT)
                take_hT()
                s = ringA.take(pe)
                for i in range(2):
                    group([chT(s, 512, Q0 + P * i, P)])
                group([chT(s, 512, KV0, P)])
                group([chT(s, 512, KV0 + P, HD)])
                group([rowsof(s, 512, KV0 + P + HD, HD, t, HD * t) for t in range(NT)], ringA)
                n = RET0 - 512
                s = ringA.take(pe)
                group([chT(s, n, 0, HD)])
                group([rowsof(s, n, HD, n - HD, t, P * t) for t in range(NT)], ringA)
                cw = ringA.take(pe)[0:HD, :].rearrange("d (c l e) -> d c l e", c=2, l=CMP_LEN)
                X = U(5, parts=HD, size=2 * NCMP * CMP_LEN).rearrange("p (c n l) -> p c n l", c=2, l=CMP_LEN)
                pe.wait_ge(sem("cmp_windows"), due("pe", "cmp_windows"))
                for i in range(CMP_LEN):
                    mm(ps[0:HD, 4, 0:NCMP], cw[:, 0, i, :], X[:, 0, :, i], start=(i == 0), stop=(i == CMP_LEN - 1))
                for i in range(CMP_LEN):
                    last = mm(ps[0:NCMP, 4, 64:64 + HD], X[:, 1, :, i], cw[:, 1, i, :], start=(i == 0), stop=(i == CMP_LEN - 1))
                last.then_inc(sem("slabA_used"), up("slabA_used"))
                add_zero(ps[0:NCMP, 4, 64:65]).then_inc(sem("cmp_psum"), up("cmp_psum"))
                kcT = U(4, off=256, size=NCMP, parts=HD)
                vc = U(4, off=320, size=HD, parts=NCMP)
                pe.wait_ge(sem("cmp_ready"), due("pe", "cmp_ready"))
                mm(ps[:, 3, :], zeros[0:1, :], cst[0:1, C_SEL:C_SEL + 512], start=True, stop=False, skip_group_check=True)
                for t in range(NT):
                    for kind in range(3):
                        n = (NCMP, T, T)[kind]
                        for h in range(H):
                            last = mm(banks(4, 2)[:, h * n:(h + 1) * n],
                                      qT[:, h, t * P:(t + 1) * P], kcT if kind == 0 else kT[:, 1 + kind, :], start=True, stop=True)
                        last.then_inc(sem("scores"), up("scores"))
                        softmax_T(n)
                        PT = U(1)
                        for h in range(H):
                            o = ps[HD * (h % 2):HD * (h % 2 + 1), 3, (h // 2) * T + t * P:(h // 2) * T + (t + 1) * P]
                            if kind == 0:
                                last = mm(o, vc, PT[0:NCMP, h * P:(h + 1) * P], start=False, stop=False, skip_group_check=True)
                            else:
                                for s2 in range(NT):
                                    last = mm(o, vr[:, s2, (kind - 1) * HD:kind * HD], PT[:, (2 * h + s2) * P:(2 * h + s2 + 1) * P],
                                              start=False, stop=(kind == 2 and t == 1 and s2 == 1), skip_group_check=True)
                        last.then_inc(sem("attn_out"), up("attn_out"))

            def retention():
                n = 512
                s = ringA.take(pe)
                for t in range(NT):
                    group([rowsof(s, n, 0, n, t)], ringA if t == NT - 1 else None)
                s = ringA.take(pe)
                for t in range(NT):
                    group([rowsof(s, n, 0, n, t)], ringA if t == NT - 1 else None)
                rot = U(8).rearrange("p (t c) -> p t c", t=NT)
                qkT = U(9, 2, parts=HD).rearrange("p (h t) -> p h t", h=8)
                att = U(11, 2).rearrange("p (h n t) -> p h n t", h=H, n=NT)
                vg = U(7).rearrange("p (t c) -> p t c", t=NT)
                for t in range(NT):
                    pe.wait_ge(sem("ret_rotated"), due("pe", "ret_rotated"))
                    for h in range(8):
                        last = tr(banks(4 + 2 * t, 2, HD)[:, h * P:(h + 1) * P], rot[:, t, h * HD:(h + 1) * HD], P)
                    last.then_inc(sem("ret_T_psum"), up("ret_T_psum"))
                pe.wait_ge(sem("ret_T"), due("pe", "ret_T", 2))
                for h in range(H):
                    for s2 in range(NT):
                        last = mm(ps[:, 4 + h, s2 * T:(s2 + 1) * T], qkT[:, 4 + h, s2 * P:(s2 + 1) * P], qkT[:, h, :], start=True, stop=True)
                    last.then_inc(sem("ret_scores"), up("ret_scores"))
                pe.wait_ge(sem("ret_att"), due("pe", "ret_att", 4))
                for t in range(NT):
                    for h in range(H):
                        for s2 in range(t + 1):
                            last = mm(ps[:, 4, t * MW + h * HD:t * MW + (h + 1) * HD], att[:, h, s2, t * P:(t + 1) * P],
                                      vg[:, s2, h * HD:(h + 1) * HD], start=(s2 == 0), stop=(s2 == t))
                last.then_inc(sem("ret_out_psum"), up("ret_out_psum"))
                orow = U(13, size=512).rearrange("p (t c) -> p t c", t=NT)
                pe.wait_ge(sem("ret_out_rows"), due("pe", "ret_out_rows"))
                for t in range(NT):
                    for k in range(2):
                        last = tr(ps[:, 5, k * T + t * P:k * T + (t + 1) * P], orow[:, t, k * P:(k + 1) * P], P)
                last.then_inc(sem("ret_outT"), up("ret_outT"))

            def conv():
                s = ringA.take(pe)
                for i in range(2):
                    group([chT(s, 512, 256 * i + P * j, P, T * j) for j in range(2)], ringA if i == 1 else None)
                s = ringA.take(pe)
                group([chT(s, 256, P * j, P, T * j) for j in range(2)], ringA)

            def rwkv(l):
                s = ringA.take(pe)
                for i in range(4):
                    group([chT(s, 512, P * i, P)], ringA if i == 3 else None)
                s = ringA.take(pe)
                n = CONV0 - RWKV0 - 512
                for i in range(3):
                    group([chT(s, n, P * i, P)], ringA if i == 2 else None)
                lora = U(7, off=0)
                open_sides()
                side_units(4)
                pe.wait_ge(sem("rwkv_lora"), due("pe", "rwkv_lora"))
                tw, al, sg = lora[0:32, 0:256], lora[0:32, 256:512], lora[0:HD, 512:768]
                for w, src, b in ((w2s, tw, 4), (a2s, al, 6)):
                    for h in range(H):
                        last = mm(banks(b, 2, HD)[:, h * T:(h + 1) * T], w[:, l, h * HD:(h + 1) * HD], src, start=True, stop=True)
                last.then_inc(sem("rwkv_lora_psum"), up("rwkv_lora_psum"))
                side_units(1)
                pe.wait_ge(sem("rwkv_kk_sq"), due("pe", "rwkv_kk_sq"))
                pe.wait_ge(sem("rwkv_sigmoids"), due("pe", "rwkv_sigmoids"))
                for i in range(2):
                    last = mm(ps[0:HD, 4 + i, :], ones[0:HD, :], U(11, parts=HD)[:, 512 * i:512 * (i + 1)], start=True, stop=True)
                last.then_inc(sem("rwkv_kk_norm"), up("rwkv_kk_norm"))
                B, K, V, AR, rk = U(0, parts=HD), U(2, parts=HD), U(6, parts=HD), U(13, 2, parts=HD), U(12, parts=HD)
                AR = AR.rearrange("p (g c) -> p g c", g=HC)
                Bt, Kt, Vt = (U(i, parts=HD).rearrange("p (g c) -> p g c", g=HC) for i in (1, 3, 4))
                gB, gK = (U(i, 2, parts=HD).rearrange("p (g c) -> p g c", g=HC) for i in (8, 10))
                side_units(5)
                pe.wait_ge(sem("rwkv_operands"), due("pe", "rwkv_operands"))

                def ch(m, g):
                    return m[:, g * CH:(g + 1) * CH]
                for src, b in ((B, 4), (K, 6)):
                    for g in range(HC):
                        last = tr(ch(banks(b, 2, HD), g), ch(src, g), HD)
                    last.then_inc(sem("rwkv_rows_psum"), up("rwkv_rows_psum"))
                pe.wait_ge(sem("rwkv_rows"), due("pe", "rwkv_rows"))
                for g in range(HC):
                    last = tr(ch(banks(4, 2, HD), g), ch(V, g), HD)
                last.then_inc(sem("rwkv_rows_psum"), up("rwkv_rows_psum"))
                pe.wait_ge(sem("rwkv_rows"), due("pe", "rwkv_rows"))
                for g in range(HC):
                    mm(ps[0:HD, 6, g:g + 1], ch(rk, g), ones[0:HD, 0:1], start=True, stop=True)
                pe.wait_ge(sem("rwkv_rows"), due("pe", "rwkv_rows"))
                for c in range(NC):
                    last = mm(banks(4, 2, HD)[:, c * MW:(c + 1) * MW], sg[:, c * CH:(c + 1) * CH], g2s[:, l, :], start=True, stop=True)
                last.then_inc(sem("rwkv_gate_psum"), up("rwkv_gate_psum"))
                pe.wait_ge(sem("rwkv_gate_rows"), due("pe", "rwkv_gate_rows"))
                for lhs in (B, K):
                    for g in range(HC):
                        last = mm(banks(4, 4, HD)[:, g * 128:(g + 1) * 128], ch(lhs, g), AR[:, g, :], start=True, stop=True)
                    last.then_inc(sem("rwkv_gram_psum"), up("rwkv_gram_psum"))
                    side_units(1)
                    pe.wait_ge(sem("rwkv_gram"), due("pe", "rwkv_gram"))
                for g in range(HC):
                    last = mm(ch(banks(4, 2, HD), g), AR[:, g, 0:CH], ch(B, g), start=True, stop=True)
                last.then_inc(sem("rwkv_gram_psum"), up("rwkv_gram_psum"))
                X, XT, M, Y = U(15, parts=HD), U(6, parts=HD), U(12, parts=HD), U(7, parts=HD)
                for n, b in enumerate(LEVELS):
                    side_units(1)
                    pe.wait_ge(sem("rwkv_inv_M"), due("pe", "rwkv_inv_M"))
                    for g in range(HC):
                        last = mm(ch(banks(4, 2, HD), g), ch(M, g), ch(X, g), start=True, stop=True)
                    last.then_inc(sem("rwkv_inv_Y_psum"), up("rwkv_inv_Y_psum"))
                    pe.wait_ge(sem("rwkv_inv_Y"), due("pe", "rwkv_inv_Y"))
                    for g in range(HC):
                        last = mm(ch(banks(6, 2, HD), g), ch(XT, g), ch(Y, g), start=True, stop=True)
                    for g in range(HC):
                        last = mm(ch(banks(4, 2, HD), g), ch(Y, g), ch(XT, g), start=True, stop=True)
                    last.then_inc(sem("rwkv_inv_X_psum"), up("rwkv_inv_X_psum"))
                S = U(15, off=512, size=256, parts=HD)
                Wsb, SA = U(15, off=0, size=256, parts=HD), U(15, off=256, size=256, parts=HD)
                for c in range(NC):
                    if c < 3:
                        side_units(1)
                    pe.wait_ge(sem("rwkv_state"), due("pe", "rwkv_state"))
                    for h in range(H):
                        g, hs = h * NC + c, slice(h * HD, (h + 1) * HD)
                        mm(ps[0:HD, 4, hs], AR[:, g, 0:CH], S[:, hs], start=True, stop=False)
                        last = mm(ps[0:HD, 4, hs], gK[:, g, 0:CH], Vt[:, g, :], start=False, stop=True)
                    last.then_inc(sem("rwkv_W_psum"), up("rwkv_W_psum"))
                    pe.wait_ge(sem("rwkv_W"), due("pe", "rwkv_W"))
                    for h in range(H):
                        g, hs = h * NC + c, slice(h * HD, (h + 1) * HD)
                        last = mm(ps[0:HD, 5, hs], ch(XT, g), Wsb[:, hs], start=True, stop=True)
                    last.then_inc(sem("rwkv_SA_psum"), up("rwkv_SA_psum"))
                    pe.wait_ge(sem("rwkv_SA"), due("pe", "rwkv_SA"))
                    for h in range(H):
                        g, hs = h * NC + c, slice(h * HD, (h + 1) * HD)
                        mm(ps[0:HD, 7, hs], Bt[:, g, :], SA[:, hs], start=True, stop=False)
                        mm(ps[0:HD, 7, hs], Kt[:, g, :], Vt[:, g, :], start=False, stop=True)
                        mm(ps[0:HD, 6, hs], AR[:, g, CH:], S[:, hs], start=True, stop=False)
                        mm(ps[0:HD, 6, hs], gB[:, g, CH:], SA[:, hs], start=False, stop=False)
                        last = mm(ps[0:HD, 6, hs], gK[:, g, CH:], Vt[:, g, :], start=False, stop=True)
                    last.then_inc(sem("rwkv_Y_psum"), up("rwkv_Y_psum"))
                y = U(0, parts=HD).rearrange("p (c n) -> p c n", c=NC)
                side_units(4)
                pe.wait_ge(sem("rwkv_out_rows"), due("pe", "rwkv_out_rows"))
                for c in range(NC):
                    for k in range(2):
                        last = tr(ps[:, 4, k * T + c * CH:k * T + (c + 1) * CH], y[:, c, k * P:(k + 1) * P], HD)
                last.then_inc(sem("rwkv_outT"), up("rwkv_outT"))

            def rows_out(src, name="rows_psum"):
                for half in range(2):
                    s = kview(ringA.take(pe), 512)
                    for t in range(NT):
                        for k in range(KD):
                            last = mm(ps[:, 4 + 2 * t + half, :], src[:, k, t * P:(t + 1) * P], s[:, k, :], start=(k == 0), stop=(k == KD - 1))
                    last.then_inc(sem("slabA_used"), up("slabA_used"))
                add_zero(ps[0:32, 7, 0:1]).then_inc(sem(name), up(name))

            def open_sides():
                pe.wait_ge(sem("proj_free"), due("pe", "proj_free", proj["held"]))
                proj["held"] = 0
                side.update(unit=0)

            def side_units(n):
                for u in range(side["unit"], side["unit"] + n):
                    m, c, b = SIDE[u // KD], u % KD, u % PROJ
                    if c == 0:
                        ended = ("nsa_done", "ret_done", "rwkv_done", "conv_done")[m]
                        pe.wait_ge(sem(ended), due("pe", ended))
                    if c % 4 == 0:
                        side["gates"] = kview(ringA.take(pe), 512)
                    if c == 0:
                        side["branch"] = ringB.take(pe).rearrange("p (k n) -> p k n", k=2)
                    if u >= PROJ:
                        pe.wait_ge(sem("side_gate"), due("pe", "side_gate"))
                    for k in range(KD):
                        last = mm(ps[:, b, 0:T], side["gates"][:, k, c % 4 * P:(c % 4 + 1) * P], hT[:, k, :], start=(k == 0), stop=(k == KD - 1))
                    if c % 4 == 3:
                        last.then_inc(sem("slabA_used"), up("slabA_used"))
                    for k in range(2):
                        last = mm(ps[:, b, T:2 * T], side["branch"][:, k, c * P:(c + 1) * P], oT[:, m, k, :], start=(k == 0), stop=(k == 1))
                    if c < KD - 1:
                        last.then_inc(sem("side_psum"), up("side_psum"))
                    else:
                        last.then_inc(sem("slabB_used"), up("slabB_used"))
                        add_zero(ps[0:32, b, T:T + 1]).then_inc(sem("side_psum"), up("side_psum"))
                side["unit"] += n

            def merge():
                side_units(4 * KD - side["unit"])
                pe.wait_ge(sem("side_gate"), due("pe", "side_gate", PROJ))
                pe.wait_ge(sem("side_summed"), due("pe", "side_summed", 4 * KD))
                rows_out(merged)

            def cross():
                xq, xk = (U(2 + 2 * i, 2).rearrange("p (c t) -> p c t", c=KD) for i in range(2))
                xv, xo = U(6, 2).rearrange("p (n c) -> p n c", n=NT), U(8, 2).rearrange("p (c t) -> p c t", c=KD)
                take_hT()
                for half in range(2):
                    s = ringA.take(pe)
                    for i in range(2):
                        group([chT(s, 512, 256 * i + P * j, P, T * j) for j in range(2)], ringA if i == 1 else None)
                pe.wait_ge(sem("mem_ready"), due("pe", "mem_ready"))
                for half in range(2):
                    s = ringA.take(pe)
                    v = kview(s, 512)
                    for i in range(2):
                        group([((lambda k, c0=256 * i + P * j: v[:, k, c0:c0 + P]), (lambda k: merged[:, k, :]), P, T * j, T) for j in range(2)], ringA if i == 1 else None)
                for half in range(2):
                    s = ringA.take(pe)
                    for t in range(NT):
                        group([rowsof(s, 512, 0, 512, t, src=merged)], ringA if t == NT - 1 else None)
                pe.wait_ge(sem("cross_kv"), due("pe", "cross_kv"))
                for t in range(NT):
                    for h in range(4):
                        for c in range(2):
                            last = mm(banks(4, 2)[:, h * T:(h + 1) * T], xq[:, 2 * h + c, t * P:(t + 1) * P], xk[:, 2 * h + c, :], start=(c == 0), stop=(c == 1))
                    last.then_inc(sem("scores"), up("scores"))
                    softmax_T(T)
                    PT = U(1)
                    for c in range(KD):
                        for s2 in range(NT):
                            last = mm(banks(4, 2)[:, c * P:(c + 1) * P], xv[:, s2, c * P:(c + 1) * P], PT[:, (c // 2 * 2 + s2) * P:(c // 2 * 2 + s2 + 1) * P],
                                      start=(s2 == 0), stop=(s2 == 1))
                    last.then_inc(sem("cross_out_psum"), up("cross_out_psum"))
                    pe.wait_ge(sem("cross_out"), due("pe", "cross_out"))
                rows_out(xo)

            def ffn(steps, gated):
                def up_part(i):
                    s = ringA.take(pe, 2 if gated else 1)
                    for j in range(2):
                        for w in range(2 if gated else 1):
                            v = s[:, 2048 * w:2048 * (w + 1)].rearrange("p (k n) -> p k n", k=KD)
                            for k in range(KD):
                                last = mm(ps[:, 2 * (i % 2) + j, w * T:(w + 1) * T], v[:, k, j * P:(j + 1) * P], hT[:, k, :], start=(k == 0), stop=(k == KD - 1))
                        last.then_inc(sem("hidden_psum"), up("hidden_psum"))

                def down_part(i):
                    w2 = ringB.take(pe).rearrange("p (j n) -> p j n", j=2)
                    he = U(i % 2, size=512).rearrange("p (j t) -> p j t", j=2)
                    pe.wait_ge(sem("hidden_ready"), due("pe", "hidden_ready", 2))
                    for j in range(2):
                        for t in range(NT):
                            for half in range(2):
                                last = mm(ps[:, 4 + 2 * t + half, :], he[:, j, t * P:(t + 1) * P], w2[:, j, half * 512:(half + 1) * 512],
                                          start=False, stop=False, skip_group_check=True)
                    last.then_inc(sem("slabB_used"), up("slabB_used"))
                for i in range(steps):
                    up_part(i)
                    if i:
                        down_part(i - 1)
                    add_zero(ps[0:32, 4, 0:1]).then_inc(sem("slabA_used"), up("slabA_used"))
                down_part(steps - 1)

            def seed():
                for b in range(4, 8):
                    mm(ps[:, b, :], zeros[0:1, :], cst[0:1, C_SEL:C_SEL + 512], start=True, stop=False, skip_group_check=True)

            def close(name):
                for b in range(4, 8):
                    last = mm(ps[0:32, b, 0:1], zeros[0:1, 0:32], zeros[0:1, 0:1], start=False, stop=True, skip_group_check=True)
                last.then_inc(sem(name), up(name))

            pe.wait_ge(sem("consts_loaded"), due("pe", "consts_loaded", 32))
            pe.wait_ge(sem("bias_operands"), due("pe", "bias_operands"))
            for h in range(H):
                last = mm(ps[:, h, :], relb[:, h:h + 1].broadcast_to([NBUCKET + 1, P]), U(0, size=SPAN, parts=NBUCKET + 1), start=True, stop=True)
            last.then_inc(sem("bias_psum"), up("bias_psum"))
            pe.wait_ge(sem("bias_rows"), due("pe", "bias_rows"))
            memrows = U(4, 2).rearrange("p (n d) -> p n d", n=NT)
            hrows = U(14, 2).rearrange("p (n d) -> p n d", n=NT)
            norm_T(memrows)
            for l in range(DEPTH):
                norm_T(hrows)
                nsa()
                retention()
                conv()
                rwkv(l)
                merge()
                norm_T(hrows)
                cross()
                norm_T(hrows)
                take_hT()
                seed()
                ffn(FF1 // STEP, False)
                close("rows_psum")
            norm_T(hrows)

            take_hT()
            for i in range(2):
                s = ringA.take(pe)
                for half in range(2):
                    group([chT(s, 512, 256 * half + P * j, P, T * j) for j in range(2)], ringA if half == 1 else None)
            for i in range(2):
                s = ringA.take(pe)
                for j in range(4):
                    group([chT(s, 512, P * j, P)], ringA if j == 3 else None)
            s = ringA.take(pe)
            for t in range(NT):
                group([rowsof(s, 512, 0, 512, t)], ringA if t == NT - 1 else None)
            s = ringA.take(pe)
            group([chT(s, 8, 0, 8)], ringA)
            gd = fbT[:, 0:1024].rearrange("p (w c n) -> p w c n", w=2, c=4)
            xc = U(13).rearrange("p (c t) -> p c t", c=4)
            pe.wait_ge(sem("lru_conv"), due("pe", "lru_conv"))
            pe.wait_ge(sem("lru_gate_loaded"), due("pe", "lru_gate_loaded", 64))
            for w in range(2):
                for c in range(4):
                    last = mm(banks(4 + 2 * w, 2)[:, c * T:(c + 1) * T], gd[:, w, c, :], xc[:, c, :], start=True, stop=True)
            last.then_inc(sem("lru_gate_psum"), up("lru_gate_psum"))
            fq, fk = (fbT[0:HD, 2048 * i:2048 * (i + 1)].rearrange("p (h t) -> p h t", h=8) for i in (1, 2))
            fv = fbT[:, 6144:7168].rearrange("p (n c) -> p n c", n=NT)
            cum, ncum = U(2, off=512, size=256, parts=8), U(2, off=768, size=256, parts=8)
            pe.wait_ge(sem("fox_cum"), due("pe", "fox_cum"))
            pe.wait_ge(sem("lru_done"), due("pe", "lru_done"))
            for t in range(NT):
                for hg in range(2):
                    for i in range(4):
                        h = 4 * hg + i
                        o = banks(4, 2)[:, i * T:(i + 1) * T]
                        mm(o, fq[:, h, t * P:(t + 1) * P], fk[:, h, :], start=True, stop=False)
                        mm(o, sel[:, h, :], ncum, start=False, stop=False)
                        last = mm(o, cum[:, t * P:(t + 1) * P], cst[0:8, C_SEL + 128 * h:C_SEL + 128 * (h + 1)].unsqueeze(1).broadcast_to([8, 2, P]), start=False, stop=True)
                    last.then_inc(sem("scores"), up("scores"))
                    softmax_T(T)
                    PT = U(1)
                    if hg == 0 and t:
                        pe.wait_ge(sem("fox_out"), due("pe", "fox_out"))
                    for i in range(4):
                        h = 4 * hg + i
                        for s2 in range(NT):
                            last = mm(ps[HD * (h % 2):HD * (h % 2 + 1), 3, (h // 2) * P:(h // 2 + 1) * P], fv[:, s2, h * HD:(h + 1) * HD],
                                      PT[:, (2 * i + s2) * P:(2 * i + s2 + 1) * P], start=(s2 == 0), stop=(s2 == 1))
                    if hg:
                        last.then_inc(sem("fox_out_psum"), up("fox_out_psum"))
            pe.wait_ge(sem("fox_out"), due("pe", "fox_out"))
            rows_out(merged, "sum_psum")
            norm_T(hrows)
            take_hT()
            seed()
            ffn(FF2 // STEP, True)
            close("sum_psum")

            norm_T(hrows)
            take_hT()
            for i in range(2):
                s = ringA.take(pe)
                for half in range(2):
                    group([chT(s, 512, 256 * half + P * j, P, T * j) for j in range(2)], ringA if half == 1 else None)
            for i in range(4):
                s = ringA.take(pe)
                for t in range(NT):
                    group([rowsof(s, 512, 0, 512, t)], ringA if t == NT - 1 else None)
            s = ringA.take(pe)
            group([chT(s, 16, 0, 16)], ringA)
            lrT = U(15, off=0, size=256, parts=16)
            pe.wait_ge(sem("gla_lr"), due("pe", "gla_lr"))
            for h in range(H):
                last = mm(banks(4, 2)[:, h * T:(h + 1) * T], gw2[:, h * P:(h + 1) * P], lrT, start=True, stop=True)
            last.then_inc(sem("gla_gate_psum"), up("gla_gate_psum"))
            qd, ki, ks = (U(i).rearrange("p (g c) -> p g c", g=HC) for i in (8, 9, 10))
            ksr = U(11, 2, parts=CH).rearrange("p (g c) -> p g c", g=HC)
            sc = U(13, parts=CH).rearrange("p (g c) -> p g c", g=HC)
            vrow = U(0, 4, parts=CH).rearrange("p (c n) -> p c n", c=NC)
            state = U(14).rearrange("p (h e) -> p h e", h=H)
            pe.wait_ge(sem("gla_operands"), due("pe", "gla_operands"))
            for g in range(HC):
                last = tr(banks(4, 4, CH)[:, g * P:(g + 1) * P], ks[:, g, :], P)
            last.then_inc(sem("gla_rows_psum"), up("gla_rows_psum"))
            pe.wait_ge(sem("gla_rows"), due("pe", "gla_rows"))
            for g in range(HC):
                last = mm(banks(4, 2, CH)[:, g * CH:(g + 1) * CH], ki[:, g, :], qd[:, g, :], start=True, stop=True)
            last.then_inc(sem("gla_scores_psum"), up("gla_scores_psum"))
            pe.wait_ge(sem("gla_scores"), due("pe", "gla_scores"))
            for c in range(NC):
                pe.wait_ge(sem("gla_state"), due("pe", "gla_state"))
                for h in range(H):
                    g = h * NC + c
                    o = banks(4, 2, CH)[:, h * T:(h + 1) * T]
                    mm(o, sc[:, g, :], vrow[:, c, h * T:(h + 1) * T], start=True, stop=False)
                    mm(o, qd[:, g, :], state[:, h, :], start=False, stop=True)
                    last = mm(banks(6, 2)[:, h * T:(h + 1) * T], ksr[:, g, :], vrow[:, c, h * T:(h + 1) * T], start=True, stop=True)
                last.then_inc(sem("gla_out_psum"), up("gla_out_psum"))
            orow = fbT[0:CH, 4096:8192].rearrange("p (c n) -> p c n", c=NC)
            pe.wait_ge(sem("gla_out_rows"), due("pe", "gla_out_rows"))
            for k in range(KD):
                for c in range(NC):
                    last = tr(banks(4, 4)[:, k * T + c * CH:k * T + (c + 1) * CH], orow[:, c, k * P:(k + 1) * P], CH)
            last.then_inc(sem("gla_outT_psum"), up("gla_outT_psum"))
            pe.wait_ge(sem("gla_outT"), due("pe", "gla_outT"))
            rows_out(merged, "sum_psum")
            norm_T(hrows)
            take_hT()
            for t in range(NT):
                for k in range(KD):
                    last = mm(ps[:, 0, t * NEXP:(t + 1) * NEXP], hT[:, k, t * P:(t + 1) * P], routw[:, k, :], start=(k == 0), stop=(k == KD - 1))
            last.then_inc(sem("router_psum"), up("router_psum"))
            gates = U(4, size=2 * NEXP).rearrange("p (t e) -> p t e", t=NT)
            pe.wait_ge(sem("router_gates"), due("pe", "router_gates"))
            before, all_ = cst[:, C_BEFORE:C_BEFORE + P], cst[:, C_ONES:C_ONES + P]
            pe.wait_ge(sem("chosen"), due("pe", "chosen"))
            mm(ps[:, 2, 0:8], before, chosen[:, 0, :], start=True, stop=True)
            mm(ps[:, 2, 8:16], before, chosen[:, 1, :], start=True, stop=False)
            mm(ps[:, 2, 8:16], all_, chosen[:, 0, :], start=False, stop=True)
            mm(ps[:, 2, 16:24], all_, chosen[:, 0, :], start=True, stop=False)
            mm(ps[:, 2, 16:24], all_, chosen[:, 1, :], start=False, stop=True).then_inc(sem("slots_psum"), up("slots_psum"))
            seed()

            def slot_ffn(steps):
                def up_part(i):
                    s = ringA.take(pe, 2)
                    for j in range(2):
                        for w in range(2):
                            v = s[:, 2048 * w:2048 * (w + 1)].rearrange("p (k n) -> p k n", k=KD)
                            for k in range(KD):
                                last = mm(ps[:, i % 2, (2 * w + j) * P:(2 * w + j + 1) * P], v[:, k, j * P:(j + 1) * P], slot_x[:, k, :],
                                          start=(k == 0), stop=(k == KD - 1))
                    last.then_inc(sem("slot_hidden_psum"), up("slot_hidden_psum"))

                def down_part(i):
                    w2 = ringB.take(pe).rearrange("p (j n) -> p j n", j=2)
                    he = U(i % 2, size=2 * SLOTS).rearrange("p (j c) -> p j c", j=2)
                    pe.wait_ge(sem("slot_hidden_ready"), due("pe", "slot_hidden_ready"))
                    for j in range(2):
                        for half in range(2):
                            last = mm(ps[:, 2 + half, :], he[:, j, :], w2[:, j, half * 512:(half + 1) * 512],
                                      start=(i == 0 and j == 0), stop=(i == steps - 1 and j == 1))
                    last.then_inc(sem("slabB_used"), up("slabB_used"))
                for i in range(steps):
                    up_part(i)
                    if i:
                        down_part(i - 1)
                    add_zero(ps[0:32, 4, 0:1]).then_inc(sem("slabA_used"), up("slabA_used"))
                down_part(steps - 1)
                add_zero(ps[0:32, 2, 0:1]).then_inc(sem("slot_y_psum"), up("slot_y_psum"))

            pe.wait_ge(sem("most_known"), due("pe", "most_known"))
            fullest = pe.value_load(most_int, min_val=0, max_val=T)
            before_branch, slabs_before = counts_now(), (ringA.taken, ringB.taken)
            with pe.If(fullest <= SLOTS):
                pe.wait_ge(sem("picks"), due("pe", "picks"))
                for e in range(NEXP):
                    for t in range(NT):
                        c = e * T + t * P
                        last = tr(ps[:, c // 512, c % 512:c % 512 + P], pick_gate[:, e, t, :], P)
                last.then_inc(sem("spread_psum"), up("spread_psum"))
                pe.wait_ge(sem("spread_ready"), due("pe", "spread_ready"))
                with pe.Fori(0, NEXP) as e:
                    enter(e)
                    for k in range(KD):
                        for t in range(NT):
                            last = mm(ps[:, k // 4, k % 4 * SLOTS:(k % 4 + 1) * SLOTS], hrows[:, t, k::KD],
                                      fbT[:, bass.ds(e * (NT * SLOTS) + t * SLOTS, SLOTS)], start=(t == 0), stop=(t == NT - 1))
                    last.then_inc(sem("slot_x_psum"), up("slot_x_psum"))
                    pe.wait_ge(sem("slot_x"), due("pe", "slot_x"))
                    slot_ffn(FFE // STEP)
                    pe.wait_ge(sem("slot_y"), due("pe", "slot_y"))
                    for t in range(NT):
                        for half in range(2):
                            mm(ps[:, 4 + 2 * t + half, :], spread_e[:, t * P:(t + 1) * P], slot_y[:, half * 512:(half + 1) * 512],
                               start=False, stop=False, skip_group_check=True)
                    leave(NEXP)
            go_back(before_branch)
            ringA.taken, ringB.taken = slabs_before
            with pe.Else():
                for t in range(NT):
                    last = tr(ps[0:NEXP, 1, t * P:(t + 1) * P], gates[:, t, :], P)
                last.then_inc(sem("router_T_psum"), up("router_T_psum"))
                gatesT = U(4, off=64, size=T, parts=NEXP)
                pe.wait_ge(sem("router_T"), due("pe", "router_T"))
                for e in range(NEXP):
                    last = mm(ps[:, e // 2, (e % 2) * T:(e % 2 + 1) * T], sel[:, e, :], gatesT, start=True, stop=True)
                last.then_inc(sem("router_rows_psum"), up("router_rows_psum"))
                pe.wait_ge(sem("router_rows"), due("pe", "router_rows"))
                with pe.Fori(0, NEXP) as e:
                    enter(e)
                    ffn(FFE // STEP, True)
                    leave(NEXP)
            close("sum_psum")

        @block.scalar
        def _(act):
            def A(o, i, f=ACT.Copy, **kw):
                nc.scalar.activation(o, i, f, **kw).then_inc(sem("act_order"), up("act_order"))
                act.wait_ge(sem("act_order"), at("act_order"))

            def take():
                act.wait_ge(sem("proj_ready"), due("act", "proj_ready"))
                b = proj["act"] % PROJ
                proj["act"] += 1
                return ps[:, b, :]

            def side_gates(n):
                for u in range(gated["act"], gated["act"] + n):
                    act.wait_ge(sem("side_psum"), due("act", "side_psum"))
                    if u >= 2:
                        act.wait_ge(sem("side_summed"), due("act", "side_summed"))
                    half = gainrow[:, u % 2 * 512:(u % 2 + 1) * 512]
                    A(half[:, 0:T], ps[:, u % PROJ, 0:T], ACT.Sigmoid)
                    nc.scalar.activation(half[:, T:2 * T], ps[:, u % PROJ, T:2 * T], ACT.Copy).then_inc(sem("side_gate"), up("side_gate"))
                    act.wait_ge(sem("side_gate"), at("side_gate"))
                gated["act"] += n
                if gated["act"] == 4 * KD:
                    act.wait_ge(sem("side_summed"), due("act", "side_summed", 2))
                    gated["act"] = 0

            gated = {"act": 0}

            def softmax(n, heads=4):
                act.wait_ge(sem("exp_in"), due("act", "exp_in"))
                nc.scalar.activation(U(0)[:, 0:heads * n], U(0)[:, 0:heads * n], ACT.Exp).then_inc(sem("exp_out"), up("exp_out"))
                act.wait_ge(sem("exp_out"), at("exp_out"))

            def two_heads(dst, h, p, scale=1.0, done=True):
                A(dst[:, h, :], p[0:HD, 0:T], scale=scale)
                nc.scalar.activation(dst[:, h + 1, :], p[HD:P, 0:T], ACT.Copy, scale=scale).then_inc(sem("proj_free"), up("proj_free"))
                act.wait_ge(sem("proj_free"), at("proj_free"))

            def square_rows():
                act.wait_ge(sem("rows_psum"), due("act", "rows_psum"))
                for t in range(NT):
                    A(U(12), banks(4 + 2 * t, 2), ACT.Square, accum_out=stat[:, 8 + t:9 + t])
                    nc.scalar.activation(stat[:, 8 + t:9 + t], stat[:, 8 + t:9 + t], ACT.Sqrt, scale=1.0 / D, bias=eps).then_inc(sem("rows_square"), up("rows_square"))
                    act.wait_ge(sem("rows_square"), at("rows_square"))

            def norm(src=None, col=0):
                for t in range(NT):
                    if src is None:
                        act.wait_ge(sem("norm_in"), due("act", "norm_in"))
                    rows = (x if src is None else src)[:, t, :]
                    m = stat[:, col + t:col + t + 1]
                    A(U(12), rows, ACT.Square, accum_out=m)
                    nc.scalar.activation(m, m, ACT.Sqrt, scale=1.0 / D, bias=eps).then_inc(sem("norm_root"), up("norm_root"))
                    act.wait_ge(sem("norm_root"), at("norm_root"))

            def root(o):
                act.wait_ge(sem("root_in"), due("act", "root_in"))
                nc.scalar.activation(o, o, ACT.Sqrt).then_inc(sem("root_out"), up("root_out"))
                act.wait_ge(sem("root_out"), at("root_out"))

            def ffn(steps, gated):
                for i in range(steps):
                    for j in range(2):
                        act.wait_ge(sem("hidden_psum"), due("act", "hidden_psum"))
                        b = 2 * (i % 2) + j
                        nc.scalar.activation(U(2 + b, size=T), ps[:, b, 0:T], ACT.Silu if gated else ACT.Relu).then_inc(sem("hidden_act"), up("hidden_act"))
                        act.wait_ge(sem("hidden_act"), at("hidden_act"))

            act.wait_ge(sem("params_loaded"), count_of("params_loaded").posted)
            act.wait_ge(sem("consts_loaded"), due("act", "consts_loaded", 32))
            eps = cst[:, C_EPS:C_EPS + 1]
            norm(merged[:, :, :].rearrange("p k t -> p (k t)").rearrange("p (n d) -> p n d", n=NT), 4)
            act.wait_ge(sem("x_loaded"), due("act", "x_loaded", 16))
            for l in range(DEPTH):
                norm(x if l == 0 else None)
                qT = U(2, parts=HD).rearrange("p (h t) -> p h t", h=H)
                kT = U(3, parts=HD).rearrange("p (h t) -> p h t", h=H)
                vr = U(4, size=256).rearrange("p (t c) -> p t c", t=NT)
                for i in range(2):
                    two_heads(qT, 2 * i, take())
                two_heads(kT, 0, take())
                nc.scalar.activation(kT[:, 2, :], take()[0:HD, 0:T], ACT.Copy).then_inc(sem("proj_free"), up("proj_free"))
                act.wait_ge(sem("proj_free"), at("proj_free"))
                nc.scalar.activation(vr[:, :, 0:HD], take()[:, 0:2 * HD].rearrange("p (t c) -> p t c", t=NT), ACT.Copy).then_inc(sem("proj_free"), up("proj_free"))
                act.wait_ge(sem("proj_free"), at("proj_free"))
                nc.scalar.activation(kT[:, 3, :], take()[0:HD, 0:T], ACT.Copy).then_inc(sem("proj_free"), up("proj_free"))
                act.wait_ge(sem("proj_free"), at("proj_free"))
                p = take()[:, 0:2 * P].rearrange("p (t c) -> p t c", t=NT)
                A(vr[:, :, HD:P], p[:, :, 0:HD])
                nc.scalar.activation(U(4, off=512, size=24).rearrange("p (t c) -> p t c", t=NT), p[:, :, HD:HD + 12], ACT.Sigmoid).then_inc(sem("proj_free"), up("proj_free"))
                act.wait_ge(sem("proj_free"), at("proj_free"))
                nc.scalar.activation(stat[:, 60:61], stat[:, 60:61], ACT.Copy).then_inc(sem("nsa_inputs"), up("nsa_inputs"))
                act.wait_ge(sem("nsa_inputs"), at("nsa_inputs"))
                for t in range(NT):
                    for n in (NCMP, T, T):
                        softmax(n)
                qk, vg = (U(i).rearrange("p (t c) -> p t c", t=NT) for i in (6, 7))
                for t in range(NT):
                    nc.scalar.activation(qk[:, t, :], take(), ACT.Copy).then_inc(sem("proj_free"), up("proj_free"))
                    act.wait_ge(sem("proj_free"), at("proj_free"))
                for t in range(NT):
                    p = take()
                    A(vg[:, t, 0:MW], p[:, 0:MW])
                    nc.scalar.activation(vg[:, t, MW:2 * MW], p[:, MW:2 * MW], ACT.Silu).then_inc(sem("proj_free"), up("proj_free"))
                    act.wait_ge(sem("proj_free"), at("proj_free"))
                nc.scalar.activation(stat[:, 60:61], stat[:, 60:61], ACT.Copy).then_inc(sem("ret_inputs"), up("ret_inputs"))
                act.wait_ge(sem("ret_inputs"), at("ret_inputs"))
                root(st2[:, 48:48 + NT * H])
                act.wait_ge(sem("ret_done"), due("act", "ret_done"))
                for i in range(3):
                    nc.scalar.activation(U(13 + i // 2, off=512 * (i % 2), size=512), take(), ACT.Copy).then_inc(sem("proj_free"), up("proj_free"))
                    act.wait_ge(sem("proj_free"), at("proj_free"))
                nc.scalar.activation(stat[:, 60:61], stat[:, 60:61], ACT.Copy).then_inc(sem("conv_inputs"), up("conv_inputs"))
                act.wait_ge(sem("conv_inputs"), at("conv_inputs"))
                z = U(0, 4, size=15 * (T + 1), parts=HD).rearrange("p (g t) -> p g t", g=15)
                act.wait_ge(sem("rwkv_z_cleared"), due("act", "rwkv_z_cleared"))
                for i in range(6):
                    p = take()
                    A(z[:, 2 * i, 1:T + 1], p[0:HD, 0:T])
                    nc.scalar.activation(z[:, 2 * i + 1, 1:T + 1], p[HD:P, 0:T], ACT.Copy).then_inc(sem("proj_free"), up("proj_free"))
                    act.wait_ge(sem("proj_free"), at("proj_free"))
                p = take()
                A(z[0:32, 12, 1:T + 1], p[0:32, 0:T])
                A(z[0:32, 13, 1:T + 1], p[32:64, 0:T])
                nc.scalar.activation(z[:, 14, 1:T + 1], p[64:128, 0:T], ACT.Copy).then_inc(sem("proj_free"), up("proj_free"))
                act.wait_ge(sem("proj_free"), at("proj_free"))
                nc.scalar.activation(stat[:, 60:61], stat[:, 60:61], ACT.Copy).then_inc(sem("rwkv_inputs"), up("rwkv_inputs"))
                act.wait_ge(sem("rwkv_inputs"), at("rwkv_inputs"))
                lora = U(7, off=0)
                act.wait_ge(sem("rwkv_mixed"), due("act", "rwkv_mixed"))
                A(lora[0:32, 0:256], lora[0:32, 0:256], ACT.Tanh)
                nc.scalar.activation(lora[0:HD, 512:768], lora[0:HD, 512:768], ACT.Sigmoid).then_inc(sem("rwkv_lora"), up("rwkv_lora"))
                act.wait_ge(sem("rwkv_lora"), at("rwkv_lora"))
                side_gates(4)
                act.wait_ge(sem("rwkv_lora_psum"), due("act", "rwkv_lora_psum"))
                for b, name, dst in ((4, "rwkv_w0", 0), (6, "rwkv_a0", 1)):
                    for h in range(H):
                        done = "rwkv_sigmoids" if dst and h == H - 1 else "act_order"
                        nc.scalar.activation(U(dst, parts=HD)[:, h * T:(h + 1) * T], banks(b, 2, HD)[:, h * T:(h + 1) * T], ACT.Sigmoid, bias=vecs[name][:, l, h:h + 1]).then_inc(sem(done), up(done))
                        act.wait_ge(sem(done), at(done))
                side_gates(1)
                act.wait_ge(sem("rwkv_cumulated"), due("act", "rwkv_cumulated"))
                A(U(8, parts=HD), U(2, parts=HD), ACT.Exp)
                A(U(9, parts=HD), U(2, parts=HD), ACT.Exp, scale=-1.0)
                nc.scalar.activation(U(3, parts=HD), U(3, parts=HD), ACT.Exp).then_inc(sem("rwkv_decays"), up("rwkv_decays"))
                act.wait_ge(sem("rwkv_decays"), at("rwkv_decays"))
                root(U(11, parts=HD))
                side_gates(15)
                root(st2[0:HD, 48:48 + HC])
                side_gates(4)
                side_gates(KD)
                square_rows()
                norm()
                xq, xk = (U(2 + 2 * i, 2).rearrange("p (c t) -> p c t", c=KD) for i in range(2))
                xv, xo = U(6, 2).rearrange("p (n c) -> p n c", n=NT), U(8, 2).rearrange("p (c t) -> p c t", c=KD)
                for dst in (xq, xk):
                    for i in range(4):
                        nc.scalar.activation(dst[:, 2 * i:2 * i + 2, :].rearrange("p c t -> p (c t)"), take(), ACT.Copy).then_inc(sem("proj_free"), up("proj_free"))
                        act.wait_ge(sem("proj_free"), at("proj_free"))
                for half in range(2):
                    for t in range(NT):
                        nc.scalar.activation(xv[:, t, 512 * half:512 * (half + 1)], take(), ACT.Copy).then_inc(sem("proj_free"), up("proj_free"))
                        act.wait_ge(sem("proj_free"), at("proj_free"))
                nc.scalar.activation(stat[:, 60:61], stat[:, 60:61], ACT.Copy).then_inc(sem("cross_kv"), up("cross_kv"))
                act.wait_ge(sem("cross_kv"), at("cross_kv"))
                for t in range(NT):
                    softmax(T)
                    act.wait_ge(sem("cross_out_psum"), due("act", "cross_out_psum"))
                    nc.scalar.activation(xo[:, :, t * P:(t + 1) * P], banks(4, 2).rearrange("p (c t) -> p c t", c=KD), ACT.Copy).then_inc(sem("cross_out"), up("cross_out"))
                    act.wait_ge(sem("cross_out"), at("cross_out"))
                square_rows()
                norm()
                ffn(FF1 // STEP, False)
                square_rows()
            xr = U(8, 2, size=4 * (T + 3)).rearrange("p (c t) -> p c t", c=4)
            yr = U(10).rearrange("p (c t) -> p c t", c=4)
            fq, fk = (fbT[0:HD, 2048 * i:2048 * (i + 1)].rearrange("p (h t) -> p h t", h=8) for i in (1, 2))
            fv = fbT[:, 6144:7168].rearrange("p (n c) -> p n c", n=NT)
            norm()
            act.wait_ge(sem("lru_pad"), due("act", "lru_pad"))
            for i in range(2):
                nc.scalar.activation(xr[:, 2 * i:2 * i + 2, 3:T + 3], take().rearrange("p (c t) -> p c t", c=2), ACT.Copy).then_inc(sem("proj_free"), up("proj_free"))
                act.wait_ge(sem("proj_free"), at("proj_free"))
            for i in range(2):
                nc.scalar.activation(yr[:, 2 * i:2 * i + 2, :].rearrange("p c t -> p (c t)"), take(), ACT.Copy).then_inc(sem("proj_free"), up("proj_free"))
                act.wait_ge(sem("proj_free"), at("proj_free"))
            for i in range(4):
                two_heads(fq, 2 * i, take(), HD ** -0.5)
            for i in range(4):
                two_heads(fk, 2 * i, take())
            for t in range(NT):
                nc.scalar.activation(fv[:, t, :], take(), ACT.Copy).then_inc(sem("proj_free"), up("proj_free"))
                act.wait_ge(sem("proj_free"), at("proj_free"))
            nc.scalar.activation(U(2, off=0, size=256, parts=8), take()[0:8, 0:T], ACT.Identity, bias=fb[:, 0:1]).then_inc(sem("proj_free"), up("proj_free"))
            act.wait_ge(sem("proj_free"), at("proj_free"))
            nc.scalar.activation(stat[:, 60:61], stat[:, 60:61], ACT.Copy).then_inc(sem("even_inputs"), up("even_inputs"))
            act.wait_ge(sem("even_inputs"), at("even_inputs"))
            lam, lru = vec2["ev_lambda_2"], (U(4), U(5))
            A(stat[:, 32:36], lam[:, :], ACT.Abs)
            nc.scalar.activation(stat[:, 36:40], stat[:, 32:36], ACT.Exp, scale=-1.0).then_inc(sem("lru_exp"), up("lru_exp"))
            act.wait_ge(sem("lru_exp"), at("lru_exp"))
            act.wait_ge(sem("fox_exp_in"), due("act", "fox_exp_in"))
            A(U(2, off=768, size=256, parts=8), U(2, off=512, size=256, parts=8), ACT.Exp, scale=-1.0)
            nc.scalar.activation(U(2, off=768, size=256, parts=8), U(2, off=768, size=256, parts=8), ACT.Ln, bias=1.0).then_inc(sem("fox_ln"), up("fox_ln"))
            act.wait_ge(sem("fox_ln"), at("fox_ln"))
            act.wait_ge(sem("lru_gate_psum"), due("act", "lru_gate_psum"))
            for w, n in enumerate(("ev_ga_b_2", "ev_gx_b_2")):
                for c in range(4):
                    done = "lru_sigmoids" if w and c == 3 else "act_order"
                    nc.scalar.activation(lru[w][:, c * T:(c + 1) * T], banks(4 + 2 * w, 2)[:, c * T:(c + 1) * T], ACT.Sigmoid, bias=vec2[n][:, c:c + 1]).then_inc(sem(done), up(done))
                    act.wait_ge(sem(done), at(done))
            act.wait_ge(sem("lru_log_a"), due("act", "lru_log_a"))
            A(U(6), U(4), ACT.Exp, scale=-1.0)
            nc.scalar.activation(U(7), U(4), ACT.Tanh).then_inc(sem("lru_a"), up("lru_a"))
            act.wait_ge(sem("lru_a"), at("lru_a"))
            act.wait_ge(sem("gelu_in"), due("act", "gelu_in"))
            nc.scalar.activation(U(11), U(11), ACT.Tanh).then_inc(sem("gelu_tanh"), up("gelu_tanh"))
            act.wait_ge(sem("gelu_tanh"), at("gelu_tanh"))
            root(U(7))
            for t in range(NT):
                for hg in range(2):
                    softmax(T)
                act.wait_ge(sem("fox_out_psum"), due("act", "fox_out_psum"))
                nc.scalar.activation(merged[:, 4:8, t * P:(t + 1) * P], ps[:, 3, :].rearrange("p (c t) -> p c t", c=4), ACT.Copy).then_inc(sem("fox_out"), up("fox_out"))
                act.wait_ge(sem("fox_out"), at("fox_out"))
            norm()
            ffn(FF2 // STEP, True)
            norm()
            q, k = (U(i).rearrange("p (c t) -> p c t", c=H) for i in (8, 9))
            vrow = U(0, 4, parts=CH).rearrange("p (c n) -> p c n", c=NC)
            grow = fbT[0:CH, 0:4096].rearrange("p (c n) -> p c n", c=NC)
            for dst, sc in ((q, P ** -0.5), (k, 1.0)):
                for i in range(2):
                    nc.scalar.activation(dst[:, 2 * i:2 * i + 2, :].rearrange("p c t -> p (c t)"), take(), ACT.Copy, scale=sc).then_inc(sem("proj_free"), up("proj_free"))
                    act.wait_ge(sem("proj_free"), at("proj_free"))
            for dst, f in ((vrow, ACT.Copy), (grow, ACT.Silu)):
                for half in range(2):
                    for t in range(NT):
                        p = take()
                        A(dst[:, 2 * t, 512 * half:512 * (half + 1)], p[0:CH, :], f)
                        nc.scalar.activation(dst[:, 2 * t + 1, 512 * half:512 * (half + 1)], p[CH:P, :], f).then_inc(sem("proj_free"), up("proj_free"))
                        act.wait_ge(sem("proj_free"), at("proj_free"))
            nc.scalar.activation(U(15, off=0, size=256, parts=16), take()[0:16, 0:T], ACT.Copy).then_inc(sem("proj_free"), up("proj_free"))
            act.wait_ge(sem("proj_free"), at("proj_free"))
            nc.scalar.activation(stat[:, 60:61], stat[:, 60:61], ACT.Copy).then_inc(sem("gla_lr"), up("gla_lr"))
            act.wait_ge(sem("gla_lr"), at("gla_lr"))
            act.wait_ge(sem("gla_exp_in"), due("act", "gla_exp_in"))
            A(U(6), U(5), ACT.Exp, scale=-1.0)
            nc.scalar.activation(U(6), U(6), ACT.Ln, bias=1.0).then_inc(sem("gla_ln"), up("gla_ln"))
            act.wait_ge(sem("gla_ln"), at("gla_ln"))
            act.wait_ge(sem("gla_cum"), due("act", "gla_cum"))
            A(U(5), U(4), ACT.Exp)
            A(U(6), U(4), ACT.Exp, scale=-1.0)
            nc.scalar.activation(U(7), U(7), ACT.Exp).then_inc(sem("gla_exps"), up("gla_exps"))
            act.wait_ge(sem("gla_exps"), at("gla_exps"))
            nc.scalar.activation(st2[:, 0:HC], st2[:, 0:HC], ACT.Exp).then_inc(sem("gla_decay"), up("gla_decay"))
            act.wait_ge(sem("gla_decay"), at("gla_decay"))
            root(st2[0:CH, 16:32])
            norm()
            act.wait_ge(sem("router_diff"), due("act", "router_diff"))
            nc.scalar.activation(stat[:, 40:42], stat[:, 42:44], ACT.Exp).then_inc(sem("router_exp"), up("router_exp"))
            act.wait_ge(sem("router_exp"), at("router_exp"))
            act.wait_ge(sem("most_known"), due("act", "most_known"))
            fullest = act.value_load(most_int, min_val=0, max_val=T)
            before_branch = counts_now()
            with act.If(fullest <= SLOTS):
                with act.Fori(0, NEXP) as e:
                    enter(e)
                    for i in range(FFE // STEP):
                        act.wait_ge(sem("slot_hidden_psum"), due("act", "slot_hidden_psum"))
                        nc.scalar.activation(U(2 + i % 2, size=2 * SLOTS), ps[:, i % 2, 0:2 * SLOTS], ACT.Silu).then_inc(sem("slot_hidden_act"), up("slot_hidden_act"))
                        act.wait_ge(sem("slot_hidden_act"), at("slot_hidden_act"))
                    leave(NEXP)
            go_back(before_branch)
            with act.Else():
                with act.Fori(0, NEXP) as e:
                    enter(e)
                    ffn(FFE // STEP, True)
                    leave(NEXP)
            norm()

        @block.vector
        def _(dve):
            v = nc.vector

            def V(ins):
                ins.then_inc(sem("dve_order"), up("dve_order"))
                dve.wait_ge(sem("dve_order"), at("dve_order"))

            def mul(o, i0, i1):
                V(v.tensor_tensor(o, i0, i1, ALU.mult))

            def add(o, i0, i1):
                V(v.tensor_tensor(o, i0, i1, ALU.add))

            def sub(o, i0, i1):
                V(v.tensor_tensor(o, i0, i1, ALU.subtract))

            def ts(o, i, s1, s2, op0, op1=None):
                V(v.tensor_scalar(o, i, s1, s2, op0, op1) if op1 is not None else v.tensor_scalar(o, i, s1, None, op0))

            def stt(o, i0, sc, i1, op0, op1):
                V(v.scalar_tensor_tensor(o, i0, sc, i1, op0, op1))

            def copy(o, i):
                V(v.tensor_copy(o, i))

            def red(o, i, op):
                V(v.tensor_reduce(o, i, AX, op))

            def inv_root(o, ss, n, eps):
                v.tensor_scalar(o, ss, 1.0 / n, eps, ALU.mult, ALU.add).then_inc(sem("root_in"), up("root_in"))
                dve.wait_ge(sem("root_in"), at("root_in"))
                dve.wait_ge(sem("root_out"), due("dve", "root_out"))
                V(v.reciprocal(o, o))

            hrows = U(14, 2).rearrange("p (n d) -> p n d", n=NT)

            def norm(src, rows, gain, dst, col=0):
                for t in range(NT):
                    dve.wait_ge(sem("norm_root"), due("dve", "norm_root"))
                    m = stat[:, col + t:col + t + 1]
                    V(v.reciprocal(m, m))
                    v.tensor_scalar(rows[:, t, :], src[:, t, :], m, None, ALU.mult).then_inc(sem("norm_rows"), up("norm_rows"))
                    dve.wait_ge(sem("norm_rows"), at("norm_rows"))
                for t in range(NT):
                    for half in range(2):
                        dve.wait_ge(sem("norm_T"), due("dve", "norm_T"))
                        p = ps[:, 4 + 2 * t + half, :].rearrange("p (k t) -> p k t", k=4)
                        d = dst[:, 4 * half:4 * half + 4, t * P:(t + 1) * P]
                        if gain is None:
                            copy(d, p)
                        else:
                            done = "hT_ready" if t == 1 and half == 1 else "dve_order"
                            v.tensor_tensor(d, p, gain[:, 4 * half:4 * half + 4].unsqueeze(2).broadcast_to([P, 4, P]), ALU.mult).then_inc(sem(done), up(done))
                            dve.wait_ge(sem(done), at(done))

            def residual():
                dve.wait_ge(sem("gainrow_loaded"), due("dve", "gainrow_loaded", 16))
                for t in range(NT):
                    dve.wait_ge(sem("rows_square"), due("dve", "rows_square"))
                    V(v.reciprocal(stat[:, 8 + t:9 + t], stat[:, 8 + t:9 + t]))
                    done = "gainrow_used" if t else "dve_order"
                    v.scalar_tensor_tensor(U(13), banks(4 + 2 * t, 2), stat[:, 8 + t:9 + t], gainrow[:, :], ALU.mult, ALU.mult).then_inc(sem(done), up(done))
                    dve.wait_ge(sem(done), at(done))
                    v.tensor_tensor(x[:, t, :], x[:, t, :], U(13), ALU.add).then_inc(sem("norm_in"), up("norm_in"))
                    dve.wait_ge(sem("norm_in"), at("norm_in"))

            def plain_residual():
                dve.wait_ge(sem("sum_psum"), due("dve", "sum_psum"))
                for t in range(NT):
                    v.tensor_tensor(x[:, t, :], x[:, t, :], banks(4 + 2 * t, 2), ALU.add).then_inc(sem("norm_in"), up("norm_in"))
                    dve.wait_ge(sem("norm_in"), at("norm_in"))

            def softmax(n, scale, table, factor=None):
                S3 = U(0)[:, 0:4 * n].rearrange("p (h s) -> p h s", h=4)
                p = banks(4, 2)[:, 0:4 * n].rearrange("p (h s) -> p h s", h=4)
                dve.wait_ge(sem("scores"), due("dve", "scores"))
                if table is None:
                    ts(S3, p, scale, None, ALU.mult)
                else:
                    stt(S3, p, scale, table, ALU.mult, ALU.add)
                red(stat[:, 16:20], S3, ALU.max)
                v.tensor_tensor(S3, S3, stat[:, 16:20].unsqueeze(2).broadcast_to([P, 4, n]), ALU.subtract).then_inc(sem("exp_in"), up("exp_in"))
                dve.wait_ge(sem("exp_in"), at("exp_in"))
                dve.wait_ge(sem("exp_out"), due("dve", "exp_out"))
                red(stat[:, 20:24], S3, ALU.add)
                V(v.reciprocal(stat[:, 24:28], stat[:, 20:24]))
                if factor is not None:
                    factor()
                v.tensor_tensor(S3, S3, stat[:, 24:28].unsqueeze(2).broadcast_to([P, 4, n]), ALU.mult).then_inc(sem("weights_ready"), up("weights_ready"))
                dve.wait_ge(sem("weights_ready"), at("weights_ready"))
                dve.wait_ge(sem("weightsT_psum"), due("dve", "weightsT_psum"))
                w = min(n, P)
                cols_ = 4 * P * max(1, n // P)
                v.tensor_copy(U(1)[0:w, 0:cols_], banks(6, 2, w)[:, 0:cols_]).then_inc(sem("weightsT_ready"), up("weightsT_ready"))
                dve.wait_ge(sem("weightsT_ready"), at("weightsT_ready"))

            def ffn(steps, gated, gate=None):
                for i in range(steps):
                    for j in range(2):
                        b = 2 * (i % 2) + j
                        he, a1 = U(i % 2, off=j * T, size=T), U(2 + b, size=T)
                        dve.wait_ge(sem("hidden_act"), due("dve", "hidden_act"))
                        if not gated:
                            v.tensor_tensor(he, a1, a1, ALU.mult).then_inc(sem("hidden_ready"), up("hidden_ready"))
                            dve.wait_ge(sem("hidden_ready"), at("hidden_ready"))
                        elif gate is None:
                            v.tensor_tensor(he, a1, ps[:, b, T:2 * T], ALU.mult).then_inc(sem("hidden_ready"), up("hidden_ready"))
                            dve.wait_ge(sem("hidden_ready"), at("hidden_ready"))
                        else:
                            v.tensor_tensor(a1, a1, gate, ALU.mult).then_inc(sem("gate_order"), up("gate_order"))
                            dve.wait_ge(sem("gate_order"), at("gate_order"))
                            v.tensor_tensor(he, a1, ps[:, b, T:2 * T], ALU.mult).then_inc(sem("hidden_ready"), up("hidden_ready"))
                            dve.wait_ge(sem("hidden_ready"), at("hidden_ready"))

            V(v.memset(relb[NBUCKET:NBUCKET + 1, :], NEG))
            V(v.memset(muT[:, :, :], 0.0))
            V(v.memset(stat[:, :], 0.0))
            V(v.memset(resets[:, :, :], 1.0))
            v.memset(resets[:, :, 0:1], 0.0).then_inc(sem("cleared"), up("cleared"))
            dve.wait_ge(sem("cleared"), at("cleared"))
            dve.wait_ge(sem("params_loaded"), count_of("params_loaded").posted)
            dve.wait_ge(sem("consts_loaded"), due("dve", "consts_loaded", 32))
            v.tensor_copy(stat[:, 61:62], stat[:, 62:63]).then_inc(sem("bias_operands"), up("bias_operands"))
            dve.wait_ge(sem("bias_operands"), at("bias_operands"))
            dve.wait_ge(sem("bias_psum"), due("dve", "bias_psum"))
            v.tensor_copy(U(2, 2), banks(0, 4)).then_inc(sem("bias_rows"), up("bias_rows"))
            dve.wait_ge(sem("bias_rows"), at("bias_rows"))
            mem = merged[:, :, :].rearrange("p k t -> p (k t)").rearrange("p (n d) -> p n d", n=NT)
            norm(mem, U(4, 2).rearrange("p (n d) -> p n d", n=NT), None, memT, 4)
            dve.wait_ge(sem("x_loaded"), due("dve", "x_loaded", 16))
            dve.wait_ge(sem("bias_table"), due("dve", "bias_table", 32))
            for l in range(DEPTH):
                norm(x, hrows, gT["ln_mix_pre"][:, l, :], hT)
                kT = U(3, parts=HD).rearrange("p (h t) -> p h t", h=H)
                X = U(5, parts=HD, size=2 * NCMP * CMP_LEN).rearrange("p (c n l) -> p c n l", c=2, l=CMP_LEN)
                dve.wait_ge(sem("nsa_inputs"), due("dve", "nsa_inputs"))
                for c in range(2):
                    win = kT[:, c, :].rearrange("p (n l) -> p n l", l=CMP_STRIDE)
                    for half in range(2):
                        r = slice(half * CMP_STRIDE, (half + 1) * CMP_STRIDE)
                        done = "cmp_windows" if c and half else "dve_order"
                        v.tensor_tensor(X[:, c, :, r], win[:, half:half + NCMP, :], peT[:, l, r].unsqueeze(1).broadcast_to([HD, NCMP, CMP_STRIDE]), ALU.add).then_inc(sem(done), up(done))
                        dve.wait_ge(sem(done), at(done))
                dve.wait_ge(sem("cmp_psum"), due("dve", "cmp_psum"))
                copy(U(4, off=256, size=NCMP, parts=HD), ps[0:HD, 4, 0:NCMP])
                v.tensor_copy(U(4, off=320, size=HD, parts=NCMP), ps[0:NCMP, 4, 64:64 + HD]).then_inc(sem("cmp_ready"), up("cmp_ready"))
                dve.wait_ge(sem("cmp_ready"), at("cmp_ready"))
                g3 = U(4, off=512, size=24).rearrange("p (t h b) -> p t h b", t=NT, h=H)
                for t in range(NT):
                    for kind, n in enumerate((NCMP, T, T)):
                        def gate():
                            mul(stat[:, 24:28], stat[:, 24:28], g3[:, t, :, kind])
                            if kind == 0 and t == 0:
                                ts(stat[:, 24:28], stat[:, 24:28], cst[:, C_TMASK:C_TMASK + 1], None, ALU.mult)
                        softmax(n, HD ** -0.5, bias[:, t, :, CMP_LEN - 1::CMP_STRIDE] if kind == 0 else bias[:, t, :, :], gate)
                        dve.wait_ge(sem("attn_out"), due("dve", "attn_out"))
                v.tensor_copy(oT[:, 0, :, :], ps[:, 3, :].rearrange("p (k t) -> p k t", k=2)).then_inc(sem("nsa_done"), up("nsa_done"))
                dve.wait_ge(sem("nsa_done"), at("nsa_done"))
                qk, vg, rot = (U(i).rearrange("p (t c) -> p t c", t=NT) for i in (6, 7, 8))
                qkT = U(9, 2, parts=HD).rearrange("p (h t) -> p h t", h=8)
                att = U(11, 2).rearrange("p (h n t) -> p h n t", h=H, n=NT)
                dve.wait_ge(sem("ret_inputs"), due("dve", "ret_inputs"))
                for t in range(NT):
                    u = qk[:, t, :].rearrange("p (h f d) -> p h f d", h=8, f=2)
                    r = rot[:, t, :].rearrange("p (h f d) -> p h f d", h=8, f=2)
                    tmp = U(13, size=512).rearrange("p (f h d) -> p f h d", f=2, h=8)
                    cos, sin = (cst[:, c + 32 * t:c + 32 * (t + 1)].unsqueeze(1).broadcast_to([P, 8, 32]) for c in (C_COS, C_SIN))
                    for f, comb in ((0, ALU.subtract), (1, ALU.add)):
                        mul(tmp[:, 0], u[:, :, f, :], cos)
                        mul(tmp[:, 1], u[:, :, 1 - f, :], sin)
                        done = "ret_rotated" if f else "dve_order"
                        v.tensor_tensor(r[:, :, f, :], tmp[:, 0], tmp[:, 1], comb).then_inc(sem(done), up(done))
                        dve.wait_ge(sem(done), at(done))
                for t in range(NT):
                    dve.wait_ge(sem("ret_T_psum"), due("dve", "ret_T_psum"))
                    v.tensor_copy(qkT[:, :, t * P:(t + 1) * P], banks(4 + 2 * t, 2, HD).rearrange("p (h t) -> p h t", h=8)).then_inc(sem("ret_T"), up("ret_T"))
                    dve.wait_ge(sem("ret_T"), at("ret_T"))
                for h in range(H):
                    dve.wait_ge(sem("ret_scores"), due("dve", "ret_scores"))
                    v.tensor_tensor(att[:, h, :, :], ps[:, 4 + h, :].rearrange("p (n t) -> p n t", n=NT), decay[:, h, :, :], ALU.mult).then_inc(sem("ret_att"), up("ret_att"))
                    dve.wait_ge(sem("ret_att"), at("ret_att"))
                dve.wait_ge(sem("ret_out_psum"), due("dve", "ret_out_psum"))

                def head_norm(o3, src, n, eps, parts, tmp3):
                    m, q = st2[0:parts, 32:32 + n], st2[0:parts, 48:48 + n]
                    red(m, src, ALU.add)
                    ts(m, m, 1.0 / HD, None, ALU.mult)
                    sub(o3, src, m.unsqueeze(2).broadcast_to([parts, n, HD]))
                    mul(tmp3, o3, o3)
                    red(q, tmp3, ALU.add)
                    inv_root(q, q, HD, eps)
                    mul(o3, o3, q.unsqueeze(2).broadcast_to([parts, n, HD]))
                orow = U(13, size=512)
                head_norm(orow.rearrange("p (g d) -> p g d", d=HD), ps[:, 4, :].rearrange("p (g d) -> p g d", d=HD), NT * H, 1e-5, P,
                          U(13, off=512, size=512).rearrange("p (g d) -> p g d", d=HD))
                o3 = orow.rearrange("p (t c) -> p t c", t=NT)
                mul(o3, o3, retg[:, l, :].unsqueeze(1).broadcast_to([P, NT, MW]))
                v.tensor_tensor(o3, o3, vg[:, :, MW:2 * MW], ALU.mult).then_inc(sem("ret_out_rows"), up("ret_out_rows"))
                dve.wait_ge(sem("ret_out_rows"), at("ret_out_rows"))
                dve.wait_ge(sem("ret_outT"), due("dve", "ret_outT"))
                v.tensor_copy(oT[:, 1, :, :], ps[:, 5, :].rearrange("p (k t) -> p k t", k=2)).then_inc(sem("ret_done"), up("ret_done"))
                dve.wait_ge(sem("ret_done"), at("ret_done"))
                z = U(0, 4, size=15 * (T + 1), parts=HD).rearrange("p (g t) -> p g t", g=15)
                V(v.memset(z[:, :, 0:1], 0.0))
                v.memset(z[:, 12:14, :], 0.0).then_inc(sem("rwkv_z_cleared"), up("rwkv_z_cleared"))
                dve.wait_ge(sem("rwkv_z_cleared"), at("rwkv_z_cleared"))
                cb, cc, cx = (U(13 + i // 2, off=512 * (i % 2), size=512).rearrange("p (k t) -> p k t", k=2) for i in range(3))
                cu = U(12, size=2 * (T + 2)).rearrange("p (k t) -> p k t", k=2)
                cy = U(14, off=512, size=512).rearrange("p (k t) -> p k t", k=2)
                dve.wait_ge(sem("conv_inputs"), due("dve", "conv_inputs"))
                V(v.memset(cu[:, :, 0:2], 0.0))
                mul(cu[:, :, 2:T + 2], cc, cx)
                for k in range(2):
                    ts(cy[:, k, :], cu[:, k, 0:T], convw[:, l, 0, k:k + 1], None, ALU.mult)
                    for j in (1, 2):
                        stt(cy[:, k, :], cu[:, k, j:j + T], convw[:, l, j, k:k + 1], cy[:, k, :], ALU.mult, ALU.add)
                v.tensor_tensor(oT[:, 3, :, :], cb, cy, ALU.mult).then_inc(sem("conv_done"), up("conv_done"))
                dve.wait_ge(sem("conv_done"), at("conv_done"))
                dve.wait_ge(sem("rwkv_inputs"), due("dve", "rwkv_inputs"))
                mix = U(4, 4, size=15 * T, parts=HD).rearrange("p (g t) -> p g t", g=15)
                sub(mix, z[:, :, 0:T], z[:, :, 1:T + 1])
                mul(mix, mix, muT[:, l, :].unsqueeze(2).broadcast_to([HD, 15, T]))
                v.tensor_tensor(mix, mix, z[:, :, 1:T + 1], ALU.add).then_inc(sem("rwkv_mixed"), up("rwkv_mixed"))
                dve.wait_ge(sem("rwkv_mixed"), at("rwkv_mixed"))
                u4 = lambda i: U(i, parts=HD).rearrange("p (h t) -> p h t", h=H)
                u16 = lambda i: U(i, parts=HD).rearrange("p (g t) -> p g t", g=HC)
                vb = lambda name: vecs[name][:, l, :].unsqueeze(2).broadcast_to([HD, H, T])
                r, k, vv = u4(4), u4(5), u4(6)
                kk, sq, kn = u4(10), u4(11), u4(12)
                mul(kk, k, vb("rwkv_k_k"))
                v.tensor_tensor(sq, kk, kk, ALU.mult).then_inc(sem("rwkv_kk_sq"), up("rwkv_kk_sq"))
                dve.wait_ge(sem("rwkv_kk_sq"), at("rwkv_kk_sq"))
                dve.wait_ge(sem("rwkv_sigmoids"), due("dve", "rwkv_sigmoids"))
                lw, cs = u4(0), u4(2)
                ts(lw, lw, -math.exp(-0.5), None, ALU.mult)
                V(v.tensor_tensor_scan(U(2, parts=HD), resets[0:HD, :, :].rearrange("p g t -> p (g t)"), U(0, parts=HD), 0.0, ALU.mult, ALU.add))
                v.tensor_tensor(u4(3), cs, lw, ALU.subtract).then_inc(sem("rwkv_cumulated"), up("rwkv_cumulated"))
                dve.wait_ge(sem("rwkv_cumulated"), at("rwkv_cumulated"))
                ts(st2[0:HD, 0:H], vecs["rwkv_k_a"][:, l, :], -1.0, 1.0, ALU.mult, ALU.add)
                mul(kn, u4(1), vb("rwkv_k_a"))
                add(kn, kn, st2[0:HD, 0:H].unsqueeze(2).broadcast_to([HD, H, T]))
                mul(kn, kn, k)
                dve.wait_ge(sem("rwkv_kk_norm"), due("dve", "rwkv_kk_norm"))
                v.tensor_scalar(sq, banks(4, 2, HD).rearrange("p (h t) -> p h t", h=H), 1e-24, None, ALU.max).then_inc(sem("root_in"), up("root_in"))
                dve.wait_ge(sem("root_in"), at("root_in"))
                dve.wait_ge(sem("root_out"), due("dve", "root_out"))
                V(v.reciprocal(sq, sq))
                mul(kk, kk, sq)
                dve.wait_ge(sem("rwkv_decays"), due("dve", "rwkv_decays"))
                AR = U(13, 2, parts=HD).rearrange("p (g c) -> p g c", g=HC)
                mul(AR[:, :, 0:CH], u16(3), u16(10))
                mul(AR[:, :, CH:], u16(8), u16(4))
                copy(st2[0:HD, 16:32].rearrange("p (g a) -> p g a", a=1), u16(8)[:, :, CH - 1:CH])
                mul(u4(0), kk, u4(1))
                mul(u4(0), u4(0), u4(9))
                mul(u4(2), kn, u4(9))
                mul(kn, kn, r)
                v.tensor_tensor(kn, kn, vb("rwkv_r_k"), ALU.mult).then_inc(sem("rwkv_operands"), up("rwkv_operands"))
                dve.wait_ge(sem("rwkv_operands"), at("rwkv_operands"))
                for i, b in ((1, 4), (3, 6), (4, 4)):
                    dve.wait_ge(sem("rwkv_rows_psum"), due("dve", "rwkv_rows_psum"))
                    v.tensor_copy(U(i, parts=HD), banks(b, 2, HD)).then_inc(sem("rwkv_rows"), up("rwkv_rows"))
                    dve.wait_ge(sem("rwkv_rows"), at("rwkv_rows"))
                dve.wait_ge(sem("rwkv_gate_psum"), due("dve", "rwkv_gate_psum"))
                copy(st2[0:HD, 0:HC], ps[0:HD, 6, 0:HC])
                v.tensor_copy(U(5, parts=HD), banks(4, 2, HD)).then_inc(sem("rwkv_gate_rows"), up("rwkv_gate_rows"))
                dve.wait_ge(sem("rwkv_gate_rows"), at("rwkv_gate_rows"))
                gB, gK = (U(i, 2, parts=HD).rearrange("p (g c) -> p g c", g=HC) for i in (8, 10))
                for g in (gB, gK):
                    dve.wait_ge(sem("rwkv_gram_psum"), due("dve", "rwkv_gram_psum"))
                    v.tensor_tensor(g, banks(4, 4, HD).rearrange("p (g c) -> p g c", g=HC), cst[0:CH, C_RMASK:C_RMASK + 128].unsqueeze(1).broadcast_to([CH, HC, 128]), ALU.mult).then_inc(sem("rwkv_gram"), up("rwkv_gram"))
                    dve.wait_ge(sem("rwkv_gram"), at("rwkv_gram"))
                X, XT, M, Y = u16(15), u16(6), u16(12), u16(7)
                m64 = lambda c: cst[0:CH, c:c + CH].unsqueeze(1).broadcast_to([CH, HC, CH])
                dve.wait_ge(sem("rwkv_gram_psum"), due("dve", "rwkv_gram_psum"))
                b2 = lambda b: banks(b, 2, HD).rearrange("p (g c) -> p g c", g=HC)
                mul(X, b2(4), m64(C_M1))
                add(X, X, m64(C_IDENT))
                mul(XT, gB[:, :, 0:CH], m64(C_M1T))
                add(XT, XT, m64(C_IDENT))
                for n in range(len(LEVELS)):
                    v.tensor_tensor(M, gB[:, :, 0:CH], m64(C_LEVEL + CH * n), ALU.mult).then_inc(sem("rwkv_inv_M"), up("rwkv_inv_M"))
                    dve.wait_ge(sem("rwkv_inv_M"), at("rwkv_inv_M"))
                    dve.wait_ge(sem("rwkv_inv_Y_psum"), due("dve", "rwkv_inv_Y_psum"))
                    v.tensor_copy(Y, b2(4)).then_inc(sem("rwkv_inv_Y"), up("rwkv_inv_Y"))
                    dve.wait_ge(sem("rwkv_inv_Y"), at("rwkv_inv_Y"))
                    dve.wait_ge(sem("rwkv_inv_X_psum"), due("dve", "rwkv_inv_X_psum"))
                    sub(X, X, b2(6))
                    sub(XT, XT, b2(4))
                S = U(15, off=512, size=256, parts=HD).rearrange("p (h e) -> p h e", h=H)
                v.memset(S, 0.0).then_inc(sem("rwkv_state"), up("rwkv_state"))
                dve.wait_ge(sem("rwkv_state"), at("rwkv_state"))
                y3 = U(0, parts=HD).rearrange("p (c n) -> p c n", c=NC)
                decays = st2[0:HD, 16:32].rearrange("p (h c) -> p h c", h=H)
                for c in range(NC):
                    dve.wait_ge(sem("rwkv_W_psum"), due("dve", "rwkv_W_psum"))
                    v.tensor_copy(U(15, off=0, size=256, parts=HD), ps[0:HD, 4, 0:MW]).then_inc(sem("rwkv_W"), up("rwkv_W"))
                    dve.wait_ge(sem("rwkv_W"), at("rwkv_W"))
                    dve.wait_ge(sem("rwkv_SA_psum"), due("dve", "rwkv_SA_psum"))
                    v.tensor_scalar(U(15, off=256, size=256, parts=HD), ps[0:HD, 5, 0:MW], -1.0, None, ALU.mult).then_inc(sem("rwkv_SA"), up("rwkv_SA"))
                    dve.wait_ge(sem("rwkv_SA"), at("rwkv_SA"))
                    dve.wait_ge(sem("rwkv_Y_psum"), due("dve", "rwkv_Y_psum"))
                    if c < NC - 1:
                        add(S, S, ps[0:HD, 7, 0:MW].rearrange("p (h e) -> p h e", h=H))
                    copy(y3[:, c, :], ps[0:HD, 6, 0:MW])
                    if c < NC - 1:
                        v.tensor_tensor(S, S, decays[:, :, c:c + 1].broadcast_to([HD, H, HD]), ALU.mult).then_inc(sem("rwkv_state"), up("rwkv_state"))
                        dve.wait_ge(sem("rwkv_state"), at("rwkv_state"))
                y16 = U(0, parts=HD).rearrange("p (g d) -> p g d", d=HD)
                head_norm(y16, y16, HC, 64e-5, HD, u16(2))
                mul(y3, y3, lng[:, l, :].unsqueeze(1).broadcast_to([HD, NC, MW]))
                add(y3, y3, lnb[:, l, :].unsqueeze(1).broadcast_to([HD, NC, MW]))
                mul(u16(2), u16(4), st2[0:HD, 0:HC].unsqueeze(2).broadcast_to([HD, HC, HD]))
                y4 = U(0, parts=HD).rearrange("p (c h d) -> p c h d", c=NC, h=H)
                add(y4, y4, U(2, parts=HD).rearrange("p (h c d) -> p c h d", h=H, c=NC))
                v.tensor_tensor(U(0, parts=HD), U(0, parts=HD), U(5, parts=HD), ALU.mult).then_inc(sem("rwkv_out_rows"), up("rwkv_out_rows"))
                dve.wait_ge(sem("rwkv_out_rows"), at("rwkv_out_rows"))
                dve.wait_ge(sem("rwkv_outT"), due("dve", "rwkv_outT"))
                v.tensor_copy(oT[:, 2, :, :], ps[:, 4, :].rearrange("p (k t) -> p k t", k=2)).then_inc(sem("rwkv_done"), up("rwkv_done"))
                dve.wait_ge(sem("rwkv_done"), at("rwkv_done"))
                residual()
                norm(x, hrows, gT["ln_xa_pre"][:, l, :], hT)
                v.tensor_tensor(merged[:, :, :], memT, gT["ln_mem"][:, l, :].unsqueeze(2).broadcast_to([P, KD, T]), ALU.mult).then_inc(sem("mem_ready"), up("mem_ready"))
                dve.wait_ge(sem("mem_ready"), at("mem_ready"))
                for t in range(NT):
                    softmax(T, (D // 4) ** -0.5, None)
                residual()
                norm(x, hrows, gT["ln_mlp_pre"][:, l, :], hT)
                ffn(FF1 // STEP, False)
                residual()
            xr = U(8, 2, size=4 * (T + 3)).rearrange("p (c t) -> p c t", c=4)
            gd = fbT[:, 0:1024].rearrange("p (w c n) -> p w c n", w=2, c=4)
            v.memset(xr[:, :, 0:3], 0.0).then_inc(sem("lru_pad"), up("lru_pad"))
            dve.wait_ge(sem("lru_pad"), at("lru_pad"))
            v.memset(gd, 0.0).then_inc(sem("lru_gate_cleared"), up("lru_gate_cleared"))
            dve.wait_ge(sem("lru_gate_cleared"), at("lru_gate_cleared"))
            norm(x, hrows, gT["norm_mix_2"][:, 0, :], hT)
            dve.wait_ge(sem("lru_exp"), due("dve", "lru_exp"))
            y_, z_, z2, acc, sp8 = (stat[:, 36 + 4 * i:40 + 4 * i] for i in range(5))
            ts(z_, y_, 2.0, None, ALU.add)
            V(v.reciprocal(z_, z_))
            mul(z_, z_, y_)
            mul(z2, z_, z_)
            ts(acc, z2, 1.0 / 19, 1.0 / 17, ALU.mult, ALU.add)
            for n in (15, 13, 11, 9, 7, 5, 3, 1):
                mul(acc, acc, z2)
                ts(acc, acc, 1.0 / n, None, ALU.add)
            mul(acc, acc, z_)
            ts(sp8, vec2["ev_lambda_2"][:, :], -1.0, 0.0, ALU.mult, ALU.max)
            stt(sp8, acc, 2.0, sp8, ALU.mult, ALU.add)
            ts(sp8, sp8, 8.0, None, ALU.mult)
            dve.wait_ge(sem("even_inputs"), due("dve", "even_inputs"))
            fu, fm, f1, f2 = (U(2, off=256 * i, size=256, parts=8) for i in range(4))
            ts(fm, fu, 0.0, None, ALU.min)
            ts(f1, fu, -1.0, None, ALU.mult)
            v.tensor_tensor(f1, fu, f1, ALU.max).then_inc(sem("fox_exp_in"), up("fox_exp_in"))
            dve.wait_ge(sem("fox_exp_in"), at("fox_exp_in"))
            xc, tmp4 = U(13).rearrange("p (c t) -> p c t", c=4), U(4).rearrange("p (c t) -> p c t", c=4)
            for c in range(4):
                ts(xc[:, c, :], xr[:, c, 0:T], convw2[:, 0, c:c + 1], vec2["ev_conv_b_2"][:, c:c + 1], ALU.mult, ALU.add)
                for j in (1, 2, 3):
                    done = "lru_conv" if c == 3 and j == 3 else "dve_order"
                    v.scalar_tensor_tensor(xc[:, c, :], xr[:, c, j:j + T], convw2[:, j, c:c + 1], xc[:, c, :], ALU.mult, ALU.add).then_inc(sem(done), up(done))
                    dve.wait_ge(sem(done), at(done))
            dve.wait_ge(sem("fox_ln"), due("dve", "fox_ln"))
            sub(fm, fm, f2)
            V(v.memset(fu, 1.0))
            V(v.tensor_tensor_scan(f1, fu, fm, 0.0, ALU.mult, ALU.add))
            v.tensor_scalar(f2, f1, -1.0, None, ALU.mult).then_inc(sem("fox_cum"), up("fox_cum"))
            dve.wait_ge(sem("fox_cum"), at("fox_cum"))
            dve.wait_ge(sem("lru_sigmoids"), due("dve", "lru_sigmoids"))
            la, iu, aa, th = (U(i).rearrange("p (c t) -> p c t", c=4) for i in (4, 5, 6, 7))
            v.tensor_tensor(la, la, sp8.unsqueeze(2).broadcast_to([P, 4, T]), ALU.mult).then_inc(sem("lru_log_a"), up("lru_log_a"))
            dve.wait_ge(sem("lru_log_a"), at("lru_log_a"))
            mul(iu, iu, xc)
            yr, gl = U(10), U(11)
            mul(gl, yr, yr)
            ts(gl, gl, 0.044715, 1.0, ALU.mult, ALU.add)
            mul(gl, gl, yr)
            v.tensor_scalar(gl, gl, math.sqrt(2.0 / math.pi), None, ALU.mult).then_inc(sem("gelu_in"), up("gelu_in"))
            dve.wait_ge(sem("gelu_in"), at("gelu_in"))
            dve.wait_ge(sem("lru_a"), due("dve", "lru_a"))
            ts(la, th, 1.0, None, ALU.add)
            V(v.reciprocal(U(4), U(4)))
            mul(th, th, la)
            v.tensor_scalar(th, th, 2.0, None, ALU.mult).then_inc(sem("root_in"), up("root_in"))
            dve.wait_ge(sem("root_in"), at("root_in"))
            dve.wait_ge(sem("root_out"), due("dve", "root_out"))
            mul(iu, iu, th)
            for c in range(4):
                V(v.tensor_tensor_scan(la[:, c, :], aa[:, c, :], iu[:, c, :], 0.0, ALU.mult, ALU.add))
            dve.wait_ge(sem("gelu_tanh"), due("dve", "gelu_tanh"))
            ts(gl, gl, 1.0, 0.5, ALU.add, ALU.mult)
            mul(gl, gl, yr)
            v.tensor_tensor(merged[:, 0:4, :].rearrange("p c t -> p (c t)"), U(4), gl, ALU.mult).then_inc(sem("lru_done"), up("lru_done"))
            dve.wait_ge(sem("lru_done"), at("lru_done"))
            for t in range(NT):
                for hg in range(2):
                    softmax(T, 1.0, causal[:, t, :].unsqueeze(1).broadcast_to([P, 4, T]))
            plain_residual()
            norm(x, hrows, gT["norm_ffn_2"][:, 0, :], hT)
            ffn(FF2 // STEP, True)
            plain_residual()
            norm(x, hrows, gT["norm_mix_2"][:, 1, :], hT)
            V(v.memset(U(14), 0.0))
            dve.wait_ge(sem("gla_gate_psum"), due("dve", "gla_gate_psum"))
            u3 = lambda i: U(i).rearrange("p (h t) -> p h t", h=H)
            g3 = lambda i: U(i).rearrange("p (g t) -> p g t", g=HC)
            add(u3(4), banks(4, 2).rearrange("p (h t) -> p h t", h=H), vec2["od_gate_b_2"][:, :].unsqueeze(2).broadcast_to([P, H, T]))
            ts(u3(5), u3(4), -1.0, None, ALU.mult)
            v.tensor_tensor(U(5), U(4), U(5), ALU.max).then_inc(sem("gla_exp_in"), up("gla_exp_in"))
            dve.wait_ge(sem("gla_exp_in"), at("gla_exp_in"))
            ts(U(4), U(4), 0.0, None, ALU.min)
            dve.wait_ge(sem("gla_ln"), due("dve", "gla_ln"))
            sub(U(4), U(4), U(6))
            ts(U(5), U(4), 1.0 / 16, None, ALU.mult)
            V(v.tensor_tensor_scan(U(4), resets[:, :, :].rearrange("p g t -> p (g t)"), U(5), 0.0, ALU.mult, ALU.add))
            bl = g3(4)[:, :, CH - 1:CH]
            copy(st2[:, 0:HC].unsqueeze(2), bl)
            v.tensor_tensor(g3(7), bl.broadcast_to([P, HC, CH]), g3(4), ALU.subtract).then_inc(sem("gla_cum"), up("gla_cum"))
            dve.wait_ge(sem("gla_cum"), at("gla_cum"))
            dve.wait_ge(sem("gla_exps"), due("dve", "gla_exps"))
            mul(U(10), U(9), U(7))
            mul(U(8), U(8), U(5))
            v.tensor_tensor(U(9), U(9), U(6), ALU.mult).then_inc(sem("gla_operands"), up("gla_operands"))
            dve.wait_ge(sem("gla_operands"), at("gla_operands"))
            dve.wait_ge(sem("gla_rows_psum"), due("dve", "gla_rows_psum"))
            v.tensor_copy(U(11, 2, parts=CH), banks(4, 4, CH)).then_inc(sem("gla_rows"), up("gla_rows"))
            dve.wait_ge(sem("gla_rows"), at("gla_rows"))
            dve.wait_ge(sem("gla_scores_psum"), due("dve", "gla_scores_psum"))
            v.tensor_tensor(U(13, parts=CH).rearrange("p (g c) -> p g c", g=HC), banks(4, 2, CH).rearrange("p (g c) -> p g c", g=HC), cst[0:CH, C_RMASK + 64:C_RMASK + 128].unsqueeze(1).broadcast_to([CH, HC, CH]), ALU.mult).then_inc(sem("gla_scores"), up("gla_scores"))
            dve.wait_ge(sem("gla_scores"), at("gla_scores"))
            dve.wait_ge(sem("gla_decay"), due("dve", "gla_decay"))
            state = U(14).rearrange("p (h e) -> p h e", h=H)
            orow = fbT[0:CH, 4096:8192].rearrange("p (c n) -> p c n", c=NC)
            dec = st2[:, 0:HC].rearrange("p (h c) -> p h c", h=H)
            v.tensor_copy(stat[:, 61:62], stat[:, 62:63]).then_inc(sem("gla_state"), up("gla_state"))
            dve.wait_ge(sem("gla_state"), at("gla_state"))
            for c in range(NC):
                dve.wait_ge(sem("gla_out_psum"), due("dve", "gla_out_psum"))
                copy(orow[:, c, :], banks(4, 2, CH))
                if c < NC - 1:
                    mul(state, state, dec[:, :, c:c + 1].broadcast_to([P, H, T]))
                    v.tensor_tensor(state, state, banks(6, 2).rearrange("p (h e) -> p h e", h=H), ALU.add).then_inc(sem("gla_state"), up("gla_state"))
                    dve.wait_ge(sem("gla_state"), at("gla_state"))
            o16 = fbT[0:CH, 4096:8192].rearrange("p (g e) -> p g e", g=HC)
            sq16 = U(4, 4, parts=CH).rearrange("p (g e) -> p g e", g=HC)
            mul(sq16, o16, o16)
            red(st2[0:CH, 16:32], sq16, ALU.add)
            inv_root(st2[0:CH, 16:32], st2[0:CH, 16:32], T, 1e-6)
            mul(o16, o16, st2[0:CH, 16:32].unsqueeze(2).broadcast_to([CH, HC, T]))
            dve.wait_ge(sem("gainrow_loaded"), due("dve", "gainrow_loaded", 16))
            v.tensor_tensor(orow, orow, gainrow[0:CH, :].unsqueeze(1).broadcast_to([CH, NC, D]), ALU.mult).then_inc(sem("gainrow_used"), up("gainrow_used"))
            dve.wait_ge(sem("gainrow_used"), at("gainrow_used"))
            v.tensor_tensor(fbT[0:CH, 4096:8192], fbT[0:CH, 4096:8192], fbT[0:CH, 0:4096], ALU.mult).then_inc(sem("gla_out_rows"), up("gla_out_rows"))
            dve.wait_ge(sem("gla_out_rows"), at("gla_out_rows"))
            dve.wait_ge(sem("gla_outT_psum"), due("dve", "gla_outT_psum"))
            v.tensor_copy(merged[:, :, :].rearrange("p k t -> p (k t)"), banks(4, 4)).then_inc(sem("gla_outT"), up("gla_outT"))
            dve.wait_ge(sem("gla_outT"), at("gla_outT"))
            plain_residual()
            norm(x, hrows, gT["norm_ffn_2"][:, 1, :], hT)
            lg = U(4, off=512, size=16).rearrange("p (t e) -> p t e", t=NT)
            top = U(4, off=544, size=16).rearrange("p (t e) -> p t e", t=NT)
            idxf = U(4, off=576, size=16).rearrange("p (t e) -> p t e", t=NT)
            idx = U(4, off=608, size=16).bitcast(U32).rearrange("p (t e) -> p t e", t=NT)
            gates = U(4, size=16).rearrange("p (t e) -> p t e", t=NT)
            dve.wait_ge(sem("router_psum"), due("dve", "router_psum"))
            copy(U(4, off=512, size=16), ps[:, 0, 0:16])
            for t in range(NT):
                V(v.max(top[:, t, :], lg[:, t, :]))
                V(v.max_index(idx[:, t, :], top[:, t, :], lg[:, t, :]))
            copy(idxf, idx)
            v.tensor_tensor(stat[:, 42:44].unsqueeze(2), top[:, :, 1:2], top[:, :, 0:1], ALU.subtract).then_inc(sem("router_diff"), up("router_diff"))
            dve.wait_ge(sem("router_diff"), at("router_diff"))
            dve.wait_ge(sem("router_exp"), due("dve", "router_exp"))
            ts(stat[:, 44:46], stat[:, 40:42], 1.0, None, ALU.add)
            V(v.reciprocal(stat[:, 44:46], stat[:, 44:46]))
            mul(stat[:, 46:48], stat[:, 44:46], stat[:, 40:42])
            iota = cst[:, C_IOTA:C_IOTA + NEXP]
            for t in range(NT):
                ts(lg[:, t, :], iota, idxf[:, t, 0:1], stat[:, 44 + t:45 + t], ALU.is_equal, ALU.mult)
                ts(gates[:, t, :], iota, idxf[:, t, 1:2], stat[:, 46 + t:47 + t], ALU.is_equal, ALU.mult)
                done = "router_gates" if t else "dve_order"
                v.tensor_tensor(gates[:, t, :], gates[:, t, :], lg[:, t, :], ALU.add).then_inc(sem(done), up(done))
                dve.wait_ge(sem(done), at(done))
            for t in range(NT):
                ts(chosen[:, t, :], iota, idxf[:, t, 0:1], None, ALU.is_equal)
                done = "chosen" if t else "dve_order"
                v.scalar_tensor_tensor(chosen[:, t, :], iota, idxf[:, t, 1:2], chosen[:, t, :], ALU.is_equal, ALU.add).then_inc(sem(done), up(done))
                dve.wait_ge(sem(done), at(done))
            dve.wait_ge(sem("slots_psum"), due("dve", "slots_psum"))
            copy(fbT[:, 6160:6184], ps[:, 2, 0:24])
            red(most, load[0:1, :], ALU.max)
            v.tensor_copy(most_int, most).then_inc(sem("most_known"), up("most_known"))
            dve.wait_ge(sem("most_known"), at("most_known"))
            fullest = dve.value_load(most_int, min_val=0, max_val=T)
            before_branch = counts_now()
            with dve.If(fullest <= SLOTS):
                slots_iota = cst[:, C_IOTA:C_IOTA + SLOTS]
                for t in range(NT):
                    for e in range(NEXP):
                        v.tensor_scalar(pick[:, e, t, :], slots_iota, slot[:, t, e:e + 1], chosen[:, t, e:e + 1], ALU.is_equal, ALU.mult).then_inc(sem("pick_order"), up("pick_order"))
                        dve.wait_ge(sem("pick_order"), at("pick_order"))
                v.tensor_tensor(pick_gate, pick, gates.rearrange("p t e -> p e t").unsqueeze(3).broadcast_to([P, NEXP, NT, SLOTS]), ALU.mult).then_inc(sem("picks"), up("picks"))
                dve.wait_ge(sem("picks"), at("picks"))
                dve.wait_ge(sem("spread_psum"), due("dve", "spread_psum"))
                v.tensor_copy(spread, banks(0, 4)).then_inc(sem("spread_ready"), up("spread_ready"))
                dve.wait_ge(sem("spread_ready"), at("spread_ready"))
                gain = gT["norm_ffn_2"][:, 1, :].unsqueeze(2).broadcast_to([P, KD, SLOTS])
                with dve.Fori(0, NEXP) as e:
                    enter(e)
                    dve.wait_ge(sem("slot_x_psum"), due("dve", "slot_x_psum"))
                    v.tensor_copy(spread_e, fbT[:, bass.ds(e * T + 4096, T)]).then_inc(sem("slot_spread"), up("slot_spread"))
                    dve.wait_ge(sem("slot_spread"), at("slot_spread"))
                    v.tensor_tensor(slot_x, banks(0, 2).rearrange("p (k c) -> p k c", k=KD), gain, ALU.mult).then_inc(sem("slot_x"), up("slot_x"))
                    dve.wait_ge(sem("slot_x"), at("slot_x"))
                    for i in range(FFE // STEP):
                        dve.wait_ge(sem("slot_hidden_act"), due("dve", "slot_hidden_act"))
                        v.tensor_tensor(U(i % 2, size=2 * SLOTS), U(2 + i % 2, size=2 * SLOTS), ps[:, i % 2, 2 * SLOTS:4 * SLOTS], ALU.mult).then_inc(sem("slot_hidden_ready"), up("slot_hidden_ready"))
                        dve.wait_ge(sem("slot_hidden_ready"), at("slot_hidden_ready"))
                    dve.wait_ge(sem("slot_y_psum"), due("dve", "slot_y_psum"))
                    v.tensor_copy(slot_y, banks(2, 2)).then_inc(sem("slot_y"), up("slot_y"))
                    dve.wait_ge(sem("slot_y"), at("slot_y"))
                    leave(NEXP)
            go_back(before_branch)
            with dve.Else():
                dve.wait_ge(sem("router_T_psum"), due("dve", "router_T_psum"))
                v.tensor_copy(U(4, off=64, size=T, parts=NEXP), ps[0:NEXP, 1, 0:T]).then_inc(sem("router_T"), up("router_T"))
                dve.wait_ge(sem("router_T"), at("router_T"))
                dve.wait_ge(sem("router_rows_psum"), due("dve", "router_rows_psum"))
                grows = U(6, 2).rearrange("p (e t) -> p e t", e=NEXP)
                v.tensor_copy(U(6, 2), banks(0, 4)).then_inc(sem("router_rows"), up("router_rows"))
                dve.wait_ge(sem("router_rows"), at("router_rows"))
                with dve.Fori(0, NEXP) as e:
                    enter(e)
                    ffn(FFE // STEP, True, U(6, 2)[:, bass.ds(e * T, T)])
                    leave(NEXP)
            plain_residual()
            dve.wait_ge(sem("gainrow_loaded"), due("dve", "gainrow_loaded", 16))
            for t in range(NT):
                dve.wait_ge(sem("norm_root"), due("dve", "norm_root"))
                V(v.reciprocal(stat[:, t:t + 1], stat[:, t:t + 1]))
                v.scalar_tensor_tensor(x[:, t, :], x[:, t, :], stat[:, t:t + 1], gainrow[:, :], ALU.mult, ALU.mult).then_inc(sem("result_rows"), up("result_rows"))
                dve.wait_ge(sem("result_rows"), at("result_rows"))


_INS = ['x', 'mem', 'ln_mix_pre', 'w_in', 'nsa_cmp_w', 'nsa_cmp_pe', 'rel_bias', 'ret_norm_g', 'rwkv_mu', 'rwkv_w0',
        'rwkv_w2', 'rwkv_a0', 'rwkv_a2', 'rwkv_g2', 'rwkv_k_k', 'rwkv_k_a', 'rwkv_r_k', 'rwkv_ln_g', 'rwkv_ln_b',
        'conv_w', 'w_branch', 'w_mix_out', 'ln_mix_post', 'ln_xa_pre', 'ln_mem', 'xa_wq', 'xa_wkv', 'xa_wo',
        'ln_xa_post', 'ln_mlp_pre', 'mlp_w1', 'mlp_w2', 'ln_mlp_post', 'norm_mix_2', 'norm_ffn_2', 'norm_final_2',
        'ev_w_in_2', 'ev_conv_w_2', 'ev_conv_b_2', 'ev_ga_w_2', 'ev_ga_b_2', 'ev_gx_w_2', 'ev_gx_b_2',
        'ev_lambda_2', 'ev_f_b_2', 'ev_w_out_2', 'ev_ffn_w1_2', 'ev_ffn_w3_2', 'ev_ffn_w2_2', 'od_w_in_2',
        'od_gate_w2_2', 'od_gate_b_2', 'od_head_norm_2', 'od_w_out_2', 'od_router_2', 'od_exp_w1_2',
        'od_exp_w3_2', 'od_exp_w2_2']


def kernel(**inputs):
    import numpy as _np
    import concourse.bacc as _bacc
    from concourse import mybir as _mybir
    from concourse.bass_utils import run_bass_kernel_spmd as _run

    nc = _bacc.Bacc("TRN2", target_bir_lowering=False, num_devices=1)
    arrays, args = {}, {}
    for name in _INS:
        arrays[f"in_{name}"] = _np.ascontiguousarray(inputs[name])
    for name, value in constants().items():
        arrays[f"in_{name}"] = value
    for key, value in arrays.items():
        args[key[3:]] = nc.dram_tensor(key, value.shape, _mybir.dt.from_np(value.dtype), kind="ExternalInput").ap()
    out = nc.dram_tensor("out", (1, T, D), F32, kind="ExternalOutput").ap()
    build(nc, args, out)
    r = _run(nc, [arrays], core_ids=[0])
    return r.results[0]["out"]
```

```python
import math
from contextlib import ExitStack

import numpy as np

import concourse.bass as bass
from concourse import mybir

F32 = mybir.dt.float32
U32 = mybir.dt.uint32
I32 = mybir.dt.int32
ALU = mybir.AluOpType
ACT = mybir.ActivationFunctionType
AX = mybir.AxisListType.X

P = 128
D = 1024
T = 256
NT = T // P
KD = D // P
DEPTH = 2
HD = 64
H = 4
MW = H * HD
CH = 64
NC = T // CH
HC = H * NC
UNIT = 1024

Q0, KV0, G0, RET0, RWKV0, CONV0, GATE0 = np.cumsum([0, MW, 6 * HD, 3 * H, 4 * MW, 3 * MW + 128, 3 * MW]).tolist()
CMP_LEN, CMP_STRIDE = 32, 16
NCMP = (T - CMP_LEN) // CMP_STRIDE + 1
NBUCKET = 32
NEG = -1e30
SPAN = 2 * T
FF1, FF2, FFE = 4096, 2816, 3584
NEXP = 8
SLOTS = 128
STEP = 256
LEVELS = [2, 4, 8, 16, 32]
SIDE = (0, 1, 3, 2)

C_IDENT, C_RMASK, C_LEVEL, C_M1T, C_M1, C_SEL, C_IOTA, C_TMASK, C_CAUSAL, C_COS, C_SIN, C_ONES, C_ZEROS, C_EPS, C_BEFORE, C_W = np.cumsum(
    [0, 128, 128, 128 * len(LEVELS), 128, 128, NEXP * 128, SLOTS, 1, P + T, NT * 32, NT * 32, 128, 128, 1, 128]).tolist()


def constants():
    c = np.zeros((P, C_W), np.float32)
    c[:, C_IDENT:C_IDENT + 128] = np.eye(128)
    i = np.arange(CH)
    c[:CH, C_RMASK:C_RMASK + 64] = i[:, None] < i[None, :]
    c[:CH, C_RMASK + 64:C_RMASK + 128] = i[:, None] <= i[None, :]
    i = np.arange(P)
    for n, b in enumerate([1] + LEVELS):
        low = ((i[:, None] // (2 * b) == i[None, :] // (2 * b)) & (i[:, None] // b % 2 == 1) & (i[None, :] // b % 2 == 0))
        if b == 1:
            c[:, C_M1:C_M1 + P] = -1.0 * low
            c[:, C_M1T:C_M1T + P] = -1.0 * low.T
        else:
            c[:, C_LEVEL + P * (n - 1):C_LEVEL + P * n] = low.T
    for e in range(NEXP):
        c[e, C_SEL + 128 * e:C_SEL + 128 * (e + 1)] = 1.0
    c[:, C_IOTA:C_IOTA + SLOTS] = np.arange(SLOTS)
    c[:, C_TMASK] = np.arange(P) >= CMP_LEN - 1
    t = np.arange(T)
    for n in range(NT):
        tt = t[n * P:(n + 1) * P]
        keys = (n + 1) * P
        c[:, C_CAUSAL + n * P:C_CAUSAL + n * P + keys] = np.where(tt[:, None] >= t[None, :keys], 0.0, NEG)
        freq = np.float32(10000.0) ** (-np.arange(32, dtype=np.float32) / np.float32(32))
        ang = tt.astype(np.float32)[:, None] * freq[None, :]
        c[:, C_COS + n * 32:C_COS + (n + 1) * 32] = np.cos(ang)
        c[:, C_SIN + n * 32:C_SIN + (n + 1) * 32] = np.sin(ang)
    c[:, C_ONES:C_ONES + 128] = 1.0
    c[:, C_BEFORE:C_BEFORE + P] = np.arange(P)[:, None] < np.arange(P)[None, :]
    c[:, C_EPS] = 1e-6
    decay = np.zeros((P, H, NT, T), np.float64)
    for h in range(H):
        lg = math.log(1.0 - 2.0 ** (-5.0 - h))
        for n in range(NT):
            diff = t[None, :] - t[n * P:(n + 1) * P, None]
            decay[:, h, n, :] = np.where(diff >= 0, np.exp(np.maximum(diff, 0) * lg), 0.0) * HD ** -0.5
    hot = np.zeros((NBUCKET + 1, SPAN), np.float32)
    for j in range(SPAN):
        d = T - 1 - j
        if d < 0:
            hot[NBUCKET, j] = 1.0
        elif d < NBUCKET // 2:
            hot[d, j] = 1.0
        else:
            half = NBUCKET // 2
            b = half + int(np.float32(np.log(np.float32(d) / np.float32(half))) / np.float32(math.log(128 / half)) * np.float32(half))
            hot[min(b, NBUCKET - 1), j] = 1.0
    return {"consts": c, "decay": decay.astype(np.float32).reshape(P, -1), "hot": hot}


class Signal:

    def __init__(self, nc, ctx, name):
        self.sem = ctx.enter_context(nc.semaphore(name))
        self.posted = 0
        self.taken = {}
        self.per_round = 0


class Loop:

    def __init__(self):
        self.reg = None
        self.touched = {}


def build(nc, a, out):
    ctx = ExitStack()
    signals = {}
    loop = Loop()

    def count_of(name):
        if name not in signals:
            signals[name] = Signal(nc, ctx, name)
        return signals[name]

    def sem(name):
        return count_of(name).sem

    def value(s, count):
        return count if loop.reg is None else loop.reg * s.per_round + count

    def up(name, by=1):
        s = count_of(name)
        s.posted += by
        if loop.reg is not None:
            loop.touched[(s, "")] = s.per_round
        return by

    def at(name):
        return value(count_of(name), count_of(name).posted)

    def due(who, name, by=1):
        s = count_of(name)
        s.taken[who] = s.taken.get(who, 0) + by
        if loop.reg is not None:
            loop.touched[(s, who)] = s.per_round
        return value(s, s.taken[who])

    def enter(reg):
        loop.reg = reg
        loop.touched = {}

    def leave(rounds):
        for (s, who), per in loop.touched.items():
            if who:
                s.taken[who] += per * (rounds - 1)
            else:
                s.posted += per * (rounds - 1)
        loop.reg = None

    def counts_now():
        return {n: (s.posted, dict(s.taken)) for n, s in signals.items()}

    def go_back(before):
        for n, s in signals.items():
            posted, taken = before.get(n, (0, {}))
            s.posted, s.taken = posted, dict(taken)

    def sb(name, shape, dt=F32):
        return ctx.enter_context(nc.sbuf_tensor(name, shape, dt))

    with ctx:
        x = sb("x", [P, NT, D])
        hT = sb("hT", [P, KD, T])
        fbT = sb("fbT", [P, 8 * UNIT])
        bias = fbT[:, 0:2048].rearrange("p (t h s) -> p t h s", t=NT, h=H)
        decay = fbT[:, 2048:4096].rearrange("p (h n t) -> p h n t", h=H, n=NT)
        oT = fbT[:, 4096:6144].rearrange("p (m k t) -> p m k t", m=4, k=2)
        memT = fbT[:, 6144:8192].rearrange("p (k t) -> p k t", k=KD)
        merged = sb("merged", [P, KD, T])
        gainrow = sb("gainrow", [P, D])
        slabA = sb("slabA", [P, 2, 4096])
        slabB = sb("slabB", [P, 2, 2048])
        work = sb("work", [P, 16 * UNIT])
        cst = sb("cst", [P, C_W])
        resets = sb("resets", [P, HC, CH])
        ps = ctx.enter_context(nc.psum_tensor("ps", [P, 8, 512], F32))
        stat = sb("stat", [P, 64])
        st2 = sb("st2", [P, 64])

        def U(n, units=1, off=0, size=None, parts=P):
            size = units * UNIT if size is None else size
            return work[0:parts, n * UNIT + off:n * UNIT + off + size]

        def banks(b, n=1, parts=P):
            return ps[0:parts, b:b + n, :].rearrange("p b c -> p (b c)")

        ident = cst[:, C_IDENT:C_IDENT + 128]
        ones = cst[:, C_ONES:C_ONES + 64]
        zeros = cst[:, C_ZEROS:C_ZEROS + 128]
        sel = cst[0:NEXP, C_SEL:C_SEL + NEXP * 128].rearrange("p (e m) -> p e m", e=NEXP)
        causal = [cst[:, C_CAUSAL + n * P:C_CAUSAL + n * P + (n + 1) * P] for n in range(NT)]

        gT = {n: sb(n, [P, DEPTH, KD]) for n in ("ln_mix_pre", "ln_xa_pre", "ln_mem", "ln_mlp_pre", "norm_mix_2", "norm_ffn_2")}
        peT = sb("peT", [HD, DEPTH, CMP_LEN])
        relb = sb("relb", [NBUCKET + 1, H])
        retg = sb("retg", [P, DEPTH, MW])
        muT = sb("muT", [HD, DEPTH, 15])
        vecs = {n: sb(n, [HD, DEPTH, H]) for n in ("rwkv_w0", "rwkv_a0", "rwkv_k_k", "rwkv_k_a", "rwkv_r_k")}
        lng = sb("lng", [HD, DEPTH, MW])
        lnb = sb("lnb", [HD, DEPTH, MW])
        w2s = sb("w2s", [32, DEPTH, MW])
        a2s = sb("a2s", [32, DEPTH, MW])
        g2s = sb("g2s", [HD, DEPTH, MW])
        convw = sb("convw", [P, DEPTH, 3, 2])
        convw2 = sb("convw2", [P, 4, 4])
        vec2 = {n: sb(n, [P, 4]) for n in ("ev_conv_b_2", "ev_ga_b_2", "ev_gx_b_2", "ev_lambda_2", "od_gate_b_2")}
        fb = sb("fb", [8, 1])
        gw2 = sb("gw2", [16, 512])
        routw = sb("routw", [P, KD, NEXP])

        pick = fbT[:, 0:2048].rearrange("p (e t c) -> p e t c", e=NEXP, t=NT)
        pick_gate = fbT[:, 2048:4096].rearrange("p (e t c) -> p e t c", e=NEXP, t=NT)
        spread = fbT[:, 4096:6144]
        chosen = fbT[:, 6144:6160].rearrange("p (t e) -> p t e", t=NT)
        slot = fbT[:, 6160:6176].rearrange("p (t e) -> p t e", t=NT)
        load = fbT[:, 6176:6184]
        most = fbT[0:1, 6184:6185]
        most_int = fbT[0:1, 6185:6186].bitcast(I32)
        slot_x = U(8).rearrange("p (k c) -> p k c", k=KD)
        spread_e = U(9, size=T)
        slot_y = U(10)

        toep = nc.dram_tensor("toep", (H, P, SPAN), F32, kind="Internal").ap()

        class Ring:

            def __init__(self, name, buf):
                self.name, self.buf, self.used = name, buf, f"{name}_used"
                self.loaded = self.taken = 0

            def load(self, sp, parts):
                n = self.loaded
                self.loaded += 1
                if n >= 2:
                    sp.wait_ge(sem(self.used), due("sp", self.used))
                full = f"{self.name}_full{n % 2}"
                for dst, src in parts:
                    sp.dma_start(dst(self.buf[:, n % 2, :]), src).then_inc(sem(full), up(full, 16))

            def take(self, pe, parts=1):
                n = self.taken
                self.taken += 1
                full = f"{self.name}_full{n % 2}"
                pe.wait_ge(sem(full), due("pe", full, 16 * parts))
                return self.buf[:, n % 2, :]

        ringA, ringB = Ring("slabA", slabA), Ring("slabB", slabB)

        def cols(w, c0, n, pk=True):
            src = w.rearrange("(p k) n -> p k n" if pk else "(k p) n -> p k n", p=P)[:, :, c0:c0 + n]
            return (lambda s: s[:, 0:KD * n].rearrange("p (k n) -> p k n", k=KD)), src

        def kview(slab, n):
            return slab[:, 0:KD * n].rearrange("p (k n) -> p k n", k=KD)

        for name, by in (("slabA_full0", 16 * 2 * 7), ("slabA_full1", 16 * 2 * 7), ("slabB_full0", 16 * 7), ("slabB_full1", 16 * 7),
                         ("slabA_used", 14), ("slabB_used", 14), ("hidden_psum", 28), ("hidden_act", 28),
                         ("hidden_ready", 28), ("gate_order", 28),
                         ("slot_hidden_psum", 14), ("slot_hidden_act", 14), ("slot_hidden_ready", 14), ("slot_x_psum", 1),
                         ("slot_spread", 1), ("slot_x", 1), ("slot_y_psum", 1), ("slot_y", 1)):
            count_of(name).per_round = by

        block = ctx.enter_context(nc.Block())

        @block.sync
        def _(sp):
            def linear(w, n, pk=True, first=0):
                for c0 in range(first, n, 512):
                    ringA.load(sp, [cols(w, c0, min(512, n - c0), pk)])

            def ffn_step(w1, w3, w2, c0):
                def half(i):
                    return lambda s: s[:, 2048 * i:2048 * (i + 1)].rearrange("p (k n) -> p k n", k=KD)
                srcs = [w.rearrange("(p k) n -> p k n", p=P)[:, :, c0:c0 + STEP] for w in ([w1, w3] if w3 is not None else [w1])]
                ringA.load(sp, [(half(i), s) for i, s in enumerate(srcs)])
                ringB.load(sp, [(lambda s: s.rearrange("p (j n) -> p j n", j=2),
                                 w2[c0:c0 + STEP, :].rearrange("(j p) n -> p j n", p=P))])

            sp.dma_start(x[:, :, :], a["x"].rearrange("b (n p) d -> p (b n) d", p=P)).then_inc(sem("x_loaded"), up("x_loaded", 16))
            for l in range(DEPTH):
                w = a["w_in"][l]
                ringA.load(sp, [cols(w, 0, 512)])
                ringA.load(sp, [cols(w, 512, RET0 - 512)])
                ringA.load(sp, [(lambda s: s[0:HD, :].rearrange("d (c e) -> d c e", e=HD),
                                 a["nsa_cmp_w"][l].rearrange("c l d e -> d (c l) e"))])
                for c0, c1 in ((RET0, RET0 + 512), (RET0 + 512, RWKV0), (CONV0, CONV0 + 512), (CONV0 + 512, GATE0),
                               (RWKV0, RWKV0 + 512), (RWKV0 + 512, CONV0)):
                    ringA.load(sp, [cols(w, c0, c1 - c0)])
                for m in SIDE:
                    for half in range(2):
                        ringA.load(sp, [cols(w, GATE0 + m * D + half * 512, 512)])
                        if half == 0:
                            ringB.load(sp, [(lambda s: s.rearrange("p (k n) -> p k n", k=2),
                                             a["w_branch"][l][m].rearrange("(k p) n -> p k n", p=P))])
                linear(a["w_mix_out"][l], D, False)
                linear(a["xa_wkv"][l], D)
                linear(a["xa_wq"][l], D)
                linear(a["xa_wkv"][l], 2 * D, first=D)
                linear(a["xa_wo"][l], D, False)
                for i in range(FF1 // STEP):
                    ffn_step(a["mlp_w1"][l], None, a["mlp_w2"][l], i * STEP)
            linear(a["ev_w_in_2"][0], 2568, first=2560)
            linear(a["ev_w_in_2"][0], 2560)
            linear(a["ev_w_out_2"][0], D, False)
            for i in range(FF2 // STEP):
                ffn_step(a["ev_ffn_w1_2"][0], a["ev_ffn_w3_2"][0], a["ev_ffn_w2_2"][0], i * STEP)
            linear(a["od_w_in_2"][0], 3088, first=3072)
            linear(a["od_w_in_2"][0], 3072)
            linear(a["od_w_out_2"][0], D, False)
            with sp.Fori(0, NEXP) as e:
                enter(e)
                for i in range(FFE // STEP):
                    c = slice(i * STEP, (i + 1) * STEP)
                    ringA.load(sp, [((lambda s, w=w: s[:, 2048 * w:2048 * (w + 1)].rearrange("p (k n) -> p k n", k=KD)),
                                     a[n][0].rearrange("e (p k) n -> p e k n", p=P)[:, bass.ds(e, 1), :, c].rearrange("p e k n -> p (e k) n"))
                                    for w, n in enumerate(("od_exp_w1_2", "od_exp_w3_2"))])
                    ringB.load(sp, [(lambda s: s.rearrange("p (j n) -> p j n", j=2),
                                     a["od_exp_w2_2"][0][:, c, :].rearrange("e (j p) n -> p e j n", p=P)[:, bass.ds(e, 1), :, :].rearrange("p e j n -> p (e j) n"))])
                leave(NEXP)
            sp.wait_ge(sem("result_rows"), due("sp", "result_rows", NT))
            sp.dma_start(out.rearrange("b (n p) d -> p (b n) d", p=P), x[:, :, :]).then_inc(sem("result_out"), up("result_out", 16))
            sp.wait_ge(sem("result_out"), due("sp", "result_out", 16))

        posts = ("ln_mix_post", "ln_xa_post", "ln_mlp_post")

        PROJ = 3
        proj = {"pe": 0, "act": 0, "held": 0}

        @block.gpsimd
        def _(pool):
            def small(dst, src):
                pool.dma_start(dst, src).then_inc(sem("params_loaded"), up("params_loaded", 16))

            def row(ap1, parts):
                return bass.AP(tensor=ap1.tensor, offset=ap1.offset, ap=[[0, parts], [1, ap1.shape[0]]])

            def sum_branches():
                for u in range(4 * KD):
                    m, c = u // KD, u % KD
                    gate, branch = (gainrow[:, (u % 2 * 2 + i) * T:(u % 2 * 2 + i + 1) * T] for i in range(2))
                    pool.wait_ge(sem("side_gate"), due("pool", "side_gate"))
                    if m == 0:
                        nc.gpsimd.tensor_tensor(merged[:, c, :], gate, branch, ALU.mult).then_inc(sem("side_summed"), up("side_summed"))
                        pool.wait_ge(sem("side_summed"), at("side_summed"))
                    else:
                        nc.gpsimd.tensor_tensor(gate, gate, branch, ALU.mult).then_inc(sem("side_product"), up("side_product"))
                        pool.wait_ge(sem("side_product"), at("side_product"))
                        nc.gpsimd.tensor_tensor(merged[:, c, :], merged[:, c, :], gate, ALU.add).then_inc(sem("side_summed"), up("side_summed"))
                        pool.wait_ge(sem("side_summed"), at("side_summed"))

            pool.wait_ge(sem("cleared"), due("pool", "cleared", 1))
            with nc.allow_non_contiguous_dma(reason="small parameters, once"):
                for n, t in gT.items():
                    pool.dma_start(t[:, :, :], a[n].rearrange("l (p k) -> p l k", p=P)).then_inc(sem("first_params"), up("first_params", 16))
                pool.dma_start(relb[0:NBUCKET, :], a["rel_bias"]).then_inc(sem("first_params"), up("first_params", 16))
                pool.dma_start(U(6, size=SPAN, parts=NBUCKET + 1), a["hot"]).then_inc(sem("first_params"), up("first_params", 16))
                small(fbT[:, 2048:4096], a["decay"])
                small(peT[:, :, :], a["nsa_cmp_pe"].rearrange("l n d -> d l n"))
                for l in range(DEPTH):
                    small(muT[:, l, 0:12], a["rwkv_mu"][l, 0:768].rearrange("(g p) -> p g", p=HD))
                    small(muT[0:32, l, 12:14], a["rwkv_mu"][l, 768:832].rearrange("(g p) -> p g", p=32))
                    small(muT[:, l, 14:15], a["rwkv_mu"][l, 832:896].rearrange("(g p) -> p g", p=HD))
                    small(retg[:, l, :], row(a["ret_norm_g"][l], P))
                    small(lng[:, l, :], row(a["rwkv_ln_g"][l], HD))
                    small(lnb[:, l, :], row(a["rwkv_ln_b"][l], HD))
                    small(convw[:, l, :, :], a["conv_w"][l].rearrange("j (k p) -> p j k", p=P))
                for n, t in vecs.items():
                    small(t[:, :, :], a[n].rearrange("l (h p) -> p l h", p=HD))
                small(w2s[:, :, :], a["rwkv_w2"].rearrange("l r c -> r l c"))
                small(a2s[:, :, :], a["rwkv_a2"].rearrange("l r c -> r l c"))
                small(g2s[:, :, :], a["rwkv_g2"].rearrange("l r c -> r l c"))
                small(convw2[:, :, :], a["ev_conv_w_2"][0].rearrange("j (k p) -> p j k", p=P))
                for n, t in vec2.items():
                    small(t[:, :], a[n][0].rearrange("(k p) -> p k", p=P))
                small(fb[:, :], a["ev_f_b_2"].rearrange("a h -> h a"))
                small(gw2[:, :], a["od_gate_w2_2"][0])
                small(routw[:, :, :], a["od_router_2"][0].rearrange("(p k) e -> p k e", p=P))
                pool.wait_ge(sem("bias_rows"), due("pool", "bias_rows"))
                pool.dma_start(toep.rearrange("h p j -> p h j"), U(8, 2).rearrange("p (h j) -> p h j", h=H)).then_inc(sem("bias_out"), up("bias_out", 16))
                pool.wait_ge(sem("bias_out"), due("pool", "bias_out", 16))
                for n in range(NT):
                    src = bass.AP(tensor=toep.tensor, offset=toep.offset + T - 1 - P * n,
                                  ap=[[SPAN - 1, P], [P * SPAN, H], [1, T]])
                    pool.dma_start(bias[:, n, :, :], src).then_inc(sem("bias_table"), up("bias_table", 16))
                first = True
                for l in range(DEPTH):
                    for n in posts:
                        if n == "ln_mix_post":
                            sum_branches()
                        if not first:
                            pool.wait_ge(sem("gainrow_used"), due("pool", "gainrow_used"))
                        first = False
                        pool.dma_start(gainrow[:, :], row(a[n][l], P)).then_inc(sem("gainrow_loaded"), up("gainrow_loaded", 16))
                pool.wait_ge(sem("lru_gate_cleared"), due("pool", "lru_gate_cleared"))
                gd = fbT[:, 0:1024].rearrange("p (w c n) -> p w c n", w=2, c=4)
                for w, n in enumerate(("ev_ga_w_2", "ev_gx_w_2")):
                    for half in range(2):
                        r = slice(HD * half, HD * (half + 1))
                        pool.dma_start(gd[r, w, :, r], a[n][0].rearrange("(c f) i j -> f i c j", f=2)[half]).then_inc(sem("lru_gate_loaded"), up("lru_gate_loaded", 16))
                for src in (a["od_head_norm_2"][0], a["norm_final_2"]):
                    pool.wait_ge(sem("gainrow_used"), due("pool", "gainrow_used"))
                    pool.dma_start(gainrow[:, :], row(src, P)).then_inc(sem("gainrow_loaded"), up("gainrow_loaded", 16))


        @block.tensor
        def _(pe):
            mm = nc.tensor.matmul

            def tr(o, i, n):
                return nc.tensor.transpose(o, i, ident[0:n, 0:n])

            def add_zero(o):
                return mm(o, zeros[0:1, 0:o.shape[0]], zeros[0:1, 0:1], start=False, stop=True, skip_group_check=True)

            side = {}

            def group(pieces, done=None):
                g = proj["pe"]
                proj["pe"] += 1
                if proj["held"] == PROJ:
                    pe.wait_ge(sem("proj_free"), due("pe", "proj_free"))
                else:
                    proj["held"] += 1
                for lhs, rhs, rows, c0, n in pieces:
                    for k in range(KD):
                        last = mm(ps[0:rows, g % PROJ, c0:c0 + n], lhs(k), rhs(k), start=(k == 0), stop=(k == KD - 1))
                if done is None:
                    last.then_inc(sem("proj_ready"), up("proj_ready"))
                else:
                    last.then_inc(sem(done.used), up(done.used))
                    lhs, rhs, rows, c0, n = pieces[-1]
                    add_zero(ps[0:min(rows, 32), g % PROJ, c0:c0 + 1]).then_inc(sem("proj_ready"), up("proj_ready"))

            def chT(slab, n, c0, width, dst=0):
                v = kview(slab, n)
                return (lambda k: v[:, k, c0:c0 + width]), (lambda k: hT[:, k, :]), width, dst, T

            def rowsof(slab, n, c0, width, t, dst=0, src=None):
                v, s = kview(slab, n), (hT if src is None else src)
                return (lambda k: s[:, k, t * P:(t + 1) * P]), (lambda k: v[:, k, c0:c0 + width]), P, dst, width

            def norm_T(src):
                for t in range(NT):
                    pe.wait_ge(sem("norm_rows"), due("pe", "norm_rows"))
                    for half in range(2):
                        b = 4 + 2 * t + half
                        for j in range(4):
                            k = 4 * half + j
                            last = tr(ps[:, b, j * P:(j + 1) * P], src[:, t, k::KD], P)
                        last.then_inc(sem("norm_T"), up("norm_T"))

            def take_hT():
                pe.wait_ge(sem("hT_ready"), due("pe", "hT_ready"))

            def softmax_T(n_keys):
                pe.wait_ge(sem("weights_ready"), due("pe", "weights_ready"))
                S = U(0)
                n_st = max(1, n_keys // P)
                w = min(n_keys, P)
                for h in range(4):
                    for s in range(n_st):
                        last = tr(banks(6, 2, w)[:, (h * n_st + s) * P:(h * n_st + s + 1) * P],
                                  S[:, h * n_keys + s * P:h * n_keys + s * P + w], P)
                last.then_inc(sem("weightsT_psum"), up("weightsT_psum"))
                pe.wait_ge(sem("weightsT_ready"), due("pe", "weightsT_ready"))

            def bias_and_memory():
                memrows = U(10, 2).rearrange("p (n d) -> p n d", n=NT)
                pe.wait_ge(sem("first_params"), count_of("first_params").posted)
                for h in range(H):
                    last = mm(ps[:, 4 + h, :], relb[:, h:h + 1].broadcast_to([NBUCKET + 1, P]), U(6, size=SPAN, parts=NBUCKET + 1), start=True, stop=True)
                last.then_inc(sem("bias_psum"), up("bias_psum"))
                pe.wait_ge(sem("bias_rows"), due("pe", "bias_rows"))
                norm_T(memrows)

            def nsa(l):
                qT = U(2, parts=HD).rearrange("p (h t) -> p h t", h=H)
                kT = U(3, parts=HD).rearrange("p (h t) -> p h t", h=H)
                vr = U(4, size=256).rearrange("p (t c) -> p t c", t=NT)
                take_hT()
                s = ringA.take(pe)
                for i in range(2):
                    group([chT(s, 512, Q0 + P * i, P)])
                group([chT(s, 512, KV0, P)])
                group([chT(s, 512, KV0 + P, HD)])
                group([rowsof(s, 512, KV0 + P + HD, HD, t, HD * t) for t in range(NT)], ringA)
                if l == 0:
                    bias_and_memory()
                n = RET0 - 512
                s = ringA.take(pe)
                group([chT(s, n, 0, HD)])
                group([rowsof(s, n, HD, n - HD, t, P * t) for t in range(NT)], ringA)
                cw = ringA.take(pe)[0:HD, :].rearrange("d (c l e) -> d c l e", c=2, l=CMP_LEN)
                X = U(5, parts=HD, size=2 * NCMP * CMP_LEN).rearrange("p (c n l) -> p c n l", c=2, l=CMP_LEN)
                pe.wait_ge(sem("cmp_windows"), due("pe", "cmp_windows"))
                for i in range(CMP_LEN):
                    mm(ps[0:HD, 4, 0:NCMP], cw[:, 0, i, :], X[:, 0, :, i], start=(i == 0), stop=(i == CMP_LEN - 1))
                for i in range(CMP_LEN):
                    last = mm(ps[0:NCMP, 4, 64:64 + HD], X[:, 1, :, i], cw[:, 1, i, :], start=(i == 0), stop=(i == CMP_LEN - 1))
                last.then_inc(sem("slabA_used"), up("slabA_used"))
                add_zero(ps[0:NCMP, 4, 64:65]).then_inc(sem("cmp_psum"), up("cmp_psum"))
                kcT = U(4, off=256, size=NCMP, parts=HD)
                vc = U(4, off=320, size=HD, parts=NCMP)
                pe.wait_ge(sem("cmp_ready"), due("pe", "cmp_ready"))
                mm(ps[:, 3, :], zeros[0:1, :], cst[0:1, C_SEL:C_SEL + 512], start=True, stop=False, skip_group_check=True)
                for t in range(NT):
                    for kind in range(3):
                        n = NCMP if kind == 0 else (t + 1) * P
                        for h in range(H):
                            last = mm(banks(4, 2)[:, h * n:(h + 1) * n],
                                      qT[:, h, t * P:(t + 1) * P], kcT if kind == 0 else kT[:, 1 + kind, 0:n], start=True, stop=True)
                        last.then_inc(sem("scores"), up("scores"))
                        next_inputs(3 * t + kind)
                        softmax_T(n)
                        PT = U(1)
                        for h in range(H):
                            o = ps[HD * (h % 2):HD * (h % 2 + 1), 3, (h // 2) * T + t * P:(h // 2) * T + (t + 1) * P]
                            if kind == 0:
                                last = mm(o, vc, PT[0:NCMP, h * P:(h + 1) * P], start=False, stop=False, skip_group_check=True)
                            else:
                                for s2 in range(t + 1):
                                    last = mm(o, vr[:, s2, (kind - 1) * HD:kind * HD], PT[:, ((t + 1) * h + s2) * P:((t + 1) * h + s2 + 1) * P],
                                              start=False, stop=(kind == 2 and t == 1 and s2 == 1), skip_group_check=True)
                        last.then_inc(sem("attn_out"), up("attn_out"))

            def next_inputs(i):
                if i % 2 == 0:
                    side["slab"] = ringA.take(pe)
                s = side["slab"]
                if i < 4:
                    group([rowsof(s, 512, 0, 512, i % 2)], ringA if i % 2 else None)
                elif i < 6:
                    group([chT(s, 512, 256 * (i % 2) + P * j, P, T * j) for j in range(2)], ringA if i == 5 else None)
                else:
                    group([chT(s, 256, P * j, P, T * j) for j in range(2)], ringA)

            def rwkv_inputs(i):
                if i % 4 == 0:
                    side["slab"] = ringA.take(pe)
                n = 512 if i < 4 else CONV0 - RWKV0 - 512
                group([chT(side["slab"], n, P * (i % 4), P)], ringA if i in (3, 6) else None)

            def retention():
                next_inputs(6)
                rot = U(8).rearrange("p (t c) -> p t c", t=NT)
                qkT = U(9, 2, parts=HD).rearrange("p (h t) -> p h t", h=8)
                att = U(11, 2).rearrange("p (h n t) -> p h n t", h=H, n=NT)
                vg = U(7).rearrange("p (t c) -> p t c", t=NT)
                for t in range(NT):
                    pe.wait_ge(sem("ret_rotated"), due("pe", "ret_rotated"))
                    for h in range(8):
                        last = tr(banks(4 + 2 * t, 2, HD)[:, h * P:(h + 1) * P], rot[:, t, h * HD:(h + 1) * HD], P)
                    last.then_inc(sem("ret_T_psum"), up("ret_T_psum"))
                rwkv_inputs(0)
                pe.wait_ge(sem("ret_T"), due("pe", "ret_T", 2))
                for h in range(H):
                    for s2 in range(NT):
                        last = mm(ps[:, 4 + h, s2 * T:(s2 + 1) * T], qkT[:, 4 + h, s2 * P:(s2 + 1) * P], qkT[:, h, :], start=True, stop=True)
                    last.then_inc(sem("ret_scores"), up("ret_scores"))
                pe.wait_ge(sem("ret_att"), due("pe", "ret_att", 4))
                for t in range(NT):
                    for h in range(H):
                        for s2 in range(t + 1):
                            last = mm(ps[:, 4, t * MW + h * HD:t * MW + (h + 1) * HD], att[:, h, s2, t * P:(t + 1) * P],
                                      vg[:, s2, h * HD:(h + 1) * HD], start=(s2 == 0), stop=(s2 == t))
                last.then_inc(sem("ret_out_psum"), up("ret_out_psum"))
                orow = U(13, size=512).rearrange("p (t c) -> p t c", t=NT)
                rwkv_inputs(1)
                rwkv_inputs(2)
                pe.wait_ge(sem("ret_out_rows"), due("pe", "ret_out_rows"))
                for t in range(NT):
                    for k in range(2):
                        last = tr(ps[:, 5, k * T + t * P:k * T + (t + 1) * P], orow[:, t, k * P:(k + 1) * P], P)
                last.then_inc(sem("ret_outT"), up("ret_outT"))

            def rwkv(l):
                for i in range(3, 7):
                    rwkv_inputs(i)
                lora = U(7, off=0)
                open_sides()
                side_units(4)
                pe.wait_ge(sem("rwkv_lora"), due("pe", "rwkv_lora"))
                tw, al, sg = lora[0:32, 0:256], lora[0:32, 256:512], lora[0:HD, 512:768]
                for w, src, b in ((w2s, tw, 4), (a2s, al, 6)):
                    for h in range(H):
                        last = mm(banks(b, 2, HD)[:, h * T:(h + 1) * T], w[:, l, h * HD:(h + 1) * HD], src, start=True, stop=True)
                last.then_inc(sem("rwkv_lora_psum"), up("rwkv_lora_psum"))
                side_units(1)
                pe.wait_ge(sem("rwkv_kk_sq"), due("pe", "rwkv_kk_sq"))
                pe.wait_ge(sem("rwkv_sigmoids"), due("pe", "rwkv_sigmoids"))
                for i in range(2):
                    last = mm(ps[0:HD, 4 + i, :], ones[0:HD, :], U(11, parts=HD)[:, 512 * i:512 * (i + 1)], start=True, stop=True)
                last.then_inc(sem("rwkv_kk_norm"), up("rwkv_kk_norm"))
                B, K, V, AR, rk = U(0, parts=HD), U(2, parts=HD), U(6, parts=HD), U(13, 2, parts=HD), U(12, parts=HD)
                AR = AR.rearrange("p (g c) -> p g c", g=HC)
                Bt, Kt, Vt = (U(i, parts=HD).rearrange("p (g c) -> p g c", g=HC) for i in (1, 3, 4))
                gB, gK = (U(i, 2, parts=HD).rearrange("p (g c) -> p g c", g=HC) for i in (8, 10))
                side_units(5)
                pe.wait_ge(sem("rwkv_operands"), due("pe", "rwkv_operands"))

                def ch(m, g):
                    return m[:, g * CH:(g + 1) * CH]

                def two(m, pair):
                    return m[:, pair * P:(pair + 1) * P]
                for src, b in ((B, 4), (K, 5), (V, 6)):
                    for pair in range(HC // 2):
                        last = tr(ps[:, b, pair * HD:(pair + 1) * HD], two(src, pair), HD)
                    last.then_inc(sem("rwkv_rows_psum"), up("rwkv_rows_psum"))
                for pair in range(HC // 2):
                    mm(ps[:, 7, pair:pair + 1], two(rk, pair), ones[0:HD, 0:1], start=True, stop=True)
                pe.wait_ge(sem("rwkv_rows"), due("pe", "rwkv_rows", 3))
                for c in range(NC):
                    last = mm(banks(4, 2, HD)[:, c * MW:(c + 1) * MW], sg[:, c * CH:(c + 1) * CH], g2s[:, l, :], start=True, stop=True)
                last.then_inc(sem("rwkv_gate_psum"), up("rwkv_gate_psum"))
                pe.wait_ge(sem("rwkv_gate_rows"), due("pe", "rwkv_gate_rows"))
                for lhs in (B, K):
                    for g in range(HC):
                        last = mm(banks(4, 4, HD)[:, g * 128:(g + 1) * 128], ch(lhs, g), AR[:, g, :], start=True, stop=True)
                    last.then_inc(sem("rwkv_gram_psum"), up("rwkv_gram_psum"))
                    side_units(1)
                    pe.wait_ge(sem("rwkv_gram"), due("pe", "rwkv_gram"))
                for pair in range(HC // 2):
                    mm(two(banks(4, 2), pair), two(B, pair), two(U(15, parts=HD), pair), start=True, stop=True)
                for pair in range(HC // 2):
                    last = mm(two(banks(6, 2), pair), two(U(15, parts=HD), pair), two(B, pair), start=True, stop=True)
                last.then_inc(sem("rwkv_gram_psum"), up("rwkv_gram_psum"))
                X, XT, M, Y = U(15), U(6), U(12), U(7)
                for b in LEVELS:
                    side_units(1)
                    pe.wait_ge(sem("rwkv_inv_M"), due("pe", "rwkv_inv_M"))
                    for pair in range(HC // 2):
                        last = mm(two(banks(4, 2), pair), two(M, pair), two(X, pair), start=True, stop=True)
                    last.then_inc(sem("rwkv_inv_Y_psum"), up("rwkv_inv_Y_psum"))
                    pe.wait_ge(sem("rwkv_inv_Y"), due("pe", "rwkv_inv_Y"))
                    if b != LEVELS[-1]:
                        for pair in range(HC // 2):
                            last = mm(two(banks(6, 2), pair), two(XT, pair), two(Y, pair), start=True, stop=True)
                    for pair in range(HC // 2):
                        last = mm(two(banks(4, 2), pair), two(Y, pair), two(XT, pair), start=True, stop=True)
                    last.then_inc(sem("rwkv_inv_X_psum"), up("rwkv_inv_X_psum"))
                inverse = U(12, parts=HD)
                S = U(15, off=512, size=256, parts=HD)
                Wsb, SA = U(15, off=0, size=256, parts=HD), U(15, off=256, size=256, parts=HD)
                for c in range(NC):
                    if c < 3:
                        side_units(1)
                    pe.wait_ge(sem("rwkv_state"), due("pe", "rwkv_state"))
                    mm(ps[:, 4, 0:MW], zeros[0:1, :], cst[0:1, C_SEL:C_SEL + MW], start=True, stop=False, skip_group_check=True)
                    for h in range(H):
                        g, hs = h * NC + c, slice(h * HD, (h + 1) * HD)
                        mm(ps[:, 4, hs], AR[:, g, :], S[:, hs], start=False, stop=False, skip_group_check=True)
                        last = mm(ps[:, 4, hs], gK[:, g, :], Vt[:, g, :], start=False, stop=True, skip_group_check=True)
                    last.then_inc(sem("rwkv_W_psum"), up("rwkv_W_psum"))
                    pe.wait_ge(sem("rwkv_W"), due("pe", "rwkv_W"))
                    for h in range(H):
                        g, hs = h * NC + c, slice(h * HD, (h + 1) * HD)
                        last = mm(ps[0:HD, 5, hs], ch(inverse, g), Wsb[:, hs], start=True, stop=True)
                    last.then_inc(sem("rwkv_SA_psum"), up("rwkv_SA_psum"))
                    pe.wait_ge(sem("rwkv_SA"), due("pe", "rwkv_SA"))
                    for h in range(H):
                        g, hs = h * NC + c, slice(h * HD, (h + 1) * HD)
                        mm(ps[0:HD, 7, hs], Bt[:, g, :], SA[:, hs], start=True, stop=False)
                        mm(ps[0:HD, 7, hs], Kt[:, g, :], Vt[:, g, :], start=False, stop=True)
                        last = mm(ps[HD:P, 4, hs], gB[:, g, CH:], SA[:, hs], start=False, stop=True, skip_group_check=True)
                    last.then_inc(sem("rwkv_Y_psum"), up("rwkv_Y_psum"))
                y = U(0, parts=HD).rearrange("p (c n) -> p c n", c=NC)
                side_units(4)
                pe.wait_ge(sem("rwkv_out_rows"), due("pe", "rwkv_out_rows"))
                for c in range(NC):
                    for k in range(2):
                        last = tr(ps[:, 4, k * T + c * CH:k * T + (c + 1) * CH], y[:, c, k * P:(k + 1) * P], HD)
                last.then_inc(sem("rwkv_outT"), up("rwkv_outT"))

            def rows_out(src, name="rows_psum"):
                for half in range(2):
                    s = kview(ringA.take(pe), 512)
                    for t in range(NT):
                        for k in range(KD):
                            last = mm(ps[:, 4 + 2 * t + half, :], src[:, k, t * P:(t + 1) * P], s[:, k, :], start=(k == 0), stop=(k == KD - 1))
                    last.then_inc(sem("slabA_used"), up("slabA_used"))
                add_zero(ps[0:32, 7, 0:1]).then_inc(sem(name), up(name))

            def open_sides():
                pe.wait_ge(sem("proj_free"), due("pe", "proj_free", proj["held"]))
                proj["held"] = 0
                side.update(unit=0)

            def side_units(n):
                for u in range(side["unit"], side["unit"] + n):
                    m, c, b = SIDE[u // KD], u % KD, u % PROJ
                    if c == 0:
                        ended = ("nsa_done", "ret_done", "rwkv_done", "conv_done")[m]
                        pe.wait_ge(sem(ended), due("pe", ended))
                    if c % 4 == 0:
                        side["gates"] = kview(ringA.take(pe), 512)
                    if c == 0:
                        side["branch"] = ringB.take(pe).rearrange("p (k n) -> p k n", k=2)
                    if u >= PROJ:
                        pe.wait_ge(sem("side_gate"), due("pe", "side_gate"))
                    for k in range(KD):
                        last = mm(ps[:, b, 0:T], side["gates"][:, k, c % 4 * P:(c % 4 + 1) * P], hT[:, k, :], start=(k == 0), stop=(k == KD - 1))
                    if c % 4 == 3:
                        last.then_inc(sem("slabA_used"), up("slabA_used"))
                    for k in range(2):
                        last = mm(ps[:, b, T:2 * T], side["branch"][:, k, c * P:(c + 1) * P], oT[:, m, k, :], start=(k == 0), stop=(k == 1))
                    if c < KD - 1:
                        last.then_inc(sem("side_psum"), up("side_psum"))
                    else:
                        last.then_inc(sem("slabB_used"), up("slabB_used"))
                        add_zero(ps[0:32, b, T:T + 1]).then_inc(sem("side_psum"), up("side_psum"))
                side["unit"] += n

            def merge():
                side_units(4 * KD - side["unit"])
                pe.wait_ge(sem("side_gate"), due("pe", "side_gate", PROJ))
                pe.wait_ge(sem("side_summed"), due("pe", "side_summed", 4 * KD))
                rows_out(merged)

            def cross():
                xq, xk = (U(2 + 2 * i, 2).rearrange("p (c t) -> p c t", c=KD) for i in range(2))
                xv, xo = U(6, 2).rearrange("p (n c) -> p n c", n=NT), U(8, 2).rearrange("p (c t) -> p c t", c=KD)
                pe.wait_ge(sem("mem_ready"), due("pe", "mem_ready"))
                for half in range(2):
                    s = ringA.take(pe)
                    v = kview(s, 512)
                    for i in range(2):
                        if half and i:
                            norm_T(hrows)
                        group([((lambda k, c0=256 * i + P * j: v[:, k, c0:c0 + P]), (lambda k: merged[:, k, :]), P, T * j, T) for j in range(2)], ringA if i == 1 else None)
                take_hT()
                for half in range(2):
                    s = ringA.take(pe)
                    for i in range(2):
                        group([chT(s, 512, 256 * i + P * j, P, T * j) for j in range(2)], ringA if i == 1 else None)
                pe.wait_ge(sem("cross_inputs"), due("pe", "cross_inputs"))
                def cross_scores(t):
                    for h in range(4):
                        for c in range(2):
                            last = mm(banks(0 if t else 4, 2)[:, h * T:(h + 1) * T], xq[:, 2 * h + c, t * P:(t + 1) * P], xk[:, 2 * h + c, :], start=(c == 0), stop=(c == 1))
                    last.then_inc(sem("scores"), up("scores"))
                cross_scores(0)
                for t in range(NT):
                    if t == 0:
                        for half in range(2):
                            s = ringA.take(pe)
                            for n in range(NT):
                                group([rowsof(s, 512, 0, 512, n, src=merged)], ringA if n == NT - 1 else None)
                    softmax_T(T)
                    if t == 0:
                        pe.wait_ge(sem("cross_inputs"), due("pe", "cross_inputs"))
                        cross_scores(1)
                    else:
                        pe.wait_ge(sem("cross_out"), due("pe", "cross_out"))
                    PT = U(1)
                    for c in range(KD):
                        for s2 in range(NT):
                            last = mm(banks(4, 2)[:, c * P:(c + 1) * P], xv[:, s2, c * P:(c + 1) * P], PT[:, (c // 2 * 2 + s2) * P:(c // 2 * 2 + s2 + 1) * P],
                                      start=(s2 == 0), stop=(s2 == 1))
                    last.then_inc(sem("cross_out_psum"), up("cross_out_psum"))
                pe.wait_ge(sem("cross_out"), due("pe", "cross_out"))
                rows_out(xo)

            def ffn(steps, gated):
                def up_part(i):
                    s = ringA.take(pe, 2 if gated else 1)
                    for j in range(2):
                        for w in range(2 if gated else 1):
                            v = s[:, 2048 * w:2048 * (w + 1)].rearrange("p (k n) -> p k n", k=KD)
                            for k in range(KD):
                                last = mm(ps[:, 2 * (i % 2) + j, w * T:(w + 1) * T], v[:, k, j * P:(j + 1) * P], hT[:, k, :], start=(k == 0), stop=(k == KD - 1))
                        last.then_inc(sem("hidden_psum"), up("hidden_psum"))

                def down_part(i):
                    w2 = ringB.take(pe).rearrange("p (j n) -> p j n", j=2)
                    he = U(i % 2, size=512).rearrange("p (j t) -> p j t", j=2)
                    pe.wait_ge(sem("hidden_ready"), due("pe", "hidden_ready", 2))
                    for j in range(2):
                        for t in range(NT):
                            for half in range(2):
                                last = mm(ps[:, 4 + 2 * t + half, :], he[:, j, t * P:(t + 1) * P], w2[:, j, half * 512:(half + 1) * 512],
                                          start=False, stop=False, skip_group_check=True)
                    last.then_inc(sem("slabB_used"), up("slabB_used"))
                for i in range(steps):
                    up_part(i)
                    if i:
                        down_part(i - 1)
                    add_zero(ps[0:32, 4, 0:1]).then_inc(sem("slabA_used"), up("slabA_used"))
                down_part(steps - 1)

            def seed():
                for b in range(4, 8):
                    mm(ps[:, b, :], zeros[0:1, :], cst[0:1, C_SEL:C_SEL + 512], start=True, stop=False, skip_group_check=True)

            def close(name):
                for b in range(4, 8):
                    last = mm(ps[0:32, b, 0:1], zeros[0:1, 0:32], zeros[0:1, 0:1], start=False, stop=True, skip_group_check=True)
                last.then_inc(sem(name), up(name))

            pe.wait_ge(sem("consts_loaded"), due("pe", "consts_loaded", 16))
            hrows = U(14, 2).rearrange("p (n d) -> p n d", n=NT)
            for l in range(DEPTH):
                norm_T(hrows)
                nsa(l)
                retention()
                rwkv(l)
                merge()
                cross()
                norm_T(hrows)
                take_hT()
                seed()
                ffn(FF1 // STEP, False)
                close("rows_psum")
            norm_T(hrows)

            take_hT()
            s = ringA.take(pe)
            group([chT(s, 8, 0, 8)], ringA)
            for i in range(2):
                s = ringA.take(pe)
                for half in range(2):
                    group([chT(s, 512, 256 * half + P * j, P, T * j) for j in range(2)], ringA if half == 1 else None)
            s = ringA.take(pe)
            for j in range(4):
                group([chT(s, 512, P * j, P)], ringA if j == 3 else None)
            gd = fbT[:, 0:1024].rearrange("p (w c n) -> p w c n", w=2, c=4)
            xc = U(13).rearrange("p (c t) -> p c t", c=4)
            pe.wait_ge(sem("lru_conv"), due("pe", "lru_conv"))
            pe.wait_ge(sem("lru_gate_loaded"), due("pe", "lru_gate_loaded", 64))
            for w in range(2):
                for c in range(4):
                    last = mm(banks(4 + 2 * w, 2)[:, c * T:(c + 1) * T], gd[:, w, c, :], xc[:, c, :], start=True, stop=True)
            last.then_inc(sem("lru_gate_psum"), up("lru_gate_psum"))
            s = ringA.take(pe)
            for j in range(4):
                group([chT(s, 512, P * j, P)], ringA if j == 3 else None)
            s = ringA.take(pe)
            for t in range(NT):
                group([rowsof(s, 512, 0, 512, t)], ringA if t == NT - 1 else None)
            fq, fk = (fbT[0:HD, 2048 * i:2048 * (i + 1)].rearrange("p (h t) -> p h t", h=8) for i in (1, 2))
            fv = fbT[:, 6144:7168].rearrange("p (n c) -> p n c", n=NT)
            cum, ncum = U(2, off=512, size=256, parts=8), U(2, off=768, size=256, parts=8)
            pe.wait_ge(sem("fox_cum"), due("pe", "fox_cum"))
            pe.wait_ge(sem("lru_done"), due("pe", "lru_done"))
            pe.wait_ge(sem("even_inputs"), due("pe", "even_inputs", 2))
            def fox_scores(t, hg):
                n = (t + 1) * P
                for i in range(4):
                    h = 4 * hg + i
                    o = banks(0 if hg else 4, 2)[:, i * n:(i + 1) * n]
                    mm(o, fq[:, h, t * P:(t + 1) * P], fk[:, h, 0:n], start=True, stop=False)
                    mm(o, sel[:, h, :], ncum[:, 0:n], start=False, stop=False)
                    last = mm(o, cum[:, t * P:(t + 1) * P], cst[0:8, C_SEL + 128 * h:C_SEL + 128 * (h + 1)].unsqueeze(1).broadcast_to([8, t + 1, P]), start=False, stop=True)
                last.then_inc(sem("scores"), up("scores"))
            fox_scores(0, 0)
            for t in range(NT):
                for hg in range(2):
                    if (t, hg) != (NT - 1, 1):
                        fox_scores(t + hg, 1 - hg)
                    softmax_T((t + 1) * P)
                    PT = U(1)
                    if hg == 0 and t:
                        pe.wait_ge(sem("fox_out"), due("pe", "fox_out"))
                    for i in range(4):
                        h = 4 * hg + i
                        for s2 in range(t + 1):
                            last = mm(ps[HD * (h % 2):HD * (h % 2 + 1), 3, (h // 2) * P:(h // 2 + 1) * P], fv[:, s2, h * HD:(h + 1) * HD],
                                      PT[:, ((t + 1) * i + s2) * P:((t + 1) * i + s2 + 1) * P], start=(s2 == 0), stop=(s2 == t))
                    if hg:
                        last.then_inc(sem("fox_out_psum"), up("fox_out_psum"))
            pe.wait_ge(sem("fox_out"), due("pe", "fox_out"))
            rows_out(merged, "sum_psum")
            norm_T(hrows)
            take_hT()
            seed()
            ffn(FF2 // STEP, True)
            close("sum_psum")

            norm_T(hrows)
            take_hT()

            def rows_inputs(i):
                if i % 2 == 0:
                    side["slab"] = ringA.take(pe)
                group([rowsof(side["slab"], 512, 0, 512, i % 2)], ringA if i % 2 else None)
            s = ringA.take(pe)
            group([chT(s, 16, 0, 16)], ringA)
            lrT = U(15, off=0, size=256, parts=16)
            for i in range(2):
                s = ringA.take(pe)
                for half in range(2):
                    group([chT(s, 512, 256 * half + P * j, P, T * j) for j in range(2)], ringA if half == 1 else None)
                    if i == 0 and half == 0:
                        pe.wait_ge(sem("gla_inputs"), due("pe", "gla_inputs"))
                        for h in range(H):
                            last = mm(banks(4, 2)[:, h * T:(h + 1) * T], gw2[:, h * P:(h + 1) * P], lrT, start=True, stop=True)
                        last.then_inc(sem("gla_gate_psum"), up("gla_gate_psum"))
            for i in range(4):
                rows_inputs(i)
            qd, ki, ks = (U(i).rearrange("p (g c) -> p g c", g=HC) for i in (8, 9, 10))
            ksr = U(11, 2, parts=CH).rearrange("p (g c) -> p g c", g=HC)
            sc = U(13, parts=CH).rearrange("p (g c) -> p g c", g=HC)
            vrow = U(0, 4, parts=CH).rearrange("p (c n) -> p c n", c=NC)
            state = U(14).rearrange("p (h e) -> p h e", h=H)
            pe.wait_ge(sem("gla_operands"), due("pe", "gla_operands"))
            for g in range(HC):
                last = tr(banks(4, 4, CH)[:, g * P:(g + 1) * P], ks[:, g, :], P)
            last.then_inc(sem("gla_rows_psum"), up("gla_rows_psum"))
            pe.wait_ge(sem("gla_rows"), due("pe", "gla_rows"))
            for g in range(HC):
                last = mm(banks(4, 2, CH)[:, g * CH:(g + 1) * CH], ki[:, g, :], qd[:, g, :], start=True, stop=True)
            last.then_inc(sem("gla_scores_psum"), up("gla_scores_psum"))
            pe.wait_ge(sem("gla_scores"), due("pe", "gla_scores"))
            for c in range(NC):
                if c >= 2:
                    rows_inputs(2 + c)
                pe.wait_ge(sem("gla_state"), due("pe", "gla_state"))
                for h in range(H):
                    g = h * NC + c
                    o = banks(4, 2, CH)[:, h * T:(h + 1) * T]
                    mm(o, sc[:, g, :], vrow[:, c, h * T:(h + 1) * T], start=True, stop=False)
                    mm(o, qd[:, g, :], state[:, h, :], start=False, stop=True)
                    last = mm(banks(6, 2)[:, h * T:(h + 1) * T], ksr[:, g, :], vrow[:, c, h * T:(h + 1) * T], start=True, stop=True)
                last.then_inc(sem("gla_out_psum"), up("gla_out_psum"))
            orow = fbT[0:CH, 4096:8192].rearrange("p (c n) -> p c n", c=NC)
            rows_inputs(6)
            rows_inputs(7)
            pe.wait_ge(sem("gla_out_rows"), due("pe", "gla_out_rows"))
            for k in range(KD):
                for c in range(NC):
                    last = tr(banks(4, 4)[:, k * T + c * CH:k * T + (c + 1) * CH], orow[:, c, k * P:(k + 1) * P], CH)
            last.then_inc(sem("gla_outT_psum"), up("gla_outT_psum"))
            pe.wait_ge(sem("gla_outT"), due("pe", "gla_outT"))
            rows_out(merged, "sum_psum")
            norm_T(hrows)
            take_hT()
            for t in range(NT):
                for k in range(KD):
                    last = mm(ps[:, 0, t * NEXP:(t + 1) * NEXP], hT[:, k, t * P:(t + 1) * P], routw[:, k, :], start=(k == 0), stop=(k == KD - 1))
            last.then_inc(sem("router_psum"), up("router_psum"))
            gates = U(4, size=2 * NEXP).rearrange("p (t e) -> p t e", t=NT)
            pe.wait_ge(sem("router_gates"), due("pe", "router_gates"))
            before, all_ = cst[:, C_BEFORE:C_BEFORE + P], cst[:, C_ONES:C_ONES + P]
            pe.wait_ge(sem("chosen"), due("pe", "chosen"))
            mm(ps[:, 2, 0:8], before, chosen[:, 0, :], start=True, stop=True)
            mm(ps[:, 2, 8:16], before, chosen[:, 1, :], start=True, stop=False)
            mm(ps[:, 2, 8:16], all_, chosen[:, 0, :], start=False, stop=True)
            mm(ps[:, 2, 16:24], all_, chosen[:, 0, :], start=True, stop=False)
            mm(ps[:, 2, 16:24], all_, chosen[:, 1, :], start=False, stop=True).then_inc(sem("slots_psum"), up("slots_psum"))
            seed()

            def slot_ffn(steps):
                def up_part(i):
                    s = ringA.take(pe, 2)
                    for j in range(2):
                        for w in range(2):
                            v = s[:, 2048 * w:2048 * (w + 1)].rearrange("p (k n) -> p k n", k=KD)
                            for k in range(KD):
                                last = mm(ps[:, i % 2, (2 * w + j) * P:(2 * w + j + 1) * P], v[:, k, j * P:(j + 1) * P], slot_x[:, k, :],
                                          start=(k == 0), stop=(k == KD - 1))
                    last.then_inc(sem("slot_hidden_psum"), up("slot_hidden_psum"))

                def down_part(i):
                    w2 = ringB.take(pe).rearrange("p (j n) -> p j n", j=2)
                    he = U(i % 2, size=2 * SLOTS).rearrange("p (j c) -> p j c", j=2)
                    pe.wait_ge(sem("slot_hidden_ready"), due("pe", "slot_hidden_ready"))
                    for j in range(2):
                        for half in range(2):
                            last = mm(ps[:, 2 + half, :], he[:, j, :], w2[:, j, half * 512:(half + 1) * 512],
                                      start=(i == 0 and j == 0), stop=(i == steps - 1 and j == 1))
                    last.then_inc(sem("slabB_used"), up("slabB_used"))
                for i in range(steps):
                    up_part(i)
                    if i:
                        down_part(i - 1)
                    add_zero(ps[0:32, 4, 0:1]).then_inc(sem("slabA_used"), up("slabA_used"))
                down_part(steps - 1)
                add_zero(ps[0:32, 2, 0:1]).then_inc(sem("slot_y_psum"), up("slot_y_psum"))

            pe.wait_ge(sem("most_known"), due("pe", "most_known"))
            fullest = pe.value_load(most_int, min_val=0, max_val=T)
            before_branch, slabs_before = counts_now(), (ringA.taken, ringB.taken)
            with pe.If(fullest <= SLOTS):
                pe.wait_ge(sem("picks"), due("pe", "picks", NT * NEXP + 1))
                for e in range(NEXP):
                    for t in range(NT):
                        c = e * T + t * P
                        last = tr(ps[:, c // 512, c % 512:c % 512 + P], pick_gate[:, e, t, :], P)
                last.then_inc(sem("spread_psum"), up("spread_psum"))
                pe.wait_ge(sem("spread_ready"), due("pe", "spread_ready"))

                def gather(first):
                    for k in range(KD):
                        for t in range(NT):
                            last = mm(ps[:, k // 4, k % 4 * SLOTS:(k % 4 + 1) * SLOTS], hrows[:, t, k::KD],
                                      fbT[:, bass.ds(first + t * SLOTS, SLOTS)], start=(t == 0), stop=(t == NT - 1))
                    last.then_inc(sem("slot_x_psum"), up("slot_x_psum"))

                def scatter():
                    pe.wait_ge(sem("slot_y"), due("pe", "slot_y"))
                    for t in range(NT):
                        for half in range(2):
                            mm(ps[:, 4 + 2 * t + half, :], spread_e[:, t * P:(t + 1) * P], slot_y[:, half * 512:(half + 1) * 512],
                               start=False, stop=False, skip_group_check=True)
                gather(0)
                with pe.Fori(0, NEXP - 1) as e:
                    enter(e)
                    pe.wait_ge(sem("slot_x"), due("pe", "slot_x"))
                    slot_ffn(FFE // STEP)
                    gather(e * (NT * SLOTS) + NT * SLOTS)
                    scatter()
                    leave(NEXP - 1)
                pe.wait_ge(sem("slot_x"), due("pe", "slot_x"))
                slot_ffn(FFE // STEP)
                scatter()
            go_back(before_branch)
            ringA.taken, ringB.taken = slabs_before
            with pe.Else():
                for t in range(NT):
                    last = tr(ps[0:NEXP, 1, t * P:(t + 1) * P], gates[:, t, :], P)
                last.then_inc(sem("router_T_psum"), up("router_T_psum"))
                gatesT = U(4, off=64, size=T, parts=NEXP)
                pe.wait_ge(sem("router_T"), due("pe", "router_T"))
                for e in range(NEXP):
                    last = mm(ps[:, e // 2, (e % 2) * T:(e % 2 + 1) * T], sel[:, e, :], gatesT, start=True, stop=True)
                last.then_inc(sem("router_rows_psum"), up("router_rows_psum"))
                pe.wait_ge(sem("router_rows"), due("pe", "router_rows"))
                with pe.Fori(0, NEXP) as e:
                    enter(e)
                    ffn(FFE // STEP, True)
                    leave(NEXP)
            close("sum_psum")

        @block.scalar
        def _(act):
            def A(o, i, f=ACT.Copy, **kw):
                nc.scalar.activation(o, i, f, **kw).then_inc(sem("act_order"), up("act_order"))
                act.wait_ge(sem("act_order"), at("act_order"))

            def take():
                act.wait_ge(sem("proj_ready"), due("act", "proj_ready"))
                b = proj["act"] % PROJ
                proj["act"] += 1
                return ps[:, b, :]

            def side_gates(n):
                for u in range(gated["act"], gated["act"] + n):
                    act.wait_ge(sem("side_psum"), due("act", "side_psum"))
                    if u >= 2:
                        act.wait_ge(sem("side_summed"), due("act", "side_summed"))
                    half = gainrow[:, u % 2 * 512:(u % 2 + 1) * 512]
                    A(half[:, 0:T], ps[:, u % PROJ, 0:T], ACT.Sigmoid)
                    nc.scalar.activation(half[:, T:2 * T], ps[:, u % PROJ, T:2 * T], ACT.Copy).then_inc(sem("side_gate"), up("side_gate"))
                    act.wait_ge(sem("side_gate"), at("side_gate"))
                gated["act"] += n
                if gated["act"] == 4 * KD:
                    act.wait_ge(sem("side_summed"), due("act", "side_summed", 2))
                    gated["act"] = 0

            gated = {"act": 0}

            def softmax(n, heads=4):
                act.wait_ge(sem("exp_in"), due("act", "exp_in"))
                nc.scalar.activation(U(0)[:, 0:heads * n], U(0)[:, 0:heads * n], ACT.Exp).then_inc(sem("exp_out"), up("exp_out"))
                act.wait_ge(sem("exp_out"), at("exp_out"))

            def two_heads(dst, h, p, scale=1.0, done=True):
                A(dst[:, h, :], p[0:HD, 0:T], scale=scale)
                nc.scalar.activation(dst[:, h + 1, :], p[HD:P, 0:T], ACT.Copy, scale=scale).then_inc(sem("proj_free"), up("proj_free"))
                act.wait_ge(sem("proj_free"), at("proj_free"))

            def square_rows():
                act.wait_ge(sem("rows_psum"), due("act", "rows_psum"))
                for t in range(NT):
                    A(U(12), banks(4 + 2 * t, 2), ACT.Square, accum_out=stat[:, 8 + t:9 + t])
                    nc.scalar.activation(stat[:, 8 + t:9 + t], stat[:, 8 + t:9 + t], ACT.Sqrt, scale=1.0 / D, bias=eps).then_inc(sem("rows_square"), up("rows_square"))
                    act.wait_ge(sem("rows_square"), at("rows_square"))

            def norm(src=None, col=0):
                for t in range(NT):
                    if src is None:
                        act.wait_ge(sem("norm_in"), due("act", "norm_in"))
                    rows = (x if src is None else src)[:, t, :]
                    m = stat[:, col + t:col + t + 1]
                    A(U(12), rows, ACT.Square, accum_out=m)
                    nc.scalar.activation(m, m, ACT.Sqrt, scale=1.0 / D, bias=eps).then_inc(sem("norm_root"), up("norm_root"))
                    act.wait_ge(sem("norm_root"), at("norm_root"))

            def root(o):
                act.wait_ge(sem("root_in"), due("act", "root_in"))
                nc.scalar.activation(o, o, ACT.Sqrt).then_inc(sem("root_out"), up("root_out"))
                act.wait_ge(sem("root_out"), at("root_out"))

            def ffn(steps, gated):
                for i in range(steps):
                    for j in range(2):
                        act.wait_ge(sem("hidden_psum"), due("act", "hidden_psum"))
                        b = 2 * (i % 2) + j
                        nc.scalar.activation(U(2 + b, size=T), ps[:, b, 0:T], ACT.Silu if gated else ACT.Relu).then_inc(sem("hidden_act"), up("hidden_act"))
                        act.wait_ge(sem("hidden_act"), at("hidden_act"))

            act.dma_start(cst[:, :], a["consts"]).then_inc(sem("consts_loaded"), up("consts_loaded", 16))
            mem = merged[:, :, :].rearrange("p k t -> p (k t)").rearrange("p (n d) -> p n d", n=NT)
            act.dma_start(mem, a["mem"].rearrange("b (n p) d -> p (b n) d", p=P)).then_inc(sem("mem_loaded"), up("mem_loaded", 16))
            act.wait_ge(sem("consts_loaded"), due("act", "consts_loaded", 16))
            act.wait_ge(sem("cleared"), due("act", "cleared"))
            eps = cst[:, C_EPS:C_EPS + 1]
            act.wait_ge(sem("x_loaded"), due("act", "x_loaded", 16))
            for l in range(DEPTH):
                norm(x if l == 0 else None)
                if l == 0:
                    act.wait_ge(sem("mem_loaded"), due("act", "mem_loaded", 16))
                    norm(mem, 4)
                qT = U(2, parts=HD).rearrange("p (h t) -> p h t", h=H)
                kT = U(3, parts=HD).rearrange("p (h t) -> p h t", h=H)
                vr = U(4, size=256).rearrange("p (t c) -> p t c", t=NT)
                for i in range(2):
                    two_heads(qT, 2 * i, take())
                two_heads(kT, 0, take())
                nc.scalar.activation(kT[:, 2, :], take()[0:HD, 0:T], ACT.Copy).then_inc(sem("proj_free"), up("proj_free"))
                act.wait_ge(sem("proj_free"), at("proj_free"))
                nc.scalar.activation(vr[:, :, 0:HD], take()[:, 0:2 * HD].rearrange("p (t c) -> p t c", t=NT), ACT.Copy).then_inc(sem("proj_free"), up("proj_free"))
                act.wait_ge(sem("proj_free"), at("proj_free"))
                nc.scalar.activation(kT[:, 3, :], take()[0:HD, 0:T], ACT.Copy).then_inc(sem("proj_free"), up("proj_free"))
                act.wait_ge(sem("proj_free"), at("proj_free"))
                p = take()[:, 0:2 * P].rearrange("p (t c) -> p t c", t=NT)
                A(vr[:, :, HD:P], p[:, :, 0:HD])
                nc.scalar.activation(U(4, off=512, size=24).rearrange("p (t c) -> p t c", t=NT), p[:, :, HD:HD + 12], ACT.Sigmoid).then_inc(sem("proj_free"), up("proj_free"))
                act.wait_ge(sem("proj_free"), at("proj_free"))
                nc.scalar.activation(stat[:, 60:61], stat[:, 60:61], ACT.Copy).then_inc(sem("nsa_inputs"), up("nsa_inputs"))
                act.wait_ge(sem("nsa_inputs"), at("nsa_inputs"))
                qk, vg = (U(i).rearrange("p (t c) -> p t c", t=NT) for i in (6, 7))

                def next_inputs(i):
                    p, dst = take(), qk[:, i, :] if i < 2 else U(14 + (i - 4) // 2, off=512 * (i % 2), size=512)
                    if i in (2, 3):
                        A(vg[:, i - 2, 0:MW], p[:, 0:MW])
                        nc.scalar.activation(vg[:, i - 2, MW:2 * MW], p[:, MW:2 * MW], ACT.Silu).then_inc(sem("proj_free"), up("proj_free"))
                        act.wait_ge(sem("proj_free"), at("proj_free"))
                    else:
                        nc.scalar.activation(dst, p, ACT.Copy).then_inc(sem("proj_free"), up("proj_free"))
                        act.wait_ge(sem("proj_free"), at("proj_free"))
                for t in range(NT):
                    for kind, n in enumerate((NCMP, (t + 1) * P, (t + 1) * P)):
                        softmax(n)
                        next_inputs(3 * t + kind)
                nc.scalar.activation(stat[:, 60:61], stat[:, 60:61], ACT.Copy).then_inc(sem("ret_inputs"), up("ret_inputs"))
                act.wait_ge(sem("ret_inputs"), at("ret_inputs"))
                next_inputs(6)
                nc.scalar.activation(stat[:, 60:61], stat[:, 60:61], ACT.Copy).then_inc(sem("conv_inputs"), up("conv_inputs"))
                act.wait_ge(sem("conv_inputs"), at("conv_inputs"))
                z = U(0, 4, size=15 * (T + 1), parts=HD).rearrange("p (g t) -> p g t", g=15)
                act.wait_ge(sem("rwkv_z_cleared"), due("act", "rwkv_z_cleared"))
                for i in range(6):
                    p = take()
                    A(z[:, 2 * i, 1:T + 1], p[0:HD, 0:T])
                    nc.scalar.activation(z[:, 2 * i + 1, 1:T + 1], p[HD:P, 0:T], ACT.Copy).then_inc(sem("proj_free"), up("proj_free"))
                    act.wait_ge(sem("proj_free"), at("proj_free"))
                    if i == 0:
                        root(st2[:, 48:48 + NT * H])
                p = take()
                A(z[0:32, 12, 1:T + 1], p[0:32, 0:T])
                A(z[0:32, 13, 1:T + 1], p[32:64, 0:T])
                nc.scalar.activation(z[:, 14, 1:T + 1], p[64:128, 0:T], ACT.Copy).then_inc(sem("proj_free"), up("proj_free"))
                act.wait_ge(sem("proj_free"), at("proj_free"))
                nc.scalar.activation(stat[:, 60:61], stat[:, 60:61], ACT.Copy).then_inc(sem("rwkv_inputs"), up("rwkv_inputs"))
                act.wait_ge(sem("rwkv_inputs"), at("rwkv_inputs"))
                lora = U(7, off=0)
                act.wait_ge(sem("params_loaded"), count_of("params_loaded").posted)
                act.wait_ge(sem("rwkv_mixed"), due("act", "rwkv_mixed"))
                A(lora[0:32, 0:256], lora[0:32, 0:256], ACT.Tanh)
                nc.scalar.activation(lora[0:HD, 512:768], lora[0:HD, 512:768], ACT.Sigmoid).then_inc(sem("rwkv_lora"), up("rwkv_lora"))
                act.wait_ge(sem("rwkv_lora"), at("rwkv_lora"))
                side_gates(4)
                act.wait_ge(sem("rwkv_lora_psum"), due("act", "rwkv_lora_psum"))
                for b, name, dst in ((4, "rwkv_w0", 0), (6, "rwkv_a0", 1)):
                    for h in range(H):
                        done = "rwkv_sigmoids" if dst and h == H - 1 else "act_order"
                        nc.scalar.activation(U(dst, parts=HD)[:, h * T:(h + 1) * T], banks(b, 2, HD)[:, h * T:(h + 1) * T], ACT.Sigmoid, bias=vecs[name][:, l, h:h + 1]).then_inc(sem(done), up(done))
                        act.wait_ge(sem(done), at(done))
                side_gates(1)
                act.wait_ge(sem("rwkv_cumulated"), due("act", "rwkv_cumulated"))
                A(U(8, parts=HD), U(2, parts=HD), ACT.Exp)
                A(U(9, parts=HD), U(2, parts=HD), ACT.Exp, scale=-1.0)
                nc.scalar.activation(U(3, parts=HD), U(3, parts=HD), ACT.Exp).then_inc(sem("rwkv_decays"), up("rwkv_decays"))
                act.wait_ge(sem("rwkv_decays"), at("rwkv_decays"))
                root(U(11, parts=HD))
                side_gates(15)
                root(st2[0:HD, 48:48 + HC])
                side_gates(4)
                side_gates(KD)
                square_rows()
                norm()
                xq, xk = (U(2 + 2 * i, 2).rearrange("p (c t) -> p c t", c=KD) for i in range(2))
                xv, xo = U(6, 2).rearrange("p (n c) -> p n c", n=NT), U(8, 2).rearrange("p (c t) -> p c t", c=KD)
                for dst in (xk, xq):
                    for i in range(4):
                        nc.scalar.activation(dst[:, 2 * i:2 * i + 2, :].rearrange("p c t -> p (c t)"), take(), ACT.Copy).then_inc(sem("proj_free"), up("proj_free"))
                        act.wait_ge(sem("proj_free"), at("proj_free"))
                nc.scalar.activation(stat[:, 60:61], stat[:, 60:61], ACT.Copy).then_inc(sem("cross_inputs"), up("cross_inputs"))
                act.wait_ge(sem("cross_inputs"), at("cross_inputs"))
                for t in range(NT):
                    softmax(T)
                    if t == 0:
                        for half in range(2):
                            for n in range(NT):
                                nc.scalar.activation(xv[:, n, 512 * half:512 * (half + 1)], take(), ACT.Copy).then_inc(sem("proj_free"), up("proj_free"))
                                act.wait_ge(sem("proj_free"), at("proj_free"))
                        nc.scalar.activation(stat[:, 60:61], stat[:, 60:61], ACT.Copy).then_inc(sem("cross_inputs"), up("cross_inputs"))
                        act.wait_ge(sem("cross_inputs"), at("cross_inputs"))
                    act.wait_ge(sem("cross_out_psum"), due("act", "cross_out_psum"))
                    nc.scalar.activation(xo[:, :, t * P:(t + 1) * P], banks(4, 2).rearrange("p (c t) -> p c t", c=KD), ACT.Copy).then_inc(sem("cross_out"), up("cross_out"))
                    act.wait_ge(sem("cross_out"), at("cross_out"))
                square_rows()
                norm()
                ffn(FF1 // STEP, False)
                square_rows()
            xr = U(8, 2, size=4 * (T + 3)).rearrange("p (c t) -> p c t", c=4)
            yr = U(10).rearrange("p (c t) -> p c t", c=4)
            fq, fk = (fbT[0:HD, 2048 * i:2048 * (i + 1)].rearrange("p (h t) -> p h t", h=8) for i in (1, 2))
            fv = fbT[:, 6144:7168].rearrange("p (n c) -> p n c", n=NT)
            norm()
            nc.scalar.activation(U(2, off=0, size=256, parts=8), take()[0:8, 0:T], ACT.Identity, bias=fb[:, 0:1]).then_inc(sem("proj_free"), up("proj_free"))
            act.wait_ge(sem("proj_free"), at("proj_free"))
            act.wait_ge(sem("lru_pad"), due("act", "lru_pad"))
            for i in range(2):
                nc.scalar.activation(xr[:, 2 * i:2 * i + 2, 3:T + 3], take().rearrange("p (c t) -> p c t", c=2), ACT.Copy).then_inc(sem("proj_free"), up("proj_free"))
                act.wait_ge(sem("proj_free"), at("proj_free"))
            for i in range(2):
                nc.scalar.activation(yr[:, 2 * i:2 * i + 2, :].rearrange("p c t -> p (c t)"), take(), ACT.Copy).then_inc(sem("proj_free"), up("proj_free"))
                act.wait_ge(sem("proj_free"), at("proj_free"))
            nc.scalar.activation(stat[:, 60:61], stat[:, 60:61], ACT.Copy).then_inc(sem("even_inputs"), up("even_inputs"))
            act.wait_ge(sem("even_inputs"), at("even_inputs"))
            lam, lru = vec2["ev_lambda_2"], (U(4), U(5))
            A(stat[:, 32:36], lam[:, :], ACT.Abs)
            nc.scalar.activation(stat[:, 36:40], stat[:, 32:36], ACT.Exp, scale=-1.0).then_inc(sem("lru_exp"), up("lru_exp"))
            act.wait_ge(sem("lru_exp"), at("lru_exp"))
            for i in range(2):
                two_heads(fq, 2 * i, take(), HD ** -0.5)
            act.wait_ge(sem("fox_exp_in"), due("act", "fox_exp_in"))
            A(U(2, off=768, size=256, parts=8), U(2, off=512, size=256, parts=8), ACT.Exp, scale=-1.0)
            nc.scalar.activation(U(2, off=768, size=256, parts=8), U(2, off=768, size=256, parts=8), ACT.Ln, bias=1.0).then_inc(sem("fox_ln"), up("fox_ln"))
            act.wait_ge(sem("fox_ln"), at("fox_ln"))
            for i in range(2, 4):
                two_heads(fq, 2 * i, take(), HD ** -0.5)
            act.wait_ge(sem("lru_gate_psum"), due("act", "lru_gate_psum"))
            for w, n in enumerate(("ev_ga_b_2", "ev_gx_b_2")):
                for c in range(4):
                    done = "lru_sigmoids" if w and c == 3 else "act_order"
                    nc.scalar.activation(lru[w][:, c * T:(c + 1) * T], banks(4 + 2 * w, 2)[:, c * T:(c + 1) * T], ACT.Sigmoid, bias=vec2[n][:, c:c + 1]).then_inc(sem(done), up(done))
                    act.wait_ge(sem(done), at(done))
            two_heads(fk, 0, take())
            act.wait_ge(sem("lru_log_a"), due("act", "lru_log_a"))
            A(U(6), U(4), ACT.Exp, scale=-1.0)
            nc.scalar.activation(U(7), U(4), ACT.Tanh).then_inc(sem("lru_a"), up("lru_a"))
            act.wait_ge(sem("lru_a"), at("lru_a"))
            two_heads(fk, 2, take())
            act.wait_ge(sem("gelu_in"), due("act", "gelu_in"))
            nc.scalar.activation(U(11), U(11), ACT.Tanh).then_inc(sem("gelu_tanh"), up("gelu_tanh"))
            act.wait_ge(sem("gelu_tanh"), at("gelu_tanh"))
            root(U(7))
            for i in range(2, 4):
                two_heads(fk, 2 * i, take())
            for t in range(NT):
                nc.scalar.activation(fv[:, t, :], take(), ACT.Copy).then_inc(sem("proj_free"), up("proj_free"))
                act.wait_ge(sem("proj_free"), at("proj_free"))
            nc.scalar.activation(stat[:, 60:61], stat[:, 60:61], ACT.Copy).then_inc(sem("even_inputs"), up("even_inputs"))
            act.wait_ge(sem("even_inputs"), at("even_inputs"))
            for t in range(NT):
                for hg in range(2):
                    softmax((t + 1) * P)
                act.wait_ge(sem("fox_out_psum"), due("act", "fox_out_psum"))
                nc.scalar.activation(merged[:, 4:8, t * P:(t + 1) * P], ps[:, 3, :].rearrange("p (c t) -> p c t", c=4), ACT.Copy).then_inc(sem("fox_out"), up("fox_out"))
                act.wait_ge(sem("fox_out"), at("fox_out"))
            norm()
            ffn(FF2 // STEP, True)
            norm()
            q, k = (U(i).rearrange("p (c t) -> p c t", c=H) for i in (8, 9))
            vrow = U(0, 4, parts=CH).rearrange("p (c n) -> p c n", c=NC)
            grow = fbT[0:CH, 0:4096].rearrange("p (c n) -> p c n", c=NC)
            nc.scalar.activation(U(15, off=0, size=256, parts=16), take()[0:16, 0:T], ACT.Copy).then_inc(sem("proj_free"), up("proj_free"))
            act.wait_ge(sem("proj_free"), at("proj_free"))
            nc.scalar.activation(stat[:, 60:61], stat[:, 60:61], ACT.Copy).then_inc(sem("gla_inputs"), up("gla_inputs"))
            act.wait_ge(sem("gla_inputs"), at("gla_inputs"))

            def columns_in(dst, i, sc):
                nc.scalar.activation(dst[:, 2 * i:2 * i + 2, :].rearrange("p c t -> p (c t)"), take(), ACT.Copy, scale=sc).then_inc(sem("proj_free"), up("proj_free"))
                act.wait_ge(sem("proj_free"), at("proj_free"))

            def rows_in(dst, i, f):
                half, t, p = i // 2, i % 2, take()
                A(dst[:, 2 * t, 512 * half:512 * (half + 1)], p[0:CH, :], f)
                nc.scalar.activation(dst[:, 2 * t + 1, 512 * half:512 * (half + 1)], p[CH:P, :], f).then_inc(sem("proj_free"), up("proj_free"))
                act.wait_ge(sem("proj_free"), at("proj_free"))
            columns_in(q, 0, P ** -0.5)
            act.wait_ge(sem("gla_exp_in"), due("act", "gla_exp_in"))
            A(U(6), U(5), ACT.Exp, scale=-1.0)
            nc.scalar.activation(U(6), U(6), ACT.Ln, bias=1.0).then_inc(sem("gla_ln"), up("gla_ln"))
            act.wait_ge(sem("gla_ln"), at("gla_ln"))
            columns_in(q, 1, P ** -0.5)
            columns_in(k, 0, 1.0)
            columns_in(k, 1, 1.0)
            act.wait_ge(sem("gla_cum"), due("act", "gla_cum"))
            A(U(5), U(4), ACT.Exp)
            A(U(6), U(4), ACT.Exp, scale=-1.0)
            nc.scalar.activation(U(7), U(7), ACT.Exp).then_inc(sem("gla_exps"), up("gla_exps"))
            act.wait_ge(sem("gla_exps"), at("gla_exps"))
            for i in range(4):
                rows_in(vrow, i, ACT.Copy)
            nc.scalar.activation(st2[:, 0:HC], st2[:, 0:HC], ACT.Exp).then_inc(sem("gla_decay"), up("gla_decay"))
            act.wait_ge(sem("gla_decay"), at("gla_decay"))
            rows_in(grow, 0, ACT.Silu)
            rows_in(grow, 1, ACT.Silu)
            root(st2[0:CH, 16:32])
            rows_in(grow, 2, ACT.Silu)
            rows_in(grow, 3, ACT.Silu)
            nc.scalar.activation(stat[:, 60:61], stat[:, 60:61], ACT.Copy).then_inc(sem("gla_inputs"), up("gla_inputs"))
            act.wait_ge(sem("gla_inputs"), at("gla_inputs"))
            norm()
            act.wait_ge(sem("router_diff"), due("act", "router_diff"))
            nc.scalar.activation(stat[:, 40:42], stat[:, 42:44], ACT.Exp).then_inc(sem("router_exp"), up("router_exp"))
            act.wait_ge(sem("router_exp"), at("router_exp"))
            act.wait_ge(sem("most_known"), due("act", "most_known"))
            fullest = act.value_load(most_int, min_val=0, max_val=T)
            before_branch = counts_now()
            with act.If(fullest <= SLOTS):
                with act.Fori(0, NEXP) as e:
                    enter(e)
                    for i in range(FFE // STEP):
                        act.wait_ge(sem("slot_hidden_psum"), due("act", "slot_hidden_psum"))
                        nc.scalar.activation(U(2 + i % 2, size=2 * SLOTS), ps[:, i % 2, 0:2 * SLOTS], ACT.Silu).then_inc(sem("slot_hidden_act"), up("slot_hidden_act"))
                        act.wait_ge(sem("slot_hidden_act"), at("slot_hidden_act"))
                    leave(NEXP)
            go_back(before_branch)
            with act.Else():
                with act.Fori(0, NEXP) as e:
                    enter(e)
                    ffn(FFE // STEP, True)
                    leave(NEXP)
            norm()

        @block.vector
        def _(dve):
            v = nc.vector

            def V(ins):
                ins.then_inc(sem("dve_order"), up("dve_order"))
                dve.wait_ge(sem("dve_order"), at("dve_order"))

            def mul(o, i0, i1):
                V(v.tensor_tensor(o, i0, i1, ALU.mult))

            def add(o, i0, i1):
                V(v.tensor_tensor(o, i0, i1, ALU.add))

            def sub(o, i0, i1):
                V(v.tensor_tensor(o, i0, i1, ALU.subtract))

            def ts(o, i, s1, s2, op0, op1=None):
                V(v.tensor_scalar(o, i, s1, s2, op0, op1) if op1 is not None else v.tensor_scalar(o, i, s1, None, op0))

            def stt(o, i0, sc, i1, op0, op1):
                V(v.scalar_tensor_tensor(o, i0, sc, i1, op0, op1))

            def copy(o, i):
                V(v.tensor_copy(o, i))

            def red(o, i, op):
                V(v.tensor_reduce(o, i, AX, op))

            def inv_root(o, ss, n, eps):
                v.tensor_scalar(o, ss, 1.0 / n, eps, ALU.mult, ALU.add).then_inc(sem("root_in"), up("root_in"))
                dve.wait_ge(sem("root_in"), at("root_in"))
                dve.wait_ge(sem("root_out"), due("dve", "root_out"))
                V(v.reciprocal(o, o))

            hrows = U(14, 2).rearrange("p (n d) -> p n d", n=NT)

            def norm(src, rows, gain, dst, col=0):
                for t in range(NT):
                    dve.wait_ge(sem("norm_root"), due("dve", "norm_root"))
                    m = stat[:, col + t:col + t + 1]
                    V(v.reciprocal(m, m))
                    v.tensor_scalar(rows[:, t, :], src[:, t, :], m, None, ALU.mult).then_inc(sem("norm_rows"), up("norm_rows"))
                    dve.wait_ge(sem("norm_rows"), at("norm_rows"))
                for t in range(NT):
                    for half in range(2):
                        dve.wait_ge(sem("norm_T"), due("dve", "norm_T"))
                        p = ps[:, 4 + 2 * t + half, :].rearrange("p (k t) -> p k t", k=4)
                        d = dst[:, 4 * half:4 * half + 4, t * P:(t + 1) * P]
                        if gain is None:
                            copy(d, p)
                        else:
                            done = "hT_ready" if t == 1 and half == 1 else "dve_order"
                            v.tensor_tensor(d, p, gain[:, 4 * half:4 * half + 4].unsqueeze(2).broadcast_to([P, 4, P]), ALU.mult).then_inc(sem(done), up(done))
                            dve.wait_ge(sem(done), at(done))

            def residual():
                dve.wait_ge(sem("gainrow_loaded"), due("dve", "gainrow_loaded", 16))
                for t in range(NT):
                    dve.wait_ge(sem("rows_square"), due("dve", "rows_square"))
                    V(v.reciprocal(stat[:, 8 + t:9 + t], stat[:, 8 + t:9 + t]))
                    done = "gainrow_used" if t else "dve_order"
                    v.scalar_tensor_tensor(U(13), banks(4 + 2 * t, 2), stat[:, 8 + t:9 + t], gainrow[:, :], ALU.mult, ALU.mult).then_inc(sem(done), up(done))
                    dve.wait_ge(sem(done), at(done))
                    v.tensor_tensor(x[:, t, :], x[:, t, :], U(13), ALU.add).then_inc(sem("norm_in"), up("norm_in"))
                    dve.wait_ge(sem("norm_in"), at("norm_in"))

            def plain_residual():
                dve.wait_ge(sem("sum_psum"), due("dve", "sum_psum"))
                for t in range(NT):
                    v.tensor_tensor(x[:, t, :], x[:, t, :], banks(4 + 2 * t, 2), ALU.add).then_inc(sem("norm_in"), up("norm_in"))
                    dve.wait_ge(sem("norm_in"), at("norm_in"))

            def softmax(n, scale, table, factor=None, b=4):
                S3 = U(0)[:, 0:4 * n].rearrange("p (h s) -> p h s", h=4)
                p = banks(b, 2)[:, 0:4 * n].rearrange("p (h s) -> p h s", h=4)
                dve.wait_ge(sem("scores"), due("dve", "scores"))
                if table is None:
                    ts(S3, p, scale, None, ALU.mult)
                else:
                    stt(S3, p, scale, table, ALU.mult, ALU.add)
                red(stat[:, 16:20], S3, ALU.max)
                v.tensor_tensor(S3, S3, stat[:, 16:20].unsqueeze(2).broadcast_to([P, 4, n]), ALU.subtract).then_inc(sem("exp_in"), up("exp_in"))
                dve.wait_ge(sem("exp_in"), at("exp_in"))
                dve.wait_ge(sem("exp_out"), due("dve", "exp_out"))
                red(stat[:, 20:24], S3, ALU.add)
                V(v.reciprocal(stat[:, 24:28], stat[:, 20:24]))
                if factor is not None:
                    factor()
                v.tensor_tensor(S3, S3, stat[:, 24:28].unsqueeze(2).broadcast_to([P, 4, n]), ALU.mult).then_inc(sem("weights_ready"), up("weights_ready"))
                dve.wait_ge(sem("weights_ready"), at("weights_ready"))
                dve.wait_ge(sem("weightsT_psum"), due("dve", "weightsT_psum"))
                w = min(n, P)
                cols_ = 4 * P * max(1, n // P)
                v.tensor_copy(U(1)[0:w, 0:cols_], banks(6, 2, w)[:, 0:cols_]).then_inc(sem("weightsT_ready"), up("weightsT_ready"))
                dve.wait_ge(sem("weightsT_ready"), at("weightsT_ready"))

            def ffn(steps, gated, gate=None):
                for i in range(steps):
                    for j in range(2):
                        b = 2 * (i % 2) + j
                        he, a1 = U(i % 2, off=j * T, size=T), U(2 + b, size=T)
                        dve.wait_ge(sem("hidden_act"), due("dve", "hidden_act"))
                        if not gated:
                            v.tensor_tensor(he, a1, a1, ALU.mult).then_inc(sem("hidden_ready"), up("hidden_ready"))
                            dve.wait_ge(sem("hidden_ready"), at("hidden_ready"))
                        elif gate is None:
                            v.tensor_tensor(he, a1, ps[:, b, T:2 * T], ALU.mult).then_inc(sem("hidden_ready"), up("hidden_ready"))
                            dve.wait_ge(sem("hidden_ready"), at("hidden_ready"))
                        else:
                            v.tensor_tensor(a1, a1, gate, ALU.mult).then_inc(sem("gate_order"), up("gate_order"))
                            dve.wait_ge(sem("gate_order"), at("gate_order"))
                            v.tensor_tensor(he, a1, ps[:, b, T:2 * T], ALU.mult).then_inc(sem("hidden_ready"), up("hidden_ready"))
                            dve.wait_ge(sem("hidden_ready"), at("hidden_ready"))

            V(v.memset(relb[NBUCKET:NBUCKET + 1, :], NEG))
            V(v.memset(muT[:, :, :], 0.0))
            V(v.memset(stat[:, :], 0.0))
            V(v.memset(resets[:, :, :], 1.0))
            v.memset(resets[:, :, 0:1], 0.0).then_inc(sem("cleared"), up("cleared"))
            dve.wait_ge(sem("cleared"), at("cleared"))
            dve.wait_ge(sem("consts_loaded"), due("dve", "consts_loaded", 16))
            dve.wait_ge(sem("first_params"), count_of("first_params").posted)
            dve.wait_ge(sem("x_loaded"), due("dve", "x_loaded", 16))
            for l in range(DEPTH):
                norm(x, hrows, gT["ln_mix_pre"][:, l, :], hT)
                if l == 0:
                    dve.wait_ge(sem("bias_psum"), due("dve", "bias_psum"))
                    v.tensor_copy(U(8, 2), banks(4, 4)).then_inc(sem("bias_rows"), up("bias_rows"))
                    dve.wait_ge(sem("bias_rows"), at("bias_rows"))
                    mem = merged[:, :, :].rearrange("p k t -> p (k t)").rearrange("p (n d) -> p n d", n=NT)
                    norm(mem, U(10, 2).rearrange("p (n d) -> p n d", n=NT), None, memT, 4)
                    dve.wait_ge(sem("params_loaded"), count_of("params_loaded").posted)
                kT = U(3, parts=HD).rearrange("p (h t) -> p h t", h=H)
                X = U(5, parts=HD, size=2 * NCMP * CMP_LEN).rearrange("p (c n l) -> p c n l", c=2, l=CMP_LEN)
                dve.wait_ge(sem("nsa_inputs"), due("dve", "nsa_inputs"))
                for c in range(2):
                    win = kT[:, c, :].rearrange("p (n l) -> p n l", l=CMP_STRIDE)
                    for half in range(2):
                        r = slice(half * CMP_STRIDE, (half + 1) * CMP_STRIDE)
                        done = "cmp_windows" if c and half else "dve_order"
                        v.tensor_tensor(X[:, c, :, r], win[:, half:half + NCMP, :], peT[:, l, r].unsqueeze(1).broadcast_to([HD, NCMP, CMP_STRIDE]), ALU.add).then_inc(sem(done), up(done))
                        dve.wait_ge(sem(done), at(done))
                dve.wait_ge(sem("cmp_psum"), due("dve", "cmp_psum"))
                copy(U(4, off=256, size=NCMP, parts=HD), ps[0:HD, 4, 0:NCMP])
                v.tensor_copy(U(4, off=320, size=HD, parts=NCMP), ps[0:NCMP, 4, 64:64 + HD]).then_inc(sem("cmp_ready"), up("cmp_ready"))
                dve.wait_ge(sem("cmp_ready"), at("cmp_ready"))
                if l == 0:
                    dve.wait_ge(sem("bias_table"), due("dve", "bias_table", 32))
                g3 = U(4, off=512, size=24).rearrange("p (t h b) -> p t h b", t=NT, h=H)
                for t in range(NT):
                    for kind, n in enumerate((NCMP, (t + 1) * P, (t + 1) * P)):
                        def gate():
                            mul(stat[:, 24:28], stat[:, 24:28], g3[:, t, :, kind])
                            if kind == 0 and t == 0:
                                ts(stat[:, 24:28], stat[:, 24:28], cst[:, C_TMASK:C_TMASK + 1], None, ALU.mult)
                        softmax(n, HD ** -0.5, bias[:, t, :, CMP_LEN - 1::CMP_STRIDE] if kind == 0 else bias[:, t, :, 0:n], gate)
                        dve.wait_ge(sem("attn_out"), due("dve", "attn_out"))
                v.tensor_copy(oT[:, 0, :, :], ps[:, 3, :].rearrange("p (k t) -> p k t", k=2)).then_inc(sem("nsa_done"), up("nsa_done"))
                dve.wait_ge(sem("nsa_done"), at("nsa_done"))
                z = U(0, 4, size=15 * (T + 1), parts=HD).rearrange("p (g t) -> p g t", g=15)
                V(v.memset(z[:, :, 0:1], 0.0))
                v.memset(z[:, 12:14, :], 0.0).then_inc(sem("rwkv_z_cleared"), up("rwkv_z_cleared"))
                dve.wait_ge(sem("rwkv_z_cleared"), at("rwkv_z_cleared"))
                qk, vg, rot = (U(i).rearrange("p (t c) -> p t c", t=NT) for i in (6, 7, 8))
                qkT = U(9, 2, parts=HD).rearrange("p (h t) -> p h t", h=8)
                att = U(11, 2).rearrange("p (h n t) -> p h n t", h=H, n=NT)
                dve.wait_ge(sem("ret_inputs"), due("dve", "ret_inputs"))
                for t in range(NT):
                    u = qk[:, t, :].rearrange("p (h f d) -> p h f d", h=8, f=2)
                    r = rot[:, t, :].rearrange("p (h f d) -> p h f d", h=8, f=2)
                    tmp = U(13, size=512).rearrange("p (f h d) -> p f h d", f=2, h=8)
                    cos, sin = (cst[:, c + 32 * t:c + 32 * (t + 1)].unsqueeze(1).broadcast_to([P, 8, 32]) for c in (C_COS, C_SIN))
                    for f, comb in ((0, ALU.subtract), (1, ALU.add)):
                        mul(tmp[:, 0], u[:, :, f, :], cos)
                        mul(tmp[:, 1], u[:, :, 1 - f, :], sin)
                        done = "ret_rotated" if f else "dve_order"
                        v.tensor_tensor(r[:, :, f, :], tmp[:, 0], tmp[:, 1], comb).then_inc(sem(done), up(done))
                        dve.wait_ge(sem(done), at(done))
                for t in range(NT):
                    dve.wait_ge(sem("ret_T_psum"), due("dve", "ret_T_psum"))
                    v.tensor_copy(qkT[:, :, t * P:(t + 1) * P], banks(4 + 2 * t, 2, HD).rearrange("p (h t) -> p h t", h=8)).then_inc(sem("ret_T"), up("ret_T"))
                    dve.wait_ge(sem("ret_T"), at("ret_T"))
                for h in range(H):
                    dve.wait_ge(sem("ret_scores"), due("dve", "ret_scores"))
                    v.tensor_tensor(att[:, h, :, :], ps[:, 4 + h, :].rearrange("p (n t) -> p n t", n=NT), decay[:, h, :, :], ALU.mult).then_inc(sem("ret_att"), up("ret_att"))
                    dve.wait_ge(sem("ret_att"), at("ret_att"))
                dve.wait_ge(sem("ret_out_psum"), due("dve", "ret_out_psum"))

                def head_norm(o3, src, n, eps, parts, tmp3):
                    m, q = st2[0:parts, 32:32 + n], st2[0:parts, 48:48 + n]
                    red(m, src, ALU.add)
                    ts(m, m, 1.0 / HD, None, ALU.mult)
                    sub(o3, src, m.unsqueeze(2).broadcast_to([parts, n, HD]))
                    mul(tmp3, o3, o3)
                    red(q, tmp3, ALU.add)
                    inv_root(q, q, HD, eps)
                    mul(o3, o3, q.unsqueeze(2).broadcast_to([parts, n, HD]))
                orow = U(13, size=512)
                head_norm(orow.rearrange("p (g d) -> p g d", d=HD), ps[:, 4, :].rearrange("p (g d) -> p g d", d=HD), NT * H, 1e-5, P,
                          U(13, off=512, size=512).rearrange("p (g d) -> p g d", d=HD))
                o3 = orow.rearrange("p (t c) -> p t c", t=NT)
                mul(o3, o3, retg[:, l, :].unsqueeze(1).broadcast_to([P, NT, MW]))
                v.tensor_tensor(o3, o3, vg[:, :, MW:2 * MW], ALU.mult).then_inc(sem("ret_out_rows"), up("ret_out_rows"))
                dve.wait_ge(sem("ret_out_rows"), at("ret_out_rows"))
                dve.wait_ge(sem("ret_outT"), due("dve", "ret_outT"))
                v.tensor_copy(oT[:, 1, :, :], ps[:, 5, :].rearrange("p (k t) -> p k t", k=2)).then_inc(sem("ret_done"), up("ret_done"))
                dve.wait_ge(sem("ret_done"), at("ret_done"))
                cb, cc, cx = (U(14 + i // 2, off=512 * (i % 2), size=512).rearrange("p (k t) -> p k t", k=2) for i in range(3))
                cu = U(12, size=2 * (T + 2)).rearrange("p (k t) -> p k t", k=2)
                cy = U(15, off=512, size=512).rearrange("p (k t) -> p k t", k=2)
                dve.wait_ge(sem("conv_inputs"), due("dve", "conv_inputs"))
                V(v.memset(cu[:, :, 0:2], 0.0))
                mul(cu[:, :, 2:T + 2], cc, cx)
                for k in range(2):
                    ts(cy[:, k, :], cu[:, k, 0:T], convw[:, l, 0, k:k + 1], None, ALU.mult)
                    for j in (1, 2):
                        stt(cy[:, k, :], cu[:, k, j:j + T], convw[:, l, j, k:k + 1], cy[:, k, :], ALU.mult, ALU.add)
                v.tensor_tensor(oT[:, 3, :, :], cb, cy, ALU.mult).then_inc(sem("conv_done"), up("conv_done"))
                dve.wait_ge(sem("conv_done"), at("conv_done"))
                dve.wait_ge(sem("rwkv_inputs"), due("dve", "rwkv_inputs"))
                mix = U(4, 4, size=15 * T, parts=HD).rearrange("p (g t) -> p g t", g=15)
                sub(mix, z[:, :, 0:T], z[:, :, 1:T + 1])
                mul(mix, mix, muT[:, l, :].unsqueeze(2).broadcast_to([HD, 15, T]))
                v.tensor_tensor(mix, mix, z[:, :, 1:T + 1], ALU.add).then_inc(sem("rwkv_mixed"), up("rwkv_mixed"))
                dve.wait_ge(sem("rwkv_mixed"), at("rwkv_mixed"))
                u4 = lambda i: U(i, parts=HD).rearrange("p (h t) -> p h t", h=H)
                u16 = lambda i: U(i, parts=HD).rearrange("p (g t) -> p g t", g=HC)
                vb = lambda name: vecs[name][:, l, :].unsqueeze(2).broadcast_to([HD, H, T])
                r, k, vv = u4(4), u4(5), u4(6)
                kk, sq, kn = u4(10), u4(11), u4(12)
                mul(kk, k, vb("rwkv_k_k"))
                v.tensor_tensor(sq, kk, kk, ALU.mult).then_inc(sem("rwkv_kk_sq"), up("rwkv_kk_sq"))
                dve.wait_ge(sem("rwkv_kk_sq"), at("rwkv_kk_sq"))
                dve.wait_ge(sem("rwkv_sigmoids"), due("dve", "rwkv_sigmoids"))
                lw, cs = u4(0), u4(2)
                ts(lw, lw, -math.exp(-0.5), None, ALU.mult)
                V(v.tensor_tensor_scan(U(2, parts=HD), resets[0:HD, :, :].rearrange("p g t -> p (g t)"), U(0, parts=HD), 0.0, ALU.mult, ALU.add))
                v.tensor_tensor(u4(3), cs, lw, ALU.subtract).then_inc(sem("rwkv_cumulated"), up("rwkv_cumulated"))
                dve.wait_ge(sem("rwkv_cumulated"), at("rwkv_cumulated"))
                ts(st2[0:HD, 0:H], vecs["rwkv_k_a"][:, l, :], -1.0, 1.0, ALU.mult, ALU.add)
                mul(kn, u4(1), vb("rwkv_k_a"))
                add(kn, kn, st2[0:HD, 0:H].unsqueeze(2).broadcast_to([HD, H, T]))
                mul(kn, kn, k)
                dve.wait_ge(sem("rwkv_kk_norm"), due("dve", "rwkv_kk_norm"))
                v.tensor_scalar(sq, banks(4, 2, HD).rearrange("p (h t) -> p h t", h=H), 1e-24, None, ALU.max).then_inc(sem("root_in"), up("root_in"))
                dve.wait_ge(sem("root_in"), at("root_in"))
                dve.wait_ge(sem("root_out"), due("dve", "root_out"))
                V(v.reciprocal(sq, sq))
                mul(kk, kk, sq)
                dve.wait_ge(sem("rwkv_decays"), due("dve", "rwkv_decays"))
                AR = U(13, 2, parts=HD).rearrange("p (g c) -> p g c", g=HC)
                mul(AR[:, :, 0:CH], u16(3), u16(10))
                mul(AR[:, :, CH:], u16(8), u16(4))
                copy(st2[0:HD, 16:32].rearrange("p (g a) -> p g a", a=1), u16(8)[:, :, CH - 1:CH])
                mul(u4(0), kk, u4(1))
                mul(u4(0), u4(0), u4(9))
                mul(u4(2), kn, u4(9))
                mul(kn, kn, r)
                v.tensor_tensor(kn, kn, vb("rwkv_r_k"), ALU.mult).then_inc(sem("rwkv_operands"), up("rwkv_operands"))
                dve.wait_ge(sem("rwkv_operands"), at("rwkv_operands"))
                for i, b in ((1, 4), (3, 5), (4, 6)):
                    dve.wait_ge(sem("rwkv_rows_psum"), due("dve", "rwkv_rows_psum"))
                    rows = U(i, parts=HD).rearrange("p (g c d) -> p g c d", g=HC // 2, c=2)
                    for c in range(2):
                        done = "rwkv_rows" if c else "dve_order"
                        v.tensor_copy(rows[:, :, c, :], ps[c * HD:(c + 1) * HD, b, :].rearrange("p (g d) -> p g d", d=HD)).then_inc(sem(done), up(done))
                        dve.wait_ge(sem(done), at(done))
                dve.wait_ge(sem("rwkv_gate_psum"), due("dve", "rwkv_gate_psum"))
                for c in range(2):
                    copy(st2[0:HD, 0:HC].rearrange("p (g c) -> p g c", c=2)[:, :, c:c + 1], ps[c * HD:(c + 1) * HD, 7, 0:HC // 2].unsqueeze(2))
                v.tensor_copy(U(5, parts=HD), banks(4, 2, HD)).then_inc(sem("rwkv_gate_rows"), up("rwkv_gate_rows"))
                dve.wait_ge(sem("rwkv_gate_rows"), at("rwkv_gate_rows"))
                copy(u16(15), AR[:, :, 0:CH])
                gB, gK = (U(i, 2, parts=HD).rearrange("p (g c) -> p g c", g=HC) for i in (8, 10))
                for g in (gB, gK):
                    dve.wait_ge(sem("rwkv_gram_psum"), due("dve", "rwkv_gram_psum"))
                    v.tensor_tensor(g, banks(4, 4, HD).rearrange("p (g c) -> p g c", g=HC), cst[0:CH, C_RMASK:C_RMASK + 128].unsqueeze(1).broadcast_to([CH, HC, 128]), ALU.mult).then_inc(sem("rwkv_gram"), up("rwkv_gram"))
                    dve.wait_ge(sem("rwkv_gram"), at("rwkv_gram"))
                u8 = lambda i: U(i).rearrange("p (g t) -> p g t", g=HC // 2)
                b8 = lambda b: banks(b, 2).rearrange("p (g t) -> p g t", g=HC // 2)
                X, XT, M, Y, MT = u8(15), u8(6), u8(12), u8(7), u8(0)
                m128 = lambda c: cst[:, c:c + P].unsqueeze(1).broadcast_to([P, HC // 2, P])
                dve.wait_ge(sem("rwkv_gram_psum"), due("dve", "rwkv_gram_psum"))
                copy(MT, b8(4))
                mul(X, b8(6), m128(C_M1))
                add(X, X, m128(C_IDENT))
                mul(XT, MT, m128(C_M1T))
                add(XT, XT, m128(C_IDENT))
                for n in range(len(LEVELS)):
                    v.tensor_tensor(M, MT, m128(C_LEVEL + P * n), ALU.mult).then_inc(sem("rwkv_inv_M"), up("rwkv_inv_M"))
                    dve.wait_ge(sem("rwkv_inv_M"), at("rwkv_inv_M"))
                    dve.wait_ge(sem("rwkv_inv_Y_psum"), due("dve", "rwkv_inv_Y_psum"))
                    v.tensor_copy(Y, b8(4)).then_inc(sem("rwkv_inv_Y"), up("rwkv_inv_Y"))
                    dve.wait_ge(sem("rwkv_inv_Y"), at("rwkv_inv_Y"))
                    dve.wait_ge(sem("rwkv_inv_X_psum"), due("dve", "rwkv_inv_X_psum"))
                    if n < len(LEVELS) - 1:
                        sub(X, X, b8(6))
                    sub(XT, XT, b8(4))
                inverse = U(12, parts=HD).rearrange("p (g c t) -> p g c t", g=HC // 2, c=2)
                for c in range(2):
                    copy(inverse[:, :, c, :], XT[c * CH:(c + 1) * CH, :, c * CH:(c + 1) * CH])
                S = U(15, off=512, size=256, parts=HD).rearrange("p (h e) -> p h e", h=H)
                v.memset(S, 0.0).then_inc(sem("rwkv_state"), up("rwkv_state"))
                dve.wait_ge(sem("rwkv_state"), at("rwkv_state"))
                y3 = U(0, parts=HD).rearrange("p (c n) -> p c n", c=NC)
                decays = st2[0:HD, 16:32].rearrange("p (h c) -> p h c", h=H)
                for c in range(NC):
                    dve.wait_ge(sem("rwkv_W_psum"), due("dve", "rwkv_W_psum"))
                    v.tensor_copy(U(15, off=0, size=256, parts=HD), ps[0:HD, 4, 0:MW]).then_inc(sem("rwkv_W"), up("rwkv_W"))
                    dve.wait_ge(sem("rwkv_W"), at("rwkv_W"))
                    dve.wait_ge(sem("rwkv_SA_psum"), due("dve", "rwkv_SA_psum"))
                    v.tensor_scalar(U(15, off=256, size=256, parts=HD), ps[0:HD, 5, 0:MW], -1.0, None, ALU.mult).then_inc(sem("rwkv_SA"), up("rwkv_SA"))
                    dve.wait_ge(sem("rwkv_SA"), at("rwkv_SA"))
                    dve.wait_ge(sem("rwkv_Y_psum"), due("dve", "rwkv_Y_psum"))
                    if c < NC - 1:
                        add(S, S, ps[0:HD, 7, 0:MW].rearrange("p (h e) -> p h e", h=H))
                    copy(y3[:, c, :], ps[HD:P, 4, 0:MW])
                    if c < NC - 1:
                        v.tensor_tensor(S, S, decays[:, :, c:c + 1].broadcast_to([HD, H, HD]), ALU.mult).then_inc(sem("rwkv_state"), up("rwkv_state"))
                        dve.wait_ge(sem("rwkv_state"), at("rwkv_state"))
                y16 = U(0, parts=HD).rearrange("p (g d) -> p g d", d=HD)
                head_norm(y16, y16, HC, 64e-5, HD, u16(2))
                mul(y3, y3, lng[:, l, :].unsqueeze(1).broadcast_to([HD, NC, MW]))
                add(y3, y3, lnb[:, l, :].unsqueeze(1).broadcast_to([HD, NC, MW]))
                mul(u16(2), u16(4), st2[0:HD, 0:HC].unsqueeze(2).broadcast_to([HD, HC, HD]))
                y4 = U(0, parts=HD).rearrange("p (c h d) -> p c h d", c=NC, h=H)
                add(y4, y4, U(2, parts=HD).rearrange("p (h c d) -> p c h d", h=H, c=NC))
                v.tensor_tensor(U(0, parts=HD), U(0, parts=HD), U(5, parts=HD), ALU.mult).then_inc(sem("rwkv_out_rows"), up("rwkv_out_rows"))
                dve.wait_ge(sem("rwkv_out_rows"), at("rwkv_out_rows"))
                dve.wait_ge(sem("rwkv_outT"), due("dve", "rwkv_outT"))
                v.tensor_copy(oT[:, 2, :, :], ps[:, 4, :].rearrange("p (k t) -> p k t", k=2)).then_inc(sem("rwkv_done"), up("rwkv_done"))
                dve.wait_ge(sem("rwkv_done"), at("rwkv_done"))
                dve.wait_ge(sem("rows_psum"), due("dve", "rows_psum", 3 if l else 1))
                v.tensor_tensor(merged[:, :, :], memT, gT["ln_mem"][:, l, :].unsqueeze(2).broadcast_to([P, KD, T]), ALU.mult).then_inc(sem("mem_ready"), up("mem_ready"))
                dve.wait_ge(sem("mem_ready"), at("mem_ready"))
                residual()
                norm(x, hrows, gT["ln_xa_pre"][:, l, :], hT)
                for t in range(NT):
                    softmax(T, (D // 4) ** -0.5, None, b=0 if t else 4)
                residual()
                norm(x, hrows, gT["ln_mlp_pre"][:, l, :], hT)
                ffn(FF1 // STEP, False)
                residual()
            xr = U(8, 2, size=4 * (T + 3)).rearrange("p (c t) -> p c t", c=4)
            gd = fbT[:, 0:1024].rearrange("p (w c n) -> p w c n", w=2, c=4)
            v.memset(xr[:, :, 0:3], 0.0).then_inc(sem("lru_pad"), up("lru_pad"))
            dve.wait_ge(sem("lru_pad"), at("lru_pad"))
            v.memset(gd, 0.0).then_inc(sem("lru_gate_cleared"), up("lru_gate_cleared"))
            dve.wait_ge(sem("lru_gate_cleared"), at("lru_gate_cleared"))
            norm(x, hrows, gT["norm_mix_2"][:, 0, :], hT)
            dve.wait_ge(sem("lru_exp"), due("dve", "lru_exp"))
            y_, z_, z2, acc, sp8 = (stat[:, 36 + 4 * i:40 + 4 * i] for i in range(5))
            ts(z_, y_, 2.0, None, ALU.add)
            V(v.reciprocal(z_, z_))
            mul(z_, z_, y_)
            mul(z2, z_, z_)
            ts(acc, z2, 1.0 / 19, 1.0 / 17, ALU.mult, ALU.add)
            for n in (15, 13, 11, 9, 7, 5, 3, 1):
                mul(acc, acc, z2)
                ts(acc, acc, 1.0 / n, None, ALU.add)
            mul(acc, acc, z_)
            ts(sp8, vec2["ev_lambda_2"][:, :], -1.0, 0.0, ALU.mult, ALU.max)
            stt(sp8, acc, 2.0, sp8, ALU.mult, ALU.add)
            ts(sp8, sp8, 8.0, None, ALU.mult)
            dve.wait_ge(sem("even_inputs"), due("dve", "even_inputs"))
            fu, fm, f1, f2 = (U(2, off=256 * i, size=256, parts=8) for i in range(4))
            ts(fm, fu, 0.0, None, ALU.min)
            ts(f1, fu, -1.0, None, ALU.mult)
            v.tensor_tensor(f1, fu, f1, ALU.max).then_inc(sem("fox_exp_in"), up("fox_exp_in"))
            dve.wait_ge(sem("fox_exp_in"), at("fox_exp_in"))
            xc, tmp4 = U(13).rearrange("p (c t) -> p c t", c=4), U(4).rearrange("p (c t) -> p c t", c=4)
            for c in range(4):
                ts(xc[:, c, :], xr[:, c, 0:T], convw2[:, 0, c:c + 1], vec2["ev_conv_b_2"][:, c:c + 1], ALU.mult, ALU.add)
                for j in (1, 2, 3):
                    done = "lru_conv" if c == 3 and j == 3 else "dve_order"
                    v.scalar_tensor_tensor(xc[:, c, :], xr[:, c, j:j + T], convw2[:, j, c:c + 1], xc[:, c, :], ALU.mult, ALU.add).then_inc(sem(done), up(done))
                    dve.wait_ge(sem(done), at(done))
            dve.wait_ge(sem("fox_ln"), due("dve", "fox_ln"))
            sub(fm, fm, f2)
            V(v.memset(fu, 1.0))
            V(v.tensor_tensor_scan(f1, fu, fm, 0.0, ALU.mult, ALU.add))
            v.tensor_scalar(f2, f1, -1.0, None, ALU.mult).then_inc(sem("fox_cum"), up("fox_cum"))
            dve.wait_ge(sem("fox_cum"), at("fox_cum"))
            dve.wait_ge(sem("lru_sigmoids"), due("dve", "lru_sigmoids"))
            la, iu, aa, th = (U(i).rearrange("p (c t) -> p c t", c=4) for i in (4, 5, 6, 7))
            v.tensor_tensor(la, la, sp8.unsqueeze(2).broadcast_to([P, 4, T]), ALU.mult).then_inc(sem("lru_log_a"), up("lru_log_a"))
            dve.wait_ge(sem("lru_log_a"), at("lru_log_a"))
            mul(iu, iu, xc)
            yr, gl = U(10), U(11)
            mul(gl, yr, yr)
            ts(gl, gl, 0.044715, 1.0, ALU.mult, ALU.add)
            mul(gl, gl, yr)
            v.tensor_scalar(gl, gl, math.sqrt(2.0 / math.pi), None, ALU.mult).then_inc(sem("gelu_in"), up("gelu_in"))
            dve.wait_ge(sem("gelu_in"), at("gelu_in"))
            dve.wait_ge(sem("lru_a"), due("dve", "lru_a"))
            ts(la, th, 1.0, None, ALU.add)
            V(v.reciprocal(U(4), U(4)))
            mul(th, th, la)
            v.tensor_scalar(th, th, 2.0, None, ALU.mult).then_inc(sem("root_in"), up("root_in"))
            dve.wait_ge(sem("root_in"), at("root_in"))
            dve.wait_ge(sem("root_out"), due("dve", "root_out"))
            mul(iu, iu, th)
            for c in range(4):
                V(v.tensor_tensor_scan(la[:, c, :], aa[:, c, :], iu[:, c, :], 0.0, ALU.mult, ALU.add))
            dve.wait_ge(sem("gelu_tanh"), due("dve", "gelu_tanh"))
            ts(gl, gl, 1.0, 0.5, ALU.add, ALU.mult)
            mul(gl, gl, yr)
            v.tensor_tensor(merged[:, 0:4, :].rearrange("p c t -> p (c t)"), U(4), gl, ALU.mult).then_inc(sem("lru_done"), up("lru_done"))
            dve.wait_ge(sem("lru_done"), at("lru_done"))
            for t in range(NT):
                for hg in range(2):
                    n = (t + 1) * P
                    softmax(n, 1.0, causal[t].unsqueeze(1).broadcast_to([P, 4, n]), b=0 if hg else 4)
            plain_residual()
            norm(x, hrows, gT["norm_ffn_2"][:, 0, :], hT)
            ffn(FF2 // STEP, True)
            plain_residual()
            norm(x, hrows, gT["norm_mix_2"][:, 1, :], hT)
            V(v.memset(U(14), 0.0))
            dve.wait_ge(sem("gla_gate_psum"), due("dve", "gla_gate_psum"))
            u3 = lambda i: U(i).rearrange("p (h t) -> p h t", h=H)
            g3 = lambda i: U(i).rearrange("p (g t) -> p g t", g=HC)
            add(u3(4), banks(4, 2).rearrange("p (h t) -> p h t", h=H), vec2["od_gate_b_2"][:, :].unsqueeze(2).broadcast_to([P, H, T]))
            ts(u3(5), u3(4), -1.0, None, ALU.mult)
            v.tensor_tensor(U(5), U(4), U(5), ALU.max).then_inc(sem("gla_exp_in"), up("gla_exp_in"))
            dve.wait_ge(sem("gla_exp_in"), at("gla_exp_in"))
            ts(U(4), U(4), 0.0, None, ALU.min)
            dve.wait_ge(sem("gla_ln"), due("dve", "gla_ln"))
            sub(U(4), U(4), U(6))
            ts(U(5), U(4), 1.0 / 16, None, ALU.mult)
            V(v.tensor_tensor_scan(U(4), resets[:, :, :].rearrange("p g t -> p (g t)"), U(5), 0.0, ALU.mult, ALU.add))
            bl = g3(4)[:, :, CH - 1:CH]
            copy(st2[:, 0:HC].unsqueeze(2), bl)
            v.tensor_tensor(g3(7), bl.broadcast_to([P, HC, CH]), g3(4), ALU.subtract).then_inc(sem("gla_cum"), up("gla_cum"))
            dve.wait_ge(sem("gla_cum"), at("gla_cum"))
            dve.wait_ge(sem("gla_exps"), due("dve", "gla_exps"))
            mul(U(10), U(9), U(7))
            mul(U(8), U(8), U(5))
            v.tensor_tensor(U(9), U(9), U(6), ALU.mult).then_inc(sem("gla_operands"), up("gla_operands"))
            dve.wait_ge(sem("gla_operands"), at("gla_operands"))
            dve.wait_ge(sem("gla_rows_psum"), due("dve", "gla_rows_psum"))
            v.tensor_copy(U(11, 2, parts=CH), banks(4, 4, CH)).then_inc(sem("gla_rows"), up("gla_rows"))
            dve.wait_ge(sem("gla_rows"), at("gla_rows"))
            dve.wait_ge(sem("gla_scores_psum"), due("dve", "gla_scores_psum"))
            v.tensor_tensor(U(13, parts=CH).rearrange("p (g c) -> p g c", g=HC), banks(4, 2, CH).rearrange("p (g c) -> p g c", g=HC), cst[0:CH, C_RMASK + 64:C_RMASK + 128].unsqueeze(1).broadcast_to([CH, HC, CH]), ALU.mult).then_inc(sem("gla_scores"), up("gla_scores"))
            dve.wait_ge(sem("gla_scores"), at("gla_scores"))
            dve.wait_ge(sem("gla_decay"), due("dve", "gla_decay"))
            state = U(14).rearrange("p (h e) -> p h e", h=H)
            orow = fbT[0:CH, 4096:8192].rearrange("p (c n) -> p c n", c=NC)
            dec = st2[:, 0:HC].rearrange("p (h c) -> p h c", h=H)
            v.tensor_copy(stat[:, 61:62], stat[:, 62:63]).then_inc(sem("gla_state"), up("gla_state"))
            dve.wait_ge(sem("gla_state"), at("gla_state"))
            for c in range(NC):
                dve.wait_ge(sem("gla_out_psum"), due("dve", "gla_out_psum"))
                copy(orow[:, c, :], banks(4, 2, CH))
                if c < NC - 1:
                    mul(state, state, dec[:, :, c:c + 1].broadcast_to([P, H, T]))
                    v.tensor_tensor(state, state, banks(6, 2).rearrange("p (h e) -> p h e", h=H), ALU.add).then_inc(sem("gla_state"), up("gla_state"))
                    dve.wait_ge(sem("gla_state"), at("gla_state"))
            o16 = fbT[0:CH, 4096:8192].rearrange("p (g e) -> p g e", g=HC)
            sq16 = U(4, 4, parts=CH).rearrange("p (g e) -> p g e", g=HC)
            mul(sq16, o16, o16)
            red(st2[0:CH, 16:32], sq16, ALU.add)
            inv_root(st2[0:CH, 16:32], st2[0:CH, 16:32], T, 1e-6)
            mul(o16, o16, st2[0:CH, 16:32].unsqueeze(2).broadcast_to([CH, HC, T]))
            dve.wait_ge(sem("gainrow_loaded"), due("dve", "gainrow_loaded", 16))
            v.tensor_tensor(orow, orow, gainrow[0:CH, :].unsqueeze(1).broadcast_to([CH, NC, D]), ALU.mult).then_inc(sem("gainrow_used"), up("gainrow_used"))
            dve.wait_ge(sem("gainrow_used"), at("gainrow_used"))
            dve.wait_ge(sem("gla_inputs"), due("dve", "gla_inputs", 2))
            v.tensor_tensor(fbT[0:CH, 4096:8192], fbT[0:CH, 4096:8192], fbT[0:CH, 0:4096], ALU.mult).then_inc(sem("gla_out_rows"), up("gla_out_rows"))
            dve.wait_ge(sem("gla_out_rows"), at("gla_out_rows"))
            dve.wait_ge(sem("gla_outT_psum"), due("dve", "gla_outT_psum"))
            v.tensor_copy(merged[:, :, :].rearrange("p k t -> p (k t)"), banks(4, 4)).then_inc(sem("gla_outT"), up("gla_outT"))
            dve.wait_ge(sem("gla_outT"), at("gla_outT"))
            plain_residual()
            norm(x, hrows, gT["norm_ffn_2"][:, 1, :], hT)
            lg = U(4, off=512, size=16).rearrange("p (t e) -> p t e", t=NT)
            top = U(4, off=544, size=16).rearrange("p (t e) -> p t e", t=NT)
            idxf = U(4, off=576, size=16).rearrange("p (t e) -> p t e", t=NT)
            idx = U(4, off=608, size=16).bitcast(U32).rearrange("p (t e) -> p t e", t=NT)
            gates = U(4, size=16).rearrange("p (t e) -> p t e", t=NT)
            dve.wait_ge(sem("router_psum"), due("dve", "router_psum"))
            copy(U(4, off=512, size=16), ps[:, 0, 0:16])
            for t in range(NT):
                V(v.max(top[:, t, :], lg[:, t, :]))
                V(v.max_index(idx[:, t, :], top[:, t, :], lg[:, t, :]))
            copy(idxf, idx)
            v.tensor_tensor(stat[:, 42:44].unsqueeze(2), top[:, :, 1:2], top[:, :, 0:1], ALU.subtract).then_inc(sem("router_diff"), up("router_diff"))
            dve.wait_ge(sem("router_diff"), at("router_diff"))
            dve.wait_ge(sem("router_exp"), due("dve", "router_exp"))
            ts(stat[:, 44:46], stat[:, 40:42], 1.0, None, ALU.add)
            V(v.reciprocal(stat[:, 44:46], stat[:, 44:46]))
            mul(stat[:, 46:48], stat[:, 44:46], stat[:, 40:42])
            iota = cst[:, C_IOTA:C_IOTA + NEXP]
            for t in range(NT):
                ts(lg[:, t, :], iota, idxf[:, t, 0:1], stat[:, 44 + t:45 + t], ALU.is_equal, ALU.mult)
                ts(gates[:, t, :], iota, idxf[:, t, 1:2], stat[:, 46 + t:47 + t], ALU.is_equal, ALU.mult)
                done = "router_gates" if t else "dve_order"
                v.tensor_tensor(gates[:, t, :], gates[:, t, :], lg[:, t, :], ALU.add).then_inc(sem(done), up(done))
                dve.wait_ge(sem(done), at(done))
            for t in range(NT):
                ts(chosen[:, t, :], iota, idxf[:, t, 0:1], None, ALU.is_equal)
                done = "chosen" if t else "dve_order"
                v.scalar_tensor_tensor(chosen[:, t, :], iota, idxf[:, t, 1:2], chosen[:, t, :], ALU.is_equal, ALU.add).then_inc(sem(done), up(done))
                dve.wait_ge(sem(done), at(done))
            dve.wait_ge(sem("slots_psum"), due("dve", "slots_psum"))
            copy(fbT[:, 6160:6184], ps[:, 2, 0:24])
            red(most, load[0:1, :], ALU.max)
            v.tensor_copy(most_int, most).then_inc(sem("most_known"), up("most_known"))
            dve.wait_ge(sem("most_known"), at("most_known"))
            fullest = dve.value_load(most_int, min_val=0, max_val=T)
            before_branch = counts_now()
            with dve.If(fullest <= SLOTS):
                slots_iota = cst[:, C_IOTA:C_IOTA + SLOTS]
                for t in range(NT):
                    for e in range(NEXP):
                        v.tensor_scalar(pick[:, e, t, :], slots_iota, slot[:, t, e:e + 1], chosen[:, t, e:e + 1], ALU.is_equal, ALU.mult).then_inc(sem("picks"), up("picks"))
                        dve.wait_ge(sem("picks"), at("picks"))
                v.tensor_tensor(pick_gate, pick, gates.rearrange("p t e -> p e t").unsqueeze(3).broadcast_to([P, NEXP, NT, SLOTS]), ALU.mult).then_inc(sem("picks"), up("picks"))
                dve.wait_ge(sem("picks"), at("picks"))
                dve.wait_ge(sem("spread_psum"), due("dve", "spread_psum"))
                v.tensor_copy(spread, banks(0, 4)).then_inc(sem("spread_ready"), up("spread_ready"))
                dve.wait_ge(sem("spread_ready"), at("spread_ready"))
                gain = gT["norm_ffn_2"][:, 1, :].unsqueeze(2).broadcast_to([P, KD, SLOTS])
                with dve.Fori(0, NEXP) as e:
                    enter(e)
                    dve.wait_ge(sem("slot_x_psum"), due("dve", "slot_x_psum"))
                    v.tensor_tensor(slot_x, banks(0, 2).rearrange("p (k c) -> p k c", k=KD), gain, ALU.mult).then_inc(sem("slot_x"), up("slot_x"))
                    dve.wait_ge(sem("slot_x"), at("slot_x"))
                    for i in range(FFE // STEP):
                        dve.wait_ge(sem("slot_hidden_act"), due("dve", "slot_hidden_act"))
                        v.tensor_tensor(U(i % 2, size=2 * SLOTS), U(2 + i % 2, size=2 * SLOTS), ps[:, i % 2, 2 * SLOTS:4 * SLOTS], ALU.mult).then_inc(sem("slot_hidden_ready"), up("slot_hidden_ready"))
                        dve.wait_ge(sem("slot_hidden_ready"), at("slot_hidden_ready"))
                        if i == 0:
                            v.tensor_copy(spread_e, fbT[:, bass.ds(e * T + 4096, T)]).then_inc(sem("slot_spread"), up("slot_spread"))
                            dve.wait_ge(sem("slot_spread"), at("slot_spread"))
                    dve.wait_ge(sem("slot_y_psum"), due("dve", "slot_y_psum"))
                    v.tensor_copy(slot_y, banks(2, 2)).then_inc(sem("slot_y"), up("slot_y"))
                    dve.wait_ge(sem("slot_y"), at("slot_y"))
                    leave(NEXP)
            go_back(before_branch)
            with dve.Else():
                dve.wait_ge(sem("router_T_psum"), due("dve", "router_T_psum"))
                v.tensor_copy(U(4, off=64, size=T, parts=NEXP), ps[0:NEXP, 1, 0:T]).then_inc(sem("router_T"), up("router_T"))
                dve.wait_ge(sem("router_T"), at("router_T"))
                dve.wait_ge(sem("router_rows_psum"), due("dve", "router_rows_psum"))
                grows = U(6, 2).rearrange("p (e t) -> p e t", e=NEXP)
                v.tensor_copy(U(6, 2), banks(0, 4)).then_inc(sem("router_rows"), up("router_rows"))
                dve.wait_ge(sem("router_rows"), at("router_rows"))
                with dve.Fori(0, NEXP) as e:
                    enter(e)
                    ffn(FFE // STEP, True, U(6, 2)[:, bass.ds(e * T, T)])
                    leave(NEXP)
            plain_residual()
            dve.wait_ge(sem("gainrow_loaded"), due("dve", "gainrow_loaded", 16))
            for t in range(NT):
                dve.wait_ge(sem("norm_root"), due("dve", "norm_root"))
                V(v.reciprocal(stat[:, t:t + 1], stat[:, t:t + 1]))
                v.scalar_tensor_tensor(x[:, t, :], x[:, t, :], stat[:, t:t + 1], gainrow[:, :], ALU.mult, ALU.mult).then_inc(sem("result_rows"), up("result_rows"))
                dve.wait_ge(sem("result_rows"), at("result_rows"))


_INS = ['x', 'mem', 'ln_mix_pre', 'w_in', 'nsa_cmp_w', 'nsa_cmp_pe', 'rel_bias', 'ret_norm_g', 'rwkv_mu', 'rwkv_w0',
        'rwkv_w2', 'rwkv_a0', 'rwkv_a2', 'rwkv_g2', 'rwkv_k_k', 'rwkv_k_a', 'rwkv_r_k', 'rwkv_ln_g', 'rwkv_ln_b',
        'conv_w', 'w_branch', 'w_mix_out', 'ln_mix_post', 'ln_xa_pre', 'ln_mem', 'xa_wq', 'xa_wkv', 'xa_wo',
        'ln_xa_post', 'ln_mlp_pre', 'mlp_w1', 'mlp_w2', 'ln_mlp_post', 'norm_mix_2', 'norm_ffn_2', 'norm_final_2',
        'ev_w_in_2', 'ev_conv_w_2', 'ev_conv_b_2', 'ev_ga_w_2', 'ev_ga_b_2', 'ev_gx_w_2', 'ev_gx_b_2',
        'ev_lambda_2', 'ev_f_b_2', 'ev_w_out_2', 'ev_ffn_w1_2', 'ev_ffn_w3_2', 'ev_ffn_w2_2', 'od_w_in_2',
        'od_gate_w2_2', 'od_gate_b_2', 'od_head_norm_2', 'od_w_out_2', 'od_router_2', 'od_exp_w1_2',
        'od_exp_w3_2', 'od_exp_w2_2']


def kernel(**inputs):
    import numpy as _np
    import concourse.bacc as _bacc
    from concourse import mybir as _mybir
    from concourse.bass_utils import run_bass_kernel_spmd as _run

    nc = _bacc.Bacc("TRN2", target_bir_lowering=False, num_devices=1)
    arrays, args = {}, {}
    for name in _INS:
        arrays[f"in_{name}"] = _np.ascontiguousarray(inputs[name])
    for name, value in constants().items():
        arrays[f"in_{name}"] = value
    for key, value in arrays.items():
        args[key[3:]] = nc.dram_tensor(key, value.shape, _mybir.dt.from_np(value.dtype), kind="ExternalInput").ap()
    out = nc.dram_tensor("out", (1, T, D), F32, kind="ExternalOutput").ap()
    build(nc, args, out)
    r = _run(nc, [arrays], core_ids=[0])
    return r.results[0]["out"]
```
